# Optimizing a Trainium2 kernel written in Bass

```python
import math
import jax, jax.numpy as jnp
from jax import lax
import numpy as np

D_MODEL = 1024
BATCH = 1
SEQ = 256
DEPTH = 2

D_BRANCH = 512
M_HEADS = 4
M_HEAD_DIM = D_BRANCH // M_HEADS
M_CHUNK = 64
M_CONV = 4
R_BLOCKS = 8
R_BLOCK_DIM = D_BRANCH // R_BLOCKS
R_CONV = 4
R_C = 8.0
A_HEADS = 8
A_HEAD_DIM = D_BRANCH // A_HEADS
IDX_HEADS = 8
IDX_DIM = 64
TOPK_MAX = 256
Q_BLOCK = 128
ROPE_THETA = 10000.0
D_FF = 3 * D_MODEL
FFN_CONV = 3
EPS = 1e-6

IN_SPLITS = (
    2 * D_BRANCH,
    D_BRANCH,
    D_BRANCH,
    M_HEADS,
    M_HEADS,
    D_BRANCH,
    D_BRANCH,
    D_BRANCH,
    D_BRANCH,
    D_BRANCH,
    IDX_HEADS * IDX_DIM,
    IDX_DIM,
    IDX_HEADS,
    3 * D_MODEL,
)
N_IN = sum(IN_SPLITS)


def rms_norm(x, g):
    xf = x.astype(jnp.float32)
    y = xf * lax.rsqrt(jnp.mean(xf * xf, axis=-1, keepdims=True) + EPS)
    return (y * g.astype(jnp.float32)).astype(x.dtype)

def causal_dwconv(x, w, b):
    K, C = w.shape
    y = lax.conv_general_dilated(x, w[:, None, :].astype(x.dtype), window_strides=(1,),
                                 padding=[(K - 1, 0)], dimension_numbers=('NWC', 'WIO', 'NWC'),
                                 feature_group_count=C)
    return y + b.astype(x.dtype)

def rope_tables(positions, dim):
    inv = ROPE_THETA ** (-jnp.arange(0, dim, 2, dtype=jnp.float32) / dim)
    ang = positions.astype(jnp.float32)[..., None] * inv
    return jnp.cos(ang), jnp.sin(ang)

def apply_rope(x, cos, sin):
    x1, x2 = jnp.split(x.astype(jnp.float32), 2, axis=-1)
    c = cos[:, :, None, :]
    s = sin[:, :, None, :]
    return jnp.concatenate([x1 * c - x2 * s, x2 * c + x1 * s], axis=-1).astype(x.dtype)

def head_layer_norm(h, g):
    B, S, H, Dh = h.shape
    mu = jnp.mean(h, axis=-1, keepdims=True)
    var = jnp.mean(jnp.square(h - mu), axis=-1, keepdims=True)
    y = (h - mu) * lax.rsqrt(var + EPS)
    return y.reshape(B, S, H * Dh) * g.astype(jnp.float32)

def mlstm_chunkwise(q, k, v, i_pre, f_pre):
    B, S, H, Dh = q.shape
    L = M_CHUNK
    nc = S // L
    f32 = jnp.float32

    def to_chunks(t):
        return t.astype(f32).reshape(B, nc, L, H, Dh).transpose(1, 0, 3, 2, 4)

    def gate_chunks(t):
        return t.astype(f32).reshape(B, nc, L, H).transpose(1, 0, 3, 2)

    qc = to_chunks(q)
    kc = to_chunks(k) * (Dh ** -0.5)
    vc = to_chunks(v)
    ic = gate_chunks(i_pre)
    gc = jnp.cumsum(jax.nn.log_sigmoid(gate_chunks(f_pre)), axis=-1)
    causal = jnp.tril(jnp.ones((L, L), dtype=bool))

    def step(carry, inp):
        C, n, m = carry
        qb, kb, vb, ib, gb = inp
        logd = jnp.where(causal, gb[..., :, None] - gb[..., None, :] + ib[..., None, :], -jnp.inf)
        log_inter = gb + m[..., None]
        m_t = jnp.maximum(log_inter, jnp.max(logd, axis=-1))
        s = jnp.einsum('bhtd,bhsd->bhts', qb, kb) * jnp.exp(logd - m_t[..., None])
        w_inter = jnp.exp(log_inter - m_t)
        num = jnp.einsum('bhts,bhsd->bhtd', s, vb) + w_inter[..., None] * jnp.einsum('bhvk,bhtk->bhtv', C, qb)
        den = jnp.sum(s, axis=-1) + w_inter * jnp.einsum('bhk,bhtk->bht', n, qb)
        h = num / jnp.maximum(jnp.abs(den), jnp.exp(-m_t))[..., None]
        g_last = gb[..., -1]
        m_new = m_t[..., -1]
        w_state = jnp.exp(g_last[..., None] - gb + ib - m_new[..., None])
        decay = jnp.exp(g_last + m - m_new)
        C = decay[..., None, None] * C + jnp.einsum('bhs,bhsv,bhsk->bhvk', w_state, vb, kb)
        n = decay[..., None] * n + jnp.einsum('bhs,bhsk->bhk', w_state, kb)
        return (C, n, m_new), h

    init = (jnp.zeros((B, H, Dh, Dh), f32), jnp.zeros((B, H, Dh), f32), jnp.zeros((B, H), f32))
    _, hs = lax.scan(step, init, (qc, kc, vc, ic, gc))
    return hs.transpose(1, 0, 3, 2, 4).reshape(B, S, H, Dh)

def rg_lru(x, w_a, b_a, w_x, b_x, lam):
    B, S, C = x.shape
    xf = x.astype(jnp.float32)
    xb = xf.reshape(B, S, R_BLOCKS, R_BLOCK_DIM)
    r = jax.nn.sigmoid(jnp.einsum('bsnd,nde->bsne', xb, w_a.astype(jnp.float32)).reshape(B, S, C) + b_a.astype(jnp.float32))
    i = jax.nn.sigmoid(jnp.einsum('bsnd,nde->bsne', xb, w_x.astype(jnp.float32)).reshape(B, S, C) + b_x.astype(jnp.float32))
    log_a = -R_C * r * jax.nn.softplus(-lam.astype(jnp.float32))
    a = jnp.exp(log_a)
    u = jnp.sqrt(-jnp.expm1(2.0 * log_a)) * (i * xf)

    def combine(left, right):
        a1, b1 = left
        a2, b2 = right
        return a1 * a2, a2 * b1 + b2

    _, h = lax.associative_scan(combine, (a, u), axis=1)
    return h.astype(x.dtype)

def dsa_attention(q, k, v, q_idx, k_idx, w_idx):
    B, S, H, Dh = q.shape
    f32 = jnp.float32
    top_k = min(TOPK_MAX, S // 4)
    nb = S // Q_BLOCK
    key_pos = jnp.arange(S, dtype=jnp.int32)
    k_idx_f = k_idx.astype(f32)

    def blocks(t):
        return jnp.moveaxis(t.reshape((B, nb, Q_BLOCK) + t.shape[2:]), 1, 0)

    def attend(args):
        qb, qib, wb, start = args
        qpos = start + jnp.arange(Q_BLOCK, dtype=jnp.int32)
        visible = key_pos[None, None, :] <= qpos[None, :, None]
        logits = jnp.einsum('bqhd,bsd->bqhs', qib.astype(f32), k_idx_f) * (IDX_DIM ** -0.5)
        score = jnp.einsum('bqh,bqhs->bqs', wb.astype(f32) * (IDX_HEADS ** -0.5), jax.nn.relu(logits))
        score = jnp.where(visible, score, -jnp.inf)
        _, idx = lax.top_k(score, top_k)
        k_sel = jax.vmap(lambda kk, ii: kk[ii])(k, idx)
        v_sel = jax.vmap(lambda vv, ii: vv[ii])(v, idx)
        att = jnp.einsum('bqhd,bqkhd->bqhk', qb.astype(f32), k_sel.astype(f32)) * (Dh ** -0.5)
        keep = (idx <= qpos[None, :, None])[:, :, None, :]
        p = jax.nn.softmax(jnp.where(keep, att, -jnp.inf), axis=-1)
        return jnp.einsum('bqhk,bqkhd->bqhd', p, v_sel.astype(f32)).astype(q.dtype)

    starts = jnp.arange(nb, dtype=jnp.int32) * Q_BLOCK
    out = lax.map(attend, (blocks(q), blocks(q_idx), blocks(w_idx), starts))
    return jnp.moveaxis(out, 0, 1).reshape(B, S, H, Dh)

def first_inputs(seed: int = 0) -> dict:
    key = jax.random.key(seed)
    ks = jax.random.split(key, 24)
    f32 = jnp.float32

    def normal(k, shape, scale):
        return jax.random.normal(k, shape, f32) * scale

    def gain(k, shape):
        return 1.0 + 0.02 * jax.random.normal(k, shape, f32)

    x = normal(ks[0], (BATCH, SEQ, D_MODEL), 1.0)
    positions = (jnp.arange(SEQ, dtype=jnp.int32)[None, :]
                 + jax.random.randint(ks[1], (BATCH, 1), 0, 4096, dtype=jnp.int32))
    norm_mix = gain(ks[2], (DEPTH, D_MODEL))
    w_in = normal(ks[3], (DEPTH, D_MODEL, N_IN), D_MODEL ** -0.5)
    mlstm_conv_w = normal(ks[4], (DEPTH, M_CONV, 2 * D_BRANCH), M_CONV ** -0.5)
    mlstm_conv_b = normal(ks[5], (DEPTH, 2 * D_BRANCH), 0.02)
    mlstm_i_bias = normal(ks[6], (DEPTH, M_HEADS), 0.1)
    mlstm_f_bias = jnp.linspace(3.0, 6.0, M_HEADS, dtype=f32)[None, :] + normal(ks[7], (DEPTH, M_HEADS), 0.1)
    mlstm_norm = gain(ks[8], (DEPTH, D_BRANCH))
    rglru_conv_w = normal(ks[9], (DEPTH, R_CONV, D_BRANCH), R_CONV ** -0.5)
    rglru_conv_b = normal(ks[10], (DEPTH, D_BRANCH), 0.02)
    rglru_w_a = normal(ks[11], (DEPTH, R_BLOCKS, R_BLOCK_DIM, R_BLOCK_DIM), R_BLOCK_DIM ** -0.5)
    rglru_b_a = normal(ks[12], (DEPTH, D_BRANCH), 0.02)
    rglru_w_x = normal(ks[13], (DEPTH, R_BLOCKS, R_BLOCK_DIM, R_BLOCK_DIM), R_BLOCK_DIM ** -0.5)
    rglru_b_x = normal(ks[14], (DEPTH, D_BRANCH), 0.02)
    a_c = jax.random.uniform(ks[15], (DEPTH, D_BRANCH), f32, 0.9, 0.999)
    sig = a_c ** (1.0 / R_C)
    rglru_lambda = jnp.log(sig) - jnp.log1p(-sig)
    w_branch = normal(ks[16], (DEPTH, 3, D_BRANCH, D_MODEL), D_BRANCH ** -0.5)
    w_out = normal(ks[17], (DEPTH, D_MODEL, D_MODEL), D_MODEL ** -0.5)
    norm_ffn = gain(ks[18], (DEPTH, D_MODEL))
    ffn_up = normal(ks[19], (DEPTH, D_MODEL, 2 * D_FF), D_MODEL ** -0.5)
    ffn_conv_w = normal(ks[20], (DEPTH, FFN_CONV, D_FF), FFN_CONV ** -0.5)
    ffn_conv_b = normal(ks[21], (DEPTH, D_FF), 0.02)
    ffn_down = normal(ks[22], (DEPTH, D_FF, D_MODEL), D_FF ** -0.5)
    norm_final = gain(ks[23], (D_MODEL,))
    return {'x': x, 'positions': positions, 'norm_mix': norm_mix, 'w_in': w_in,
            'mlstm_conv_w': mlstm_conv_w, 'mlstm_conv_b': mlstm_conv_b,
            'mlstm_i_bias': mlstm_i_bias, 'mlstm_f_bias': mlstm_f_bias, 'mlstm_norm': mlstm_norm,
            'rglru_conv_w': rglru_conv_w, 'rglru_conv_b': rglru_conv_b,
            'rglru_w_a': rglru_w_a, 'rglru_b_a': rglru_b_a, 'rglru_w_x': rglru_w_x, 'rglru_b_x': rglru_b_x,
            'rglru_lambda': rglru_lambda, 'w_branch': w_branch, 'w_out': w_out, 'norm_ffn': norm_ffn,
            'ffn_up': ffn_up, 'ffn_conv_w': ffn_conv_w, 'ffn_conv_b': ffn_conv_b, 'ffn_down': ffn_down,
            'norm_final': norm_final}

def first_block(x, positions, norm_mix, w_in, mlstm_conv_w, mlstm_conv_b, mlstm_i_bias, mlstm_f_bias,
              mlstm_norm, rglru_conv_w, rglru_conv_b, rglru_w_a, rglru_b_a, rglru_w_x, rglru_b_x,
              rglru_lambda, w_branch, w_out, norm_ffn, ffn_up, ffn_conv_w, ffn_conv_b, ffn_down,
              norm_final):
    B, S, _ = x.shape
    cos, sin = rope_tables(positions, A_HEAD_DIM)
    split_at = np.cumsum(IN_SPLITS)[:-1].tolist()
    m_shape = (B, S, M_HEADS, M_HEAD_DIM)
    a_shape = (B, S, A_HEADS, A_HEAD_DIM)
    for l in range(DEPTH):
        h = rms_norm(x, norm_mix[l])
        (m_qk, m_v, m_o, m_i, m_f, r_x, r_g, a_q, a_k, a_v, a_qi, a_ki, a_w, gates) = jnp.split(
            h @ w_in[l], split_at, axis=-1)
        m_qk = jax.nn.silu(causal_dwconv(m_qk, mlstm_conv_w[l], mlstm_conv_b[l]))
        m_q, m_k = jnp.split(m_qk, 2, axis=-1)
        h_m = mlstm_chunkwise(m_q.reshape(m_shape), m_k.reshape(m_shape), m_v.reshape(m_shape),
                              m_i + mlstm_i_bias[l], m_f + mlstm_f_bias[l])
        y_a = (head_layer_norm(h_m, mlstm_norm[l]) * jax.nn.sigmoid(m_o.astype(jnp.float32))).astype(x.dtype)
        r_x = causal_dwconv(r_x, rglru_conv_w[l], rglru_conv_b[l])
        y_b = jax.nn.gelu(r_g) * rg_lru(r_x, rglru_w_a[l], rglru_b_a[l], rglru_w_x[l], rglru_b_x[l], rglru_lambda[l])
        q_c = apply_rope(a_q.reshape(a_shape), cos, sin)
        k_c = apply_rope(a_k.reshape(a_shape), cos, sin)
        qi = apply_rope(a_qi.reshape(B, S, IDX_HEADS, IDX_DIM), cos, sin)
        ki = apply_rope(a_ki[:, :, None, :], cos, sin)[:, :, 0, :]
        y_c = dsa_attention(q_c, k_c, a_v.reshape(a_shape), qi, ki, a_w).reshape(B, S, D_BRANCH)
        g_a, g_b, g_c = jnp.split(jax.nn.sigmoid(gates), 3, axis=-1)
        merged = (g_a * (y_a @ w_branch[l, 0]) + g_b * (y_b @ w_branch[l, 1])
                  + g_c * (y_c @ w_branch[l, 2]))
        x = x + merged @ w_out[l]
        h = rms_norm(x, norm_ffn[l])
        ff_g, ff_u = jnp.split(h @ ffn_up[l], 2, axis=-1)
        ff_g = causal_dwconv(ff_g, ffn_conv_w[l], ffn_conv_b[l])
        x = x + (jax.nn.gelu(ff_g) * ff_u) @ ffn_down[l]
    return rms_norm(x, norm_final)


DEPTH_2 = 1

D_MIX = 2 * D_MODEL
D_SSD = D_MIX // 2
D_SC = D_MIX - D_SSD
SSD_HEADDIM = 64
SSD_HEADS = D_SSD // SSD_HEADDIM
SSD_GROUPS = 4
SSD_HPG = SSD_HEADS // SSD_GROUPS
SSD_STATE = 128
SSD_CONV = 4
D_XBC = D_SSD + 2 * SSD_GROUPS * SSD_STATE
CHUNK = 128
SC_GROUPS = 16
SC_CONV = 3
N_META = 16
META_PAD = CHUNK - N_META
IN_COLS = D_SSD + D_XBC + SSD_HEADS + 3 * D_SC
N_EXPERT_GROUPS = 4
EXPERTS_PER_GROUP = 4
N_EXPERTS = N_EXPERT_GROUPS * EXPERTS_PER_GROUP
TOP_K = 2
D_EXPERT = 512


def rmsnorm(x, g):
    xf = x.astype(jnp.float32)
    xf = xf * lax.rsqrt(jnp.mean(xf * xf, axis=-1, keepdims=True) + EPS)
    return (xf * g.astype(jnp.float32)).astype(x.dtype)

def group_rmsnorm(x, g, n_groups):
    shp = x.shape
    xf = x.astype(jnp.float32).reshape(shp[:-1] + (n_groups, shp[-1] // n_groups))
    xf = xf * lax.rsqrt(jnp.mean(xf * xf, axis=-1, keepdims=True) + EPS)
    return (xf.reshape(shp) * g.astype(jnp.float32)).astype(x.dtype)

def causal_dwconv_2(x, w):
    K = w.shape[0]
    L = x.shape[1]
    xp = jnp.pad(x, ((0, 0), (K - 1, 0), (0, 0)))
    y = xp[:, 0:L] * w[0]
    for k in range(1, K):
        y = y + xp[:, k:k + L] * w[k]
    return y

def ssd_chunked(xs, dt, A, Bm, Cm):
    dtype = xs.dtype
    b, Lp = xs.shape[0], xs.shape[1]
    nc = Lp // CHUNK
    x = xs.reshape(b, nc, CHUNK, SSD_GROUPS, SSD_HPG, SSD_HEADDIM)
    dtc = dt.reshape(b, nc, CHUNK, SSD_GROUPS, SSD_HPG)
    Bc = Bm.reshape(b, nc, CHUNK, SSD_GROUPS, SSD_STATE)
    Cc = Cm.reshape(b, nc, CHUNK, SSD_GROUPS, SSD_STATE)

    dA = jnp.moveaxis(dtc * A.reshape(SSD_GROUPS, SSD_HPG), 2, -1)
    A_cum = jnp.cumsum(dA, axis=-1)
    xdt = x * dtc.astype(dtype)[..., None]

    causal = jnp.tril(jnp.ones((CHUNK, CHUNK), dtype=bool))
    seg = A_cum[..., :, None] - A_cum[..., None, :]
    Lmat = jnp.exp(jnp.where(causal, seg, -jnp.inf)).astype(dtype)
    CB = jnp.einsum('bcqgn,bckgn->bcgqk', Cc, Bc)
    y_diag = jnp.einsum('bcgqk,bcgrqk,bckgrp->bcqgrp', CB, Lmat, xdt)

    decay_states = jnp.exp(A_cum[..., -1:] - A_cum).astype(dtype)
    states = jnp.einsum('bckgn,bcgrk,bckgrp->bcgrpn', Bc, decay_states, xdt)
    chunk_decay = jnp.exp(A_cum[..., -1]).astype(dtype)

    def step(s, inp):
        st, dec = inp
        return dec[..., None, None] * s + st, s

    s0 = jnp.zeros((b, SSD_GROUPS, SSD_HPG, SSD_HEADDIM, SSD_STATE), dtype)
    _, prev = lax.scan(step, s0, (jnp.moveaxis(states, 1, 0), jnp.moveaxis(chunk_decay, 1, 0)))
    prev = jnp.moveaxis(prev, 0, 1)

    decay_out = jnp.exp(A_cum).astype(dtype)
    y_off = jnp.einsum('bcqgn,bcgrpn,bcgrq->bcqgrp', Cc, prev, decay_out)
    return (y_diag + y_off).reshape(b, Lp, SSD_HEADS, SSD_HEADDIM)

def ssd_branch(z, xbc, dt_raw, conv_w, conv_b, dt_bias, A_log, D_skip, norm_g):
    b, L, _ = xbc.shape
    xbc = jax.nn.silu(causal_dwconv_2(xbc, conv_w) + conv_b)
    xs = xbc[..., :D_SSD].reshape(b, L, SSD_HEADS, SSD_HEADDIM)
    Bm = xbc[..., D_SSD:D_SSD + SSD_GROUPS * SSD_STATE].reshape(b, L, SSD_GROUPS, SSD_STATE)
    Cm = xbc[..., D_SSD + SSD_GROUPS * SSD_STATE:].reshape(b, L, SSD_GROUPS, SSD_STATE)
    dt = jax.nn.softplus((dt_raw + dt_bias).astype(jnp.float32))
    A = -jnp.exp(A_log.astype(jnp.float32))

    def front_pad(t):
        return jnp.pad(t, ((0, 0), (META_PAD, 0)) + ((0, 0),) * (t.ndim - 2))

    y = ssd_chunked(front_pad(xs), front_pad(dt), A, front_pad(Bm), front_pad(Cm))[:, META_PAD:]
    y = y + D_skip[:, None] * xs
    y = y.reshape(b, L, D_SSD)
    return group_rmsnorm(y * jax.nn.silu(z), norm_g, SSD_GROUPS)

def short_conv_branch(gate_b, gate_c, h, conv_w, norm_g):
    v = causal_dwconv_2(gate_c * h, conv_w)
    return group_rmsnorm(gate_b * v, norm_g, SC_GROUPS)

def hier_moe(u, wg_r, bg_r, we_r, be_r, w_gate, w_up, w_down):
    b, L, d = u.shape
    t = u.reshape(b * L, d)
    p_group = jax.nn.softmax((t @ wg_r + bg_r).astype(jnp.float32), axis=-1)
    g_val, g_idx = lax.top_k(p_group, 1)
    e_logits = (t @ we_r + be_r).astype(jnp.float32).reshape(-1, N_EXPERT_GROUPS, EXPERTS_PER_GROUP)
    sel = jnp.take_along_axis(e_logits, g_idx[:, :, None], axis=1)[:, 0]
    top_v, top_i = lax.top_k(sel, TOP_K)
    top_w = jax.nn.softmax(top_v, axis=-1)
    in_w = jnp.einsum('tk,tke->te', top_w, jax.nn.one_hot(top_i, EXPERTS_PER_GROUP, dtype=jnp.float32))
    grp_w = jax.nn.one_hot(g_idx[:, 0], N_EXPERT_GROUPS, dtype=jnp.float32) * g_val
    combine = (grp_w[:, :, None] * in_w[:, None, :]).reshape(-1, N_EXPERTS).astype(u.dtype)
    out = jnp.zeros_like(t)
    for e in range(N_EXPERTS):
        h = jax.nn.silu(t @ w_gate[e]) * (t @ w_up[e])
        out = out + combine[:, e:e + 1] * (h @ w_down[e])
    return out.reshape(b, L, d)

def second_inputs(seed: int = 0) -> dict:
    key = jax.random.key(seed)
    ks = jax.random.split(key, 24)
    f32 = jnp.float32
    nrm = lambda k, shp, s: (jax.random.normal(k, shp, f32) * s)
    dt0 = jnp.exp(jax.random.uniform(ks[6], (DEPTH_2, SSD_HEADS), f32, np.log(1e-3), np.log(1e-1)))
    return {
        "x": jax.random.normal(ks[0], (BATCH, SEQ, D_MODEL), f32),
        "meta_tokens": nrm(ks[1], (N_META, D_MODEL), 1.0),
        "norm_mix": 1.0 + nrm(ks[2], (DEPTH_2, D_MODEL), 0.02),
        "w_in": nrm(ks[3], (DEPTH_2, D_MODEL, IN_COLS), D_MODEL ** -0.5),
        "ssd_conv_w": nrm(ks[4], (DEPTH_2, SSD_CONV, D_XBC), SSD_CONV ** -0.5),
        "ssd_conv_b": nrm(ks[5], (DEPTH_2, D_XBC), 0.02),
        "dt_bias": dt0 + jnp.log(-jnp.expm1(-dt0)),
        "A_log": jnp.log(jax.random.uniform(ks[7], (DEPTH_2, SSD_HEADS), f32, 1.0, 16.0)),
        "D_skip": 1.0 + nrm(ks[8], (DEPTH_2, SSD_HEADS), 0.1),
        "ssd_norm": 1.0 + nrm(ks[9], (DEPTH_2, D_SSD), 0.02),
        "sc_conv_w": nrm(ks[10], (DEPTH_2, SC_CONV, D_SC), SC_CONV ** -0.5),
        "sc_norm": 1.0 + nrm(ks[11], (DEPTH_2, D_SC), 0.02),
        "w_out": nrm(ks[12], (DEPTH_2, D_MIX, D_MODEL), D_MIX ** -0.5),
        "norm_ffn": 1.0 + nrm(ks[13], (DEPTH_2, D_MODEL), 0.02),
        "router_group_w": nrm(ks[14], (DEPTH_2, D_MODEL, N_EXPERT_GROUPS), D_MODEL ** -0.5),
        "router_group_b": nrm(ks[15], (DEPTH_2, N_EXPERT_GROUPS), 0.01),
        "router_expert_w": nrm(ks[16], (DEPTH_2, D_MODEL, N_EXPERTS), D_MODEL ** -0.5),
        "router_expert_b": nrm(ks[17], (DEPTH_2, N_EXPERTS), 0.01),
        "expert_w_gate": nrm(ks[18], (DEPTH_2, N_EXPERTS, D_MODEL, D_EXPERT), D_MODEL ** -0.5),
        "expert_w_up": nrm(ks[19], (DEPTH_2, N_EXPERTS, D_MODEL, D_EXPERT), D_MODEL ** -0.5),
        "expert_w_down": nrm(ks[20], (DEPTH_2, N_EXPERTS, D_EXPERT, D_MODEL), D_EXPERT ** -0.5),
        "norm_final": 1.0 + nrm(ks[21], (D_MODEL,), 0.02),
    }

def second_block(x, meta_tokens, norm_mix, w_in, ssd_conv_w, ssd_conv_b, dt_bias, A_log, D_skip,
              ssd_norm, sc_conv_w, sc_norm, w_out, norm_ffn, router_group_w, router_group_b,
              router_expert_w, router_expert_b, expert_w_gate, expert_w_up, expert_w_down,
              norm_final):
    b = x.shape[0]
    meta = jnp.broadcast_to(meta_tokens.astype(x.dtype)[None], (b, N_META, D_MODEL))
    h = jnp.concatenate([meta, x], axis=1)
    o_z = D_SSD
    o_xbc = o_z + D_XBC
    o_dt = o_xbc + SSD_HEADS
    o_b = o_dt + D_SC
    o_c = o_b + D_SC
    for l in range(DEPTH_2):
        u = rmsnorm(h, norm_mix[l])
        proj = u @ w_in[l]
        y_ssd = ssd_branch(proj[..., :o_z], proj[..., o_z:o_xbc], proj[..., o_xbc:o_dt],
                           ssd_conv_w[l], ssd_conv_b[l], dt_bias[l], A_log[l], D_skip[l], ssd_norm[l])
        y_sc = short_conv_branch(proj[..., o_dt:o_b], proj[..., o_b:o_c], proj[..., o_c:],
                                 sc_conv_w[l], sc_norm[l])
        h = h + jnp.concatenate([y_ssd, y_sc], axis=-1) @ w_out[l]
        u2 = rmsnorm(h, norm_ffn[l])
        h = h + hier_moe(u2, router_group_w[l], router_group_b[l], router_expert_w[l],
                         router_expert_b[l], expert_w_gate[l], expert_w_up[l], expert_w_down[l])
    return rmsnorm(h, norm_final)[:, N_META:]


def setup_inputs(seed=0):
    out = dict(first_inputs(seed))
    for name, value in second_inputs(seed + 1).items():
        if name != "x":
            out[name + "_2"] = value
    return out


def reference(
    x, positions, norm_mix, w_in, mlstm_conv_w, mlstm_conv_b, mlstm_i_bias, mlstm_f_bias,
    mlstm_norm, rglru_conv_w, rglru_conv_b, rglru_w_a, rglru_b_a, rglru_w_x, rglru_b_x,
    rglru_lambda, w_branch, w_out, norm_ffn, ffn_up, ffn_conv_w, ffn_conv_b, ffn_down,
    norm_final, meta_tokens_2, norm_mix_2, w_in_2, ssd_conv_w_2, ssd_conv_b_2, dt_bias_2,
    A_log_2, D_skip_2, ssd_norm_2, sc_conv_w_2, sc_norm_2, w_out_2, norm_ffn_2,
    router_group_w_2, router_group_b_2, router_expert_w_2, router_expert_b_2, expert_w_gate_2,
    expert_w_up_2, expert_w_down_2, norm_final_2,
):
    x = first_block(
        x, positions, norm_mix, w_in, mlstm_conv_w, mlstm_conv_b, mlstm_i_bias, mlstm_f_bias,
        mlstm_norm, rglru_conv_w, rglru_conv_b, rglru_w_a, rglru_b_a, rglru_w_x, rglru_b_x,
        rglru_lambda, w_branch, w_out, norm_ffn, ffn_up, ffn_conv_w, ffn_conv_b, ffn_down,
        norm_final,
    )
    return second_block(
        x, meta_tokens_2, norm_mix_2, w_in_2, ssd_conv_w_2, ssd_conv_b_2, dt_bias_2, A_log_2,
        D_skip_2, ssd_norm_2, sc_conv_w_2, sc_norm_2, w_out_2, norm_ffn_2, router_group_w_2,
        router_group_b_2, router_expert_w_2, router_expert_b_2, expert_w_gate_2, expert_w_up_2,
        expert_w_down_2, norm_final_2,
    )


_drawn_inputs = setup_inputs


def setup_inputs(seed=0):
    import zlib

    import numpy as np

    out = dict(_drawn_inputs(seed))
    spreads = {}
    factors = {'mlstm_i_bias': 64.0,
     'rglru_b_a': 7.557,
     'rglru_b_x': 3.866,
     'ssd_norm_2': 10.044,
     'sc_norm_2': 11.072,
     'router_group_b_2': 24.818,
     'router_expert_b_2': 39.574,
     'norm_final_2': 8.067,
     'mlstm_conv_b': 2.917,
     'mlstm_norm': 2.784,
     'ssd_conv_b_2': 3.128,
     'norm_ffn_2': 7.451}
    for name, (base, spread) in spreads.items():
        noise = np.random.default_rng([zlib.crc32(name.encode()), seed]).standard_normal(out[name].shape)
        drawn = base * np.exp(spread * noise) if base else spread * noise
        out[name] = __import__('jax').numpy.asarray(drawn.astype(out[name].dtype))
    for name, factor in factors.items():
        out[name] = (out[name] * factor).astype(out[name].dtype)
    return out
```

```python
import math
from contextlib import ExitStack

import numpy as np

import concourse.bass as bass
from concourse import mybir

F32 = mybir.dt.float32
F32R = mybir.dt.float32r
I32 = mybir.dt.int32
ALU = mybir.AluOpType
ACT = mybir.ActivationFunctionType
AX_X = mybir.AxisListType.X

P = 128
T = 256
D = 1024
KT = D // P
DEPTH = 2
DB = 512
NB = DB // P
DFF = 3072
EPS = 1e-6
HEADS_M = 4
HEADS_A = 8
TOPK = 64
BIG = 1e30
GONE = -3e38

C_MQK, C_MV, C_MO, C_MI, C_RX, C_RG = 0, 1024, 1536, 2048, 2056, 2568
C_AQ, C_AK, C_AV, C_AQI, C_AKI, C_GATE = 3080, 3592, 4104, 4616, 5128, 5200

M_NORM, M_CW, M_CB, M_G, M_RW, M_RB, M_BA, M_BX, M_LAM, M_IB, M_FB, M_N = (
    0, 8, 40, 48, 52, 68, 72, 76, 80, 84, 85, 86)
F_CW, F_CB, F_NORM, F_N = 0, 72, 96, 104
K_ID, K_ROT, K_ONE64, K_CAUS, K_VIS, K_INV, K_N = 0, 128, 256, 384, 640, 896, 897

RING = 3
SECTION = [("rx", 0), ("rx", 1), ("rg", 0), ("rg", 1), ("qi", 0), ("qi", 1), ("q", 0), ("q", 1),
           ("k", 0), ("k", 1), ("v", 0), ("v", 1), ("mqk", 0), ("mqk", 1), ("mqk", 2), ("mqk", 3),
           ("mv", 0), ("mv", 1), ("mo", 0), ("mo", 1)]
for _branch in (1, 0, 2):
    for _half in range(2):
        SECTION += [("gate", (_branch, 2 * _half)), ("gate", (_branch, 2 * _half + 1)), ("wb", (_branch, _half))]
SECTION += [("wo", _i) for _i in range(4)]
MIX = len(SECTION)
FFN = 3 * (DFF // 256)
PER_LAYER = MIX + FFN
assert MIX % RING == 0 and FFN % RING == 0
SECTION_COL = {"rx": C_RX, "rg": C_RG, "qi": C_AQI, "q": C_AQ, "k": C_AK, "v": C_AV, "mqk": C_MQK,
               "mv": C_MV, "mo": C_MO}
DVE_EVACUATES = ("rx", "mqk", "wb", "wo")


def groups_of(c):
    return 2 if SECTION[c][0] == "wb" else 1


GROUP0 = [sum(groups_of(i) for i in range(c)) for c in range(MIX + 1)]
G_MIX = GROUP0[MIX]
G_LAYER = G_MIX + FFN
assert G_MIX % 2 == 0


def evacuations(c, dve):
    return sum(groups_of(i) for i in range(c)
               if SECTION[i][0] != "wo" and (SECTION[i][0] in DVE_EVACUATES) == dve)


EV_ACT = evacuations(MIX, False)
EV_DVE = evacuations(MIX, True)
GATES = [c for c in range(MIX) if SECTION[c][0] == "gate"]
WB = [c for c in range(MIX) if SECTION[c][0] == "wb"]
META = 16
TM = META + T
HEADS_S, STATE, GROUPS_S = 16, 128, 4
N_EXP, D_EXP = 16, 512
D_XBC = 2048
SECTION_2 = ([("x", i) for i in range(4)] + [("B", i) for i in range(2)] + [("C", i) for i in range(2)]
             + [("z", i) for i in range(4)] + [("c", i) for i in range(4)] + [("h", i) for i in range(4)]
             + [("b", i) for i in range(4)])
COL_2 = {"z": 0, "x": 1024, "B": 2048, "C": 2560, "dt": 3072, "b": 3088, "c": 4112, "h": 5136}
IN_2 = len(SECTION_2)
OUT_2 = 8
MIX_2 = IN_2 + OUT_2
CHUNKS_2 = MIX_2 + 6 * N_EXP
DVE_EVACUATES_2 = ("x", "B", "C", "h", "b")
Q_NFIN, Q_NMIX, Q_CW, Q_CB, Q_D, Q_G, Q_SW, Q_SG, Q_NFF, Q_NOUT, Q_DT, Q_AL, Q_RB, Q_N = (
    0, 8, 16, 80, 96, 104, 112, 136, 144, 152, 160, 161, 162, 163)
SPAN = ((0, 0, T), (P - META, T, T - P + META), (2 * P - META, 2 * T - P + META, META))
S_COLS = SPAN[2][1] + META


def evacuations_2(c, dve):
    return 2 * sum(1 for i in range(c) if (SECTION_2[i][0] in DVE_EVACUATES_2) == dve)


def moe_group(n, part):
    if part == 2:
        return 2 * MIX_2 + (3 * n + 5 if not (isinstance(n, int) and n == 2 * N_EXP - 1) else 6 * N_EXP)
    if isinstance(n, int) and n == 0:
        return 2 * MIX_2 + 1 + part
    return 2 * MIX_2 + 3 * n + part


MERGE = max(WB)
BRANCHES = (1, 0, 2)
N_FF = DFF // 256


def ff_group(n, part):
    if part == 2:
        return G_MIX + 3 * n + 5 - (1 if isinstance(n, int) and n == N_FF - 1 else 0) * 2
    if isinstance(n, int) and n == 0:
        return G_MIX + 1 + part
    return G_MIX + 3 * n + part

COUNT = dict(
    hi_ready=PER_LAYER, lo_ready=PER_LAYER, group_done=G_LAYER, evac_act=EV_ACT, evac_dve=EV_DVE,
    landed0=16 * PER_LAYER // RING, landed1=16 * PER_LAYER // RING, landed2=16 * PER_LAYER // RING,
    own_act=50, own_dve=228, params=1, par_w=64, small_landed=64, small_hi=1, small_lo=1, small_done=1,
    squares=8, squares_added=2, sum_done=2, std_ready=2, scaled=16, act_hi=8, act_lo=8, x_ready=8,
    conv_tap=6, silu_done=4,
    lam_abs=1, lam_exp=1, lam_ready=1, lru_gates=2, lru_i=1, lru_in=1, lru_a=1, lru_ratio=1, lru_root=1,
    y_ready=5, yc_ready=1, y_hi=6, y_lo=6,
    rows_ready=1, f_abs=1, f_exp=1, a_row=1, m_row=1, em_row=1, aw_turned=1, aw_ready=1,
    rope_cos=6, rope_turned=7, rope_done=7, idx_done=6, idx_relu=6, idx_used=6, mask_ready=2,
    att_done=6, logits_ready=6, max_ready=2, prob_exp=2, prob_ready=2, turn_done=6, turned=6, pv_done=2, pv_out=1,
    ml_rows=4, ml_sub=4, ml_exp=4, ml_weight=4, ml_num=4, ml_h=4, ml_mean=4, ml_cent=4, ml_sq=4, ml_var=4,
    ml_std=4, ml_emb=4, wb_sum=8, merged_hi=4, merged_lo=4,
    ff_tap=N_FF, ff_conv=N_FF, ff_gelu=N_FF, ff_prod=N_FF, ff_hi=N_FF, ff_lo=N_FF,
)


def program(nc, xT, positions, par_1, consts, w_in, w_a, w_x, w_branch, w_out, ffn_up, ffn_down,
            par_2, mask_2, metaT, w_in_2, w_out_2, w_group, w_expert, e_gate, e_up, e_down, out):
    ctx = ExitStack()
    with ctx:
        first, second = ExitStack(), ExitStack()

        def sb(name, shape, dt=F32, scope=ctx):
            return scope.enter_context(nc.sbuf_tensor(name, shape, dt))

        psum = [ctx.enter_context(nc.psum_tensor(f"bank{i}", [P, 512], F32)) for i in range(8)]
        main = psum[0:2]
        sem = {n: ctx.enter_context(nc.semaphore(n)) for n in COUNT}
        for n in ("small_2", "par_2", "meta_ready", "dt_raw", "dt_abs", "dt_exp", "dt_done", "a_exp", "state_turned", "state_cols", "x_turned",
                  "x_scaled", "cb_done", "cb_ready", "decay_rows", "decay_sub", "decay_exp", "decay_weight",
                  "ssd_y", "ssd_out", "ssd_gated", "ssd_sq", "ssd_sum", "ssd_std", "ssd_norm",
                  "y2_hi", "y2_lo", "tap_2", "ev_act_2", "ev_dve_2", "silu_2", "sc_tap", "sc_conv", 
                  "sc_sq", "sc_sum", "sc_std", "sc_norm", "x2_ready", "router_done", "router_rows",
                  "router_turned", "router_max", "router_exp", "pair_max", "pair_exp", "combine_ready", "combine_turned", "combine_rows",
                  "spread_done", "combine_all", "moe_silu", "moe_scaled", "moe_prod", "moe_hi", "moe_lo",
                  "x_loaded", "const_loaded", "pos_loaded", "par_loaded", "setup_dve", "setup_act", "stored",
                  "own_pool", "zeros_ready"):
            sem[n] = ctx.enter_context(nc.semaphore(n))

        x_t = sb("x_t", [P, KT, T])
        w_raw = [sb(f"w_raw{i}", [P, 2048]) for i in range(RING)]
        w_hi = [sb(f"w_hi{i}", [P, 2048], F32R) for i in range(RING)]
        w_lo = [sb(f"w_lo{i}", [P, 2048], F32R) for i in range(RING)]
        cst = sb("cst", [P, K_N])
        ones = sb("ones", [P, T])
        eps = sb("eps", [P, 1])
        act_h = sb("act_h", [P, KT, T], F32R, first)
        act_l = sb("act_l", [P, KT, T], F32R, first)
        cos_t = sb("cos_t", [P, T], scope=first)
        sin_t = sb("sin_t", [P, T], scope=first)
        par_all = sb("par_all", [P, DEPTH, M_N + F_N], scope=first)
        par = sb("par", [P, M_N + F_N], scope=first)
        pm, pf = par[:, 0:M_N], par[:, M_N:M_N + F_N]
        wa = sb("wa", [P, NB, P], scope=first)
        wx = sb("wx", [P, NB, P], scope=first)
        lam8 = sb("lam8", [P, 2, NB], scope=first)
        y_h = [sb(f"y_h{i}", [P, NB, T], F32R, first) for i in range(2)]
        y_l = [sb(f"y_l{i}", [P, NB, T], F32R, first) for i in range(2)]
        work = sb("work", [P, 78 * T], scope=first)
        tiny = sb("tiny", [P, 896], scope=first)
        first.close()

        hx = sb("hx", [P, KT, TM], scope=second)
        act2_h = sb("act2_h", [P, KT, TM], F32R, second)
        act2_l = sb("act2_l", [P, KT, TM], F32R, second)
        y2_h = sb("y2_h", [P, 2 * KT, T], F32R, second)
        y2_l = sb("y2_l", [P, 2 * KT, T], F32R, second)
        dt_w = sb("dt_w", [P, KT, HEADS_S], scope=second)
        p2 = sb("p2", [P, Q_N], scope=second)
        w_route = sb("w_route", [P, KT, 20], scope=second)
        meta = sb("meta", [P, KT, META], scope=second)
        mask2 = sb("mask2", [P, S_COLS], scope=second)
        work2 = sb("work2", [P, 60 * T], scope=second)
        second.close()

        def at(kb, *shape):
            n = int(np.prod(shape))
            o = int(kb * T)
            ap = work[:, o:o + n]
            if len(shape) == 1:
                return ap
            names = "abcd"[:len(shape)]
            return ap.rearrange(f"p ({' '.join(names)}) -> p {' '.join(names)}",
                                **{a: s for a, s in zip(names[1:], shape[1:])})

        ident = cst[:, K_ID:K_ID + P]
        rot = cst[:, K_ROT:K_ROT + P]
        norm_f = at(0, KT, T)
        qi = at(0, NB, T)
        rope_in = [at(4, 2, T), at(6, 2, T)]
        prob = at(0, HEADS_A, T)
        q_c, k_c = at(8, NB, T), at(12, NB, T)
        v_c = at(16, 2, DB)
        ki = at(20, T)
        score, score_work = at(21, T), at(22, T)
        mask = [at(23.5, P), at(24, T)]
        rope_sin = [at(25, 2, T), at(27, 2, T)]
        relu = [at(37, 2, T), at(39, 2, T)]
        lru_x, lru_g, lru_r, lru_i, lru_t = (at(29 + 4 * i, NB, T) for i in range(5))
        prob_t = at(29, 2, HEADS_A, P)
        merged = at(37, KT, T)
        mqk = at(49, 2 * NB, T)
        mv = at(57, 2, DB)
        mo = at(61, NB, T)
        e_m, w_m = at(65, 384), at(66.5, 384)
        em_b, den_b, h_m, c_m, s_m, std_m = (at(68 + i, T) for i in range(6))
        gate = at(74, NB, T)
        small_raw = at(74, KT, P)
        small_h = y_h[1][:].rearrange("p b t -> p (b t)").rearrange("p (k m) -> p k m", k=KT)
        small_l = y_l[1][:].rearrange("p b t -> p (b t)").rearrange("p (k m) -> p k m", k=KT)
        sums_std, sums_r = at(65, T), at(66, T)
        f_row, t0, t1, t2, t3, g_row = (work[0:4, (53 + i) * T:(54 + i) * T] for i in range(6))
        rope_ki, f_in, ki_sin = at(49, T), at(50, T), at(51, T)
        iw = tiny[0:12, 0:T]
        m_row, em_r = tiny[0:4, T:2 * T], tiny[0:4, 2 * T:3 * T]
        lt = [tiny[:, 768 + 4 * i:772 + 4 * i] for i in range(5)]
        aw = tiny[:, 800:824].rearrange("p (s j) -> p s j", s=2)
        top8, a_max, a_sum, a_neg = (tiny[:, 824 + 8 * i:832 + 8 * i] for i in range(4))
        spare, spare_act = tiny[:, 856:857], tiny[:, 857:858]
        hid_f, ff_c, ff_g = at(0, 2, T), at(2, 2, T), at(4, 2, T)
        hid_h, hid_l = y_h[0], y_l[0]
        merge_t = [at(8, 2, T), at(10, 2, T)]
        y_attn = at(45, NB, T)

        def at2(col, *shape):
            n = int(np.prod(shape))
            ap = work2[:, col:col + n]
            if len(shape) == 1:
                return ap
            names = "abcd"[:len(shape)]
            return ap.rearrange(f"p ({' '.join(names)}) -> p {' '.join(names)}",
                                **{a: s for a, s in zip(names[1:], shape[1:])})

        o = 0
        norm_f2 = at2(o, KT, TM)
        v_sc = at2(o, KT, T)
        o += KT * TM
        xs = at2(o, KT, TM)
        o += KT * TM
        b_s, c_s = at2(o, 4, TM), at2(o + 4 * TM, 4, TM)
        ch = at2(o, KT, TM)
        o += KT * TM
        xdt = at2(o, 3, D)
        rows2 = [work2[0:HEADS_S, o + TM * i:o + TM * i + TM] for i in range(6)]
        combine = at2(KT * TM, N_EXP, T)
        o += 3 * D
        cb = at2(o, GROUPS_S, S_COLS)
        o += GROUPS_S * S_COLS
        decay = [at2(o + S_COLS * i, S_COLS) for i in range(2)]
        weight = [at2(o + S_COLS * (2 + i), S_COLS) for i in range(2)]
        o += 4 * S_COLS
        gy, gsq = at2(o, 2, T), at2(o + 2 * T, 2, T)
        o += 4 * T
        g_std = at2(o, T)
        o += T
        sc_s = at2(o, 2, T)
        o += 2 * T
        cols2 = at2(o, 3, 2 * HEADS_S)
        o += 6 * HEADS_S
        a_col = at2(o, 1)
        decay_row = work2[0:HEADS_S, o + 1:o + 1 + TM]
        o += 1 + TM
        assert o <= 60 * T, o
        zs = x_t
        m_sg, m_hf = at2(KT * TM + N_EXP * T, 2, T), at2(KT * TM + N_EXP * T + 2 * T, 2, T)
        rt = at2(KT * TM + N_EXP * T + 4 * T, 2, 20)
        r_base = KT * TM + N_EXP * T + 4 * T + 64
        route = [at2(r_base + 8 * i, 2, 4) for i in range(8)]
        rcol = [at2(r_base + 64 + 2 * i, 2) for i in range(8)]
        comb_t = at2(r_base + 96, 2, N_EXP)
        lg = work2[0:20, r_base + 128:r_base + 128 + T]
        comb_row = work2[0:N_EXP, r_base + 128 + T:r_base + 128 + 2 * T]
        norm2_std, norm2_r = work2[:, 2 * KT * TM:2 * KT * TM + TM], work2[:, 2 * KT * TM + TM:2 * KT * TM + 2 * TM]
        fin_std, fin_r = at2(KT * TM, T), at2(KT * TM + T, T)

        def need(eng, name, L, k):
            v = L * COUNT[name] + k
            if not isinstance(v, int) or v > 0:
                eng.wait_ge(sem[name], v)

        class Own:

            def __init__(self, eng, name):
                self.eng, self.sem, self.base, self.k, self.outer = eng, sem[name], 0, 0, []

            def __call__(self, ins):
                ins.then_inc(self.sem, 1)
                self.k += 1

            def settle(self):
                self.eng.wait_ge(self.sem, self.base + self.k)

            def enter(self, rounds_before, each):
                self.outer.append((self.base, self.k))
                self.base, self.k = self.base + self.k + rounds_before * each, 0

            def leave(self, rounds, each):
                assert self.k == each, (self.k, each)
                self.base, self.k = self.outer.pop()
                self.k += rounds * each

        def landed(c):
            return f"landed{c % RING}"

        def slot_free(eng, L, c, n=0):
            if isinstance(n, int) and c + 3 * n < RING:
                need(eng, "group_done", L, 0)
            elif isinstance(n, int) and c + 3 * n - RING < MIX:
                need(eng, "group_done", L, GROUP0[c + 3 * n - RING + 1])
            else:
                need(eng, "group_done", L, 3 * n + (G_MIX + c - RING - MIX + 1))

        def slot_free_2(eng, c, e=0):
            if isinstance(e, int) and c + 6 * e < RING:
                need(eng, "group_done", DEPTH, 0)
            elif isinstance(e, int) and c + 6 * e - RING < MIX_2:
                need(eng, "group_done", DEPTH, 2 * (c + 6 * e - RING + 1))
            else:
                need(eng, "group_done", DEPTH, 6 * e + (2 * MIX_2 + c - RING - MIX_2 + 1))

        block = ctx.enter_context(nc.Block())

        @block.sync
        def _(sp):
            sp.dma_start(cst[:], consts).then_inc(sem["const_loaded"], 16)
            sp.dma_start(x_t[:], xT.rearrange("(k p) t -> p k t", p=P)).then_inc(sem["x_loaded"], 16)
            sp.dma_start(work[:, 0:T].bitcast(I32), positions.rearrange("a t -> (a t)").partition_broadcast(P)).then_inc(sem["pos_loaded"], 16)

            sp.dma_start(par_all[:], par_1.rearrange("l p n -> p l n")).then_inc(sem["par_loaded"], 16)

            def tiles(w, rows, cols):
                return w[:, rows, cols].rearrange("l (t p) c -> p (l t) c", p=P)

            def source(L, c):
                kind, i = SECTION[c]
                if kind == "wb":
                    j, half = i
                    return w_branch.rearrange("l j r c -> (l j r) c")[bass.ds(L * 3 * DB + j * DB, DB),
                                                                     half * 512:half * 512 + 512]\
                        .rearrange("(t p) c -> p t c", p=P)
                if kind == "wo":
                    return tiles(w_out[bass.ds(L, 1)], slice(0, D), slice(i * 256, i * 256 + 256))
                if kind == "gate":
                    col = C_GATE + i[0] * D + i[1] * 256
                else:
                    col = SECTION_COL[kind] + i * 256
                if col == 0:
                    return w_in.rearrange("l r c -> (l r) c")[bass.ds(L * D, D), 0:256].rearrange("(t p) c -> p t c", p=P)
                return tiles(w_in[bass.ds(L, 1)], slice(0, D), slice(col, col + 256))

            def ffn_source(L, part, n):
                if part < 2:
                    return tiles(ffn_up[bass.ds(L, 1)], slice(0, D), bass.ds(part * DFF + n * 256, 256))
                return tiles(ffn_down[bass.ds(L, 1)], bass.ds(n * 256, 256), slice(0, D))

            def load(L, c, src, n=0):
                need(sp, "lo_ready", L, 3 * n + max(0, c - RING + 1))
                sp.dma_start(w_raw[c % RING][:].rearrange("p (t c) -> p t c", t=src.shape[1]), src)\
                    .then_inc(sem[landed(c)], 16)

            def load_small(L):
                need(sp, "lru_gates", L, 0)
                for dst, src in ((wa, w_a), (wx, w_x)):
                    for odd in range(2):
                        blocks = src[bass.ds(L, 1)].rearrange("l (b o) d e -> o d (l b) e", o=2)[odd]
                        sp.dma_start(dst[64 * odd:64 * odd + 64, :, 64 * odd:64 * odd + 64], blocks)\
                            .then_inc(sem["par_w"], 16)
                need(sp, "merged_lo", L, 0)
                for dst, col, n in ((0, C_MI, 4), (4, C_AKI + 64, 8), (32, C_MI + 4, 4), (64, C_AKI, 64)):
                    sp.dma_start(small_raw[:, :, dst:dst + n], tiles(w_in[bass.ds(L, 1)], slice(0, D), slice(col, col + n)))\
                        .then_inc(sem["small_landed"], 16)

            def load_2(c, src, e=0):
                need(sp, "lo_ready", DEPTH, 6 * e + max(0, c - RING + 1))
                sp.dma_start(w_raw[c % RING][:].rearrange("p (t c) -> p t c", t=src.shape[1]), src)\
                    .then_inc(sem[landed(c)], 16)

            def source_2(c):
                if c < IN_2:
                    kind, i = SECTION_2[c]
                    col = COL_2[kind] + 256 * i
                    return tiles(w_in_2, slice(0, D), slice(col, col + 256))
                pair, half = (c - IN_2) // 2, (c - IN_2) % 2
                return tiles(w_out_2, slice(half * D, half * D + D), slice(pair * 256, pair * 256 + 256))

            def expert_source(e, half, part):
                cut = slice(half * 256, half * 256 + 256)
                if part == 2:
                    return tiles(e_down[0][bass.ds(e, 1)], cut, slice(0, D))
                return tiles((e_gate, e_up)[part][0][bass.ds(e, 1)], slice(0, D), cut)

            def layer(L, next_source):
                load(L, 2, source(L, 2))
                sp.wait_ge(sem["zeros_ready"], 1)
                load_small(L)
                for c in range(RING, MIX):
                    load(L, c, source(L, c))
                load(L, MIX, ffn_source(L, 0, 0))
                load(L, MIX + 1, ffn_source(L, 1, 0))
                if isinstance(L, int):
                    need(sp, "y_lo", L, 6)
                    for dst, src in ((p2[:], par_2), (mask2[:], mask_2),
                                     (meta[:], metaT.rearrange("(k p) t -> p k t", p=P)),
                                     (w_route[:, :, 0:4], w_group[0].rearrange("(k p) n -> p k n", p=P)),
                                     (w_route[:, :, 4:20], w_expert[0].rearrange("(k p) n -> p k n", p=P)),
                                     (dt_w[:], w_in_2[0][:, COL_2["dt"]:COL_2["dt"] + HEADS_S]
                                      .rearrange("(k p) n -> p k n", p=P))):
                        sp.dma_start(dst, src).then_inc(sem["par_2"], 16)
                with sp.Fori(0, N_FF - 1) as n:
                    load(L, MIX + 2, ffn_source(L, 0, n + 1), n)
                    load(L, MIX + 3, ffn_source(L, 1, n + 1), n)
                    load(L, MIX + 4, ffn_source(L, 2, n), n)
                load(L, PER_LAYER - 1, ffn_source(L, 2, N_FF - 1))
                load(L, PER_LAYER, next_source(0))
                load(L, PER_LAYER + 1, next_source(1))

            load(0, 0, source(0, 0))
            load(0, 1, source(0, 1))
            with sp.Fori(0, DEPTH - 1) as L:
                layer(L, lambda c: source(L + 1, c))
            layer(DEPTH - 1, source_2)

            for c in range(2, MIX_2):
                load_2(c, source_2(c))
            load_2(MIX_2, expert_source(0, 0, 0))
            load_2(MIX_2 + 1, expert_source(0, 0, 1))

            def half_expert(e, half):
                c = MIX_2 + 3 * half - 1
                load_2(c, expert_source(e, half, 0), e)
                load_2(c + 1, expert_source(e, half, 1), e)
                load_2(c + 2, expert_source(e, 0, 2) if half else expert_source(e - 1, 1, 2), e)

            half_expert(0, 1)
            with sp.Fori(1, N_EXP) as e:
                half_expert(e, 0)
                half_expert(e, 1)
            load_2(CHUNKS_2 - 1, expert_source(N_EXP - 1, 1, 2))
            for i in range(4):
                need(sp, "scaled", DEPTH, 8 + 8 + 8 + 2 * i + 2)
                sp.dma_start(out.rearrange("(k p) t -> p k t", p=P)[:, 2 * i:2 * i + 2, :],
                             norm_f2[:, 2 * i:2 * i + 2, 0:T]).then_inc(sem["stored"], 16)
            sp.wait_ge(sem["stored"], 64)

        @block.gpsimd
        def _(pool):
            own = Own(pool, "own_pool")
            own(nc.gpsimd.memset(wa[:], 0.0))
            own(nc.gpsimd.memset(wx[:], 0.0))
            own(nc.gpsimd.memset(small_raw, 0.0))
            own(nc.gpsimd.memset(eps[:], EPS))
            own.settle()
            nc.gpsimd.memset(ones[:], 1.0).then_inc(sem["zeros_ready"], 1)

            def layer(L):
                need(pool, "x_ready", L, 0)
                nc.gpsimd.tensor_copy(par[:], par_all[:, bass.ds(L, 1), :].rearrange("p l n -> p (l n)"))\
                    .then_inc(sem["params"], 1)
                for i in range(6):
                    dst = (qi, q_c, k_c)[i // 2][:, 2 * (i % 2):2 * (i % 2) + 2, :]
                    need(pool, "evac_act", L, 2 + i + 1)
                    if i == 0:
                        need(pool, "act_lo", L, 4)
                    nc.gpsimd.tensor_tensor(dst, rope_in[i % 2], cos_t[:].unsqueeze(1).to_broadcast([P, 2, T]),
                                            ALU.mult).then_inc(sem["rope_cos"], 1)
                for i in range(8):
                    b = 2 * (i % 4)
                    c = WB[2 + i // 2]
                    need(pool, "evac_dve", L, evacuations(c, True) + i % 2 + 1)
                    nc.gpsimd.tensor_tensor(merged[:, b:b + 2, :], merged[:, b:b + 2, :], merge_t[i % 2],
                                            ALU.add).then_inc(sem["wb_sum"], 1)

            pool.wait_ge(sem["par_loaded"], 16)
            pool.wait_ge(sem["setup_act"], 2)
            with pool.Fori(0, DEPTH) as L:
                layer(L)

            pool.wait_ge(sem["par_2"], 96)
            pool.wait_ge(sem["x_ready"], DEPTH * 8)
            nc.gpsimd.tensor_copy(hx[:, :, 0:META], meta[:]).then_inc(sem["meta_ready"], 1)


        @block.scalar
        def _(act):
            own = Own(act, "own_act")
            A = nc.scalar.activation

            def split(L, c, n=0):
                need(act, landed(c), L, 16 * n + 16 * (c // RING + 1))
                slot_free(act, L, c, n)
                nc.scalar.copy(w_hi[c % RING][:], w_raw[c % RING][:]).then_inc(sem["hi_ready"], 1)

            def norm(L, which):
                own(A(spare_act, eps[:], ACT.Sqrt))
                for i in range(4):
                    need(act, "x_ready", L, i + 1 if which else 0)
                    A(norm_f[:, 2 * i:2 * i + 2, :], x_t[:, 2 * i:2 * i + 2, :], ACT.Square)\
                        .then_inc(sem["squares"], 1)
                need(act, "sum_done", L, which + 1)
                A(sums_std, psum[7][:, 0:T], ACT.Sqrt, bias=eps[:], scale=1.0 / D).then_inc(sem["std_ready"], 1)
                for i in range(4):
                    need(act, "scaled", L, 8 * which + 2 * i + 2)
                    nc.scalar.copy(act_h[:, 2 * i:2 * i + 2, :], norm_f[:, 2 * i:2 * i + 2, :])\
                        .then_inc(sem["act_hi"], 1)

            def evacuate(L, c):
                kind, i = SECTION[c]
                g = GROUP0[c]
                if kind in ("wb", "wo"):
                    return
                need(act, "group_done", L, g + 1)
                ps = main[g % 2][:].rearrange("p (b t) -> p b t", b=2)
                if kind in ("rx", "mqk"):
                    dst, w, b, n = (lru_x, M_RW + 3 * 4, M_RB, 0) if kind == "rx" else (mqk, M_CW + 3 * 8, M_CB, 2)
                    for h in range(2):
                        j = 2 * i + h
                        ins = A(dst[:, j, :], ps[:, h, :], ACT.Identity, bias=pm[:, b + j:b + j + 1],
                                scale=pm[:, w + j:w + j + 1])
                        if h == 0:
                            own(ins)
                        else:
                            ins.then_inc(sem["conv_tap"], 1)
                    return
                if kind == "rg":
                    ins = A(lru_g[:, 2 * i:2 * i + 2, :], ps, ACT.Gelu_apprx_tanh)
                elif kind in ("qi", "q", "k"):
                    n = c - 4
                    if n >= 2:
                        need(act, "rope_cos", L, n - 1)
                        need(act, "rope_turned", L, n if n > 2 else 1)
                    ins = nc.scalar.copy(rope_in[n % 2], ps)
                elif kind == "v":
                    ins = nc.scalar.copy(v_c[:, :, i * 256:i * 256 + 256], ps)
                elif kind == "mv":
                    ins = nc.scalar.copy(mv[:, :, i * 256:i * 256 + 256], ps)
                elif kind == "mo":
                    ins = A(mo[:, 2 * i:2 * i + 2, :], ps, ACT.Sigmoid)
                elif kind == "gate":
                    before_it = [w for w in WB if w < c]
                    if before_it:
                        need(act, "evac_dve", L, evacuations(before_it[-1] + 1, True))
                    b = 2 * (i[1] % 2)
                    ins = A(gate[:, b:b + 2, :], ps, ACT.Sigmoid)
                ins.then_inc(sem["evac_act"], 1)

            def silu(L, i):
                need(act, "evac_dve", L, 2 + i + 1)
                A(mqk[:, 2 * i:2 * i + 2, :], mqk[:, 2 * i:2 * i + 2, :], ACT.Silu).then_inc(sem["silu_done"], 1)

            def before(L):
                norm(L, 0)
                split(L, 2)
                need(act, "small_landed", L, 64)
                nc.scalar.copy(small_h, small_raw).then_inc(sem["small_hi"], 1)
                need(act, "lam_abs", L, 1)
                A(lt[1], lt[0], ACT.Exp, scale=-1.0).then_inc(sem["lam_exp"], 1)

            def attention_exp(L, tile):
                width = T if tile == 0 else P
                need(act, "max_ready", L, tile + 1)
                for h in range(HEADS_A):
                    pr = prob[:, h, 0:width]
                    ins = A(pr, pr, ACT.Exp, bias=a_neg[:, h:h + 1], accum_out=a_sum[:, h:h + 1])
                    if h < HEADS_A - 1:
                        own(ins)
                    else:
                        ins.then_inc(sem["prob_exp"], 1)

            def turned(L, i):
                need(act, "turn_done", L, i + 1)
                ps = psum[2 + i % 2]
                s, half = (i // 2, i % 2) if i < 4 else (0, i % 2)
                nc.scalar.copy(prob_t[:, s, 4 * half:4 * half + 4, :],
                               ps[:].rearrange("p (h t) -> p h t", h=4)).then_inc(sem["turned"], 1)

            def mlstm(L, stage, h):
                if stage == 1:
                    need(act, "ml_sub", L, h + 1)
                    A(e_m, e_m, ACT.Exp, scale=-1.0).then_inc(sem["ml_exp"], 1)
                    if h >= 1:
                        need(act, "ml_h", L, h)
                    nc.scalar.copy(em_b, psum[6][:, 256:512]).then_inc(sem["ml_emb"], 1)
                if stage == 3:
                    need(act, "ml_cent", L, h + 1)
                    A(s_m, c_m, ACT.Square).then_inc(sem["ml_sq"], 1)
                if stage == 4:
                    need(act, "ml_var", L, h + 1)
                    if h:
                        need(act, "y_lo", L, 1 + h)
                    A(std_m, psum[5][:, 256:512], ACT.Sqrt, bias=eps[:], scale=1.0 / P).then_inc(sem["ml_std"], 1)
                    y_upper(L, 2 + h, y_h[1][:, h, :], std_m)

            def y_upper(L, k, dst, src):
                need(act, "y_ready", L, k)
                nc.scalar.copy(dst, src).then_inc(sem["y_hi"], 1)

            def side(L, c):
                if c == 3:
                    for gate_i, dst, bias in ((0, lru_r, M_BA), (1, lru_i, M_BX)):
                        need(act, "lru_gates", L, gate_i + 1)
                        for b in range(NB):
                            bank = psum[(4, 2)[gate_i] + b // 2][:, 256 * (b % 2):256 * (b % 2) + 256]
                            ins = A(dst[:, b, :], bank, ACT.Sigmoid, bias=pm[:, bias + b:bias + b + 1])
                            if gate_i == 1 and b == NB - 1:
                                ins.then_inc(sem["lru_i"], 1)
                            else:
                                own(ins)
                    need(act, "small_done", L, 1)
                    own(A(f_in[32:36, :], psum[6][32:36, 0:T], ACT.Identity, bias=pm[32:36, M_FB:M_FB + 1]))
                    own(nc.scalar.copy(rope_ki[64:128, :], psum[6][64:128, 0:T]))
                    own.settle()
                    A(iw, psum[6][0:12, 0:T], ACT.Identity, bias=pm[0:12, M_IB:M_IB + 1])\
                        .then_inc(sem["rows_ready"], 1)
                if c == 4:
                    need(act, "lam_ready", L, 1)
                    for b in range(NB):
                        own(A(lru_t[:, b, :], lru_r[:, b, :], ACT.Tanh, scale=lam8[:, 1, b:b + 1]))
                    own.settle()
                    for b in range(NB):
                        ins = A(lru_r[:, b, :], lru_r[:, b, :], ACT.Exp, scale=lam8[:, 0, b:b + 1])
                        if b == NB - 1:
                            ins.then_inc(sem["lru_a"], 1)
                        else:
                            own(ins)
                    need(act, "f_abs", L, 1)
                    A(t1, t0, ACT.Exp, scale=-1.0).then_inc(sem["f_exp"], 1)
                if c == 5:
                    need(act, "lru_ratio", L, 1)
                    A(lru_t, lru_t, ACT.Sqrt).then_inc(sem["lru_root"], 1)
                if c == 7:
                    need(act, "m_row", L, 1)
                    A(em_r, em_r, ACT.Exp, scale=-1.0).then_inc(sem["em_row"], 1)
                if c == 6:
                    y_upper(L, 1, y_h[0][:], lru_x)
                if c in (8, 9, 10):
                    for i in (2 * (c - 8), 2 * (c - 8) + 1):
                        need(act, "idx_done", L, i + 1)
                        if i >= 2:
                            need(act, "idx_used", L, i - 1)
                        A(relu[i % 2], psum[2 + i % 2][:].rearrange("p (b t) -> p b t", b=2), ACT.Relu)\
                            .then_inc(sem["idx_relu"], 1)
                if 13 <= c <= 16:
                    silu(L, c - 13)
                if c == 13:
                    attention_exp(L, 0)
                if c == 15:
                    turned(L, 0)
                    turned(L, 1)
                if c == 16:
                    turned(L, 2)
                    turned(L, 3)
                if c == 18:
                    attention_exp(L, 1)
                if c == 20:
                    turned(L, 4)
                    turned(L, 5)
                for s in (3, 2, 1, 0):
                    h = c - 20 - s
                    if 0 <= h < 4:
                        mlstm(L, s + 1, h)
                if c == 28:
                    need(act, "yc_ready", L, 1)
                    nc.scalar.copy(y_h[0][:], y_attn).then_inc(sem["y_hi"], 1)
                if c in (MERGE - 1, MERGE):
                    for i in ((0, 1) if c < MERGE else (2, 3)):
                        need(act, "wb_sum", L, 4 + i + 1)
                        nc.scalar.copy(act_h[:, 2 * i:2 * i + 2, :], merged[:, 2 * i:2 * i + 2, :])\
                            .then_inc(sem["merged_hi"], 1)

            def ffn_gate(L, n):
                need(act, "group_done", L, ff_group(n, 0))
                if not (isinstance(n, int) and n == 0):
                    need(act, "ff_gelu", L, n)
                for h in range(2):
                    j = 2 * n + h
                    ins = A(ff_c[:, h, :], main[0][:, 256 * h:256 * h + 256], ACT.Identity,
                            bias=pf[:, bass.ds(F_CB + j, 1)], scale=pf[:, bass.ds(F_CW + 48 + j, 1)])
                    if h == 0:
                        own(ins)
                    else:
                        ins.then_inc(sem["ff_tap"], 1)

            def ffn_mid(L, n):
                need(act, "ff_conv", L, n + 1)
                A(ff_g, ff_c, ACT.Gelu_apprx_tanh).then_inc(sem["ff_gelu"], 1)

            def ffn_hidden(L, n):
                need(act, "ff_prod", L, n + 1)
                if not (isinstance(n, int) and n == 0):
                    need(act, "group_done", L, ff_group(n - 1, 2))
                nc.scalar.copy(hid_h[:, 0:2, :], hid_f).then_inc(sem["ff_hi"], 1)

            def layer(L):
                before(L)
                for c in range(MIX):
                    evacuate(L, c)
                    if c == MERGE:
                        side(L, c)
                        split(L, c + RING)
                    elif c < MIX - 1:
                        split(L, c + RING)
                        side(L, c)
                norm(L, 1)
                split(L, MIX + 2)
                ffn_gate(L, 0)
                split(L, MIX + 3)
                ffn_mid(L, 0)
                ffn_hidden(L, 0)
                split(L, MIX + 4)
                own_each = 1
                with act.Fori(1, N_FF) as n:
                    own.enter(n - 1, own_each)
                    ffn_gate(L, n)
                    split(L, MIX + 2, n)
                    ffn_mid(L, n)
                    split(L, MIX + 3, n)
                    ffn_hidden(L, n)
                    split(L, MIX + 4, n)
                own.leave(N_FF - 1, own_each)

            act.wait_ge(sem["setup_dve"], 2)
            A(sin_t[:], sin_t[:], ACT.Sin).then_inc(sem["setup_act"], 1)
            A(cos_t[:], cos_t[:], ACT.Sin).then_inc(sem["setup_act"], 1)
            act.wait_ge(sem["x_loaded"], 16)
            act.wait_ge(sem["zeros_ready"], 1)
            split(0, 0)
            split(0, 1)
            with act.Fori(0, DEPTH) as L:
                own.enter(L, COUNT["own_act"])
                layer(L)
            own.leave(DEPTH, COUNT["own_act"])

            def split_2(c, e=0):
                need(act, landed(c), DEPTH, 32 * e + 16 * (c // RING + 1))
                slot_free_2(act, c, e)
                nc.scalar.copy(w_hi[c % RING][:], w_raw[c % RING][:]).then_inc(sem["hi_ready"], 1)

            def deviation(n, out, width):
                need(act, "sum_done", DEPTH, n + 1)
                A(out, psum[7][:, 0:width], ACT.Sqrt, bias=eps[:], scale=1.0 / D).then_inc(sem["std_ready"], 1)

            def upper_2(n, width):
                for i in range(4):
                    need(act, "scaled", DEPTH, 8 * n + 2 * i + 2)
                    nc.scalar.copy(act2_h[:, 2 * i:2 * i + 2, 0:width], norm_f2[:, 2 * i:2 * i + 2, 0:width])\
                        .then_inc(sem["act_hi"], 1)

            def evacuate_2(c):
                kind, i = SECTION_2[c]
                for half in range(2):
                    g = 2 * c + half
                    j = 2 * i + half
                    ps = psum[g % 4]
                    if kind in ("h", "b"):
                        return
                    need(act, "group_done", DEPTH, g + 1)
                    if kind in ("x", "B", "C"):
                        dst, k = {"x": (xs, j), "B": (b_s, 8 + j), "C": (c_s, 12 + j)}[kind]
                        A(dst[:, j, :], ps[:, 0:TM], ACT.Identity, bias=p2[:, Q_CB + k:Q_CB + k + 1],
                          scale=p2[:, Q_CW + 48 + k:Q_CW + 49 + k]).then_inc(sem["tap_2"], 1)
                    elif kind == "z":
                        A(zs[:, j, :], ps[:, 0:T], ACT.Silu).then_inc(sem["ev_act_2"], 1)
                    else:
                        if j == 0:
                            act.wait_ge(sem["cb_ready"], 8)
                        nc.scalar.copy(ch[:, j, :], ps[:, 0:TM]).then_inc(sem["ev_act_2"], 1)

            def silu_2(i):
                dst = xs[:, 2 * i:2 * i + 2, :] if i < 4 else (b_s, c_s)[(i - 4) // 2][:, 2 * (i % 2):2 * (i % 2) + 2, :]
                act.wait_ge(sem["ev_dve_2"], 2 * i + 2)
                A(dst, dst, ACT.Silu).then_inc(sem["silu_2"], 1)

            def ssd_norm(g, part):
                if part == 0:
                    act.wait_ge(sem["ssd_gated"], g + 1)
                    A(gsq, gy, ACT.Square).then_inc(sem["ssd_sq"], 1)
                else:
                    act.wait_ge(sem["ssd_sum"], g + 1)
                    if g:
                        act.wait_ge(sem["ssd_norm"], g)
                    A(g_std, psum[6 + g % 2][:, 0:T], ACT.Sqrt, bias=eps[:], scale=1.0 / 256)\
                        .then_inc(sem["ssd_std"], 1)
                    act.wait_ge(sem["ssd_norm"], g + 1)
                    nc.scalar.copy(y2_h[:, 2 * g:2 * g + 2, :], gy).then_inc(sem["y2_hi"], 1)

            def sc_norm(i, part):
                if part == 0:
                    act.wait_ge(sem["ev_dve_2"], evacuations_2(20 + i + 1, True))
                    A(sc_s, v_sc[:, 2 * i:2 * i + 2, :], ACT.Square).then_inc(sem["sc_sq"], 1)
                else:
                    act.wait_ge(sem["sc_sum"], i + 1)
                    A(sc_s, psum[4 + i % 2][:].rearrange("p (b t) -> p b t", b=2), ACT.Sqrt, bias=eps[:],
                      scale=1.0 / 64).then_inc(sem["sc_std"], 1)
                    act.wait_ge(sem["sc_norm"], i + 1)
                    nc.scalar.copy(y2_h[:, 8 + 2 * i:10 + 2 * i, :], v_sc[:, 2 * i:2 * i + 2, :])\
                        .then_inc(sem["y2_hi"], 1)

            def side_2(c):
                if c == 1:
                    act.wait_ge(sem["small_2"], 1)
                    A(rows2[0], psum[4][0:HEADS_S, 0:TM], ACT.Identity, bias=p2[0:HEADS_S, Q_DT:Q_DT + 1])\
                        .then_inc(sem["dt_raw"], 1)
                    A(a_col[0:HEADS_S, :], p2[0:HEADS_S, Q_AL:Q_AL + 1], ACT.Exp).then_inc(sem["a_exp"], 1)
                    act.wait_ge(sem["dt_abs"], 1)
                    A(rows2[2], rows2[1], ACT.Exp, scale=-1.0).then_inc(sem["dt_exp"], 1)
                if 1 <= c <= 8:
                    silu_2(c - 1)
                if c == 9:
                    for g in range(GROUPS_S):
                        act.wait_ge(sem["cb_done"], g + 1)
                        bank = psum[(6, 7, 4, 5)[g]]
                        nc.scalar.copy(cb[:, g, 0:S_COLS - META], bank[:, 0:S_COLS - META])\
                            .then_inc(sem["cb_ready"], 1)
                        nc.scalar.copy(cb[0:META, g, S_COLS - META:], bank[0:META, S_COLS - META:S_COLS])\
                            .then_inc(sem["cb_ready"], 1)
                if 10 <= c <= 17:
                    for h in (2 * (c - 10), 2 * (c - 10) + 1):
                        act.wait_ge(sem["decay_sub"], h + 1)
                        A(decay[h % 2], decay[h % 2], ACT.Exp).then_inc(sem["decay_exp"], 1)
                if 12 <= c <= 19:
                    ssd_norm((c - 12) // 2, c % 2)
                if 17 <= c <= 20:
                    i = c - 17
                    act.wait_ge(sem["ev_dve_2"], evacuations_2(16 + i + 1, True))
                    for j in (2 * i, 2 * i + 1):
                        A(v_sc[:, j, :], ch[:, j, META:TM], ACT.Copy, scale=p2[:, Q_SW + 16 + j:Q_SW + 17 + j])\
                            .then_inc(sem["sc_tap"], 1)
                if 21 <= c <= 24:
                    sc_norm(c - 21, 0)
                    sc_norm(c - 21, 1)

            def moe_gate(n):
                need(act, "group_done", DEPTH, moe_group(n, 0))
                if not (isinstance(n, int) and n == 0):
                    act.wait_ge(sem["moe_prod"], n)
                A(m_sg, main[0][:].rearrange("p (b t) -> p b t", b=2), ACT.Silu).then_inc(sem["moe_silu"], 1)

            def moe_hidden(n):
                act.wait_ge(sem["moe_prod"], n + 1)
                if not (isinstance(n, int) and n == 0):
                    need(act, "group_done", DEPTH, moe_group(n - 1, 2))
                nc.scalar.copy(y2_h[:, 0:2, :], m_hf).then_inc(sem["moe_hi"], 1)

            act.wait_ge(sem["par_2"], 96)
            for i in range(4):
                act.wait_ge(sem["x_ready"], 8 * (DEPTH - 1) + 4 + i + 1)
                A(norm_f2[:, 2 * i:2 * i + 2, 0:T], x_t[:, 2 * i:2 * i + 2, :], ACT.Square)\
                    .then_inc(sem["squares"], 1)
            deviation(0, norm2_std[:, 0:T], T)
            for i in range(4):
                need(act, "scaled", DEPTH, 2 * i + 2)
                act.wait_ge(sem["meta_ready"], 1)
                A(norm_f2[:, 2 * i:2 * i + 2, :], hx[:, 2 * i:2 * i + 2, :], ACT.Square)\
                    .then_inc(sem["squares"], 1)
            split_2(2)
            deviation(1, norm2_std, TM)
            upper_2(1, TM)
            for c in range(MIX_2):
                if c < IN_2:
                    evacuate_2(c)
                if c < MIX_2 - 1:
                    split_2(c + RING)
                side_2(c)
            for i in range(4):
                act.wait_ge(sem["x2_ready"], 2 * i + 2)
                A(norm_f2[:, 2 * i:2 * i + 2, 0:T], hx[:, 2 * i:2 * i + 2, META:TM], ACT.Square)\
                    .then_inc(sem["squares"], 1)
            deviation(2, norm2_std[:, 0:T], T)
            upper_2(2, T)
            split_2(MIX_2 + 2)
            act.wait_ge(sem["router_done"], 1)
            A(lg, psum[6][0:20, 0:T], ACT.Identity, bias=p2[0:20, Q_RB:Q_RB + 1]).then_inc(sem["router_rows"], 1)
            act.wait_ge(sem["router_max"], 1)
            A(route[0], route[0], ACT.Exp).then_inc(sem["router_exp"], 1)
            act.wait_ge(sem["pair_max"], 1)
            A(rcol[4], rcol[4], ACT.Exp).then_inc(sem["pair_exp"], 1)
            moe_gate(0)
            split_2(MIX_2 + 3)
            for i in range(8):
                act.wait_ge(sem["spread_done"], i + 1)
                nc.scalar.copy(combine[:, 2 * i:2 * i + 2, :], psum[6 + i % 2][:].rearrange("p (b t) -> p b t", b=2))\
                    .then_inc(sem["combine_all"], 1)
            moe_hidden(0)
            split_2(MIX_2 + 4)

            def half_expert(e, half):
                moe_gate(2 * e + half)
                split_2(MIX_2 + 3 * half + 2, e)
                split_2(MIX_2 + 3 * half + 3, e)
                moe_hidden(2 * e + half)
                split_2(MIX_2 + 3 * half + 4, e)

            half_expert(0, 1)
            with act.Fori(1, N_EXP - 1) as e:
                half_expert(e, 0)
                half_expert(e, 1)
            half_expert(N_EXP - 1, 0)
            moe_gate(2 * N_EXP - 1)
            split_2(CHUNKS_2 - 1)
            moe_hidden(2 * N_EXP - 1)
            for i in range(4):
                act.wait_ge(sem["x2_ready"], 8 + i + 1)
                A(norm_f2[:, 2 * i:2 * i + 2, 0:T], hx[:, 2 * i:2 * i + 2, META:TM], ACT.Square)\
                    .then_inc(sem["squares"], 1)
            deviation(3, fin_std, T)

        @block.vector
        def _(dve):
            own = Own(dve, "own_dve")
            V = nc.vector
            STT = nc.vector.scalar_tensor_tensor

            def step(ins):
                own(ins)
                own.settle()

            def log1p_half(e, t_a, t_b, t_c):
                step(V.tensor_scalar(t_a, e, 2.0, None, ALU.add))
                step(V.reciprocal(t_b, t_a))
                step(V.tensor_tensor(t_a, e, t_b, ALU.mult))
                step(V.tensor_tensor(t_b, t_a, t_a, ALU.mult))
                step(V.tensor_scalar(t_c, t_b, 1.0 / 17.0, None, ALU.mult))
                for k in (15, 13, 11, 9, 7, 5, 3):
                    step(STT(t_c, t_c, 1.0 / k, t_b, ALU.add, ALU.mult))
                step(STT(t_b, t_c, 1.0, t_a, ALU.add, ALU.mult))

            def split(L, c, n=0):
                need(dve, "hi_ready", L, 3 * n + (c + 1))
                V.tensor_tensor(w_lo[c % RING][:], w_raw[c % RING][:], w_hi[c % RING][:].bitcast(F32),
                                ALU.subtract).then_inc(sem["lo_ready"], 1)

            def add_squares(L, n, sq):
                for i in (1, 2, 3):
                    need(dve, "squares", L, 4 * n + i + 1)
                    step(V.tensor_tensor(sq[:, 0:2, :], sq[:, 0:2, :], sq[:, 2 * i:2 * i + 2, :], ALU.add))
                V.tensor_tensor(sq[:, 0, :], sq[:, 0, :], sq[:, 1, :], ALU.add).then_inc(sem["squares_added"], 1)

            def norm(L, which):
                gains, col = (pf, F_NORM) if which else (pm, M_NORM)
                add_squares(L, which, norm_f)
                need(dve, "std_ready", L, which + 1)
                step(V.reciprocal(sums_r, sums_std))
                for i in range(5):
                    if i < 4:
                        for k in (2 * i, 2 * i + 1):
                            STT(norm_f[:, k, :], x_t[:, k, :], gains[:, col + k:col + k + 1], sums_r,
                                ALU.mult, ALU.mult).then_inc(sem["scaled"], 1)
                    if i:
                        need(dve, "act_hi", L, 4 * which + i)
                        V.tensor_tensor(act_l[:, 2 * i - 2:2 * i, :], norm_f[:, 2 * i - 2:2 * i, :],
                                        act_h[:, 2 * i - 2:2 * i, :].bitcast(F32), ALU.subtract)\
                            .then_inc(sem["act_lo"], 1)

            def evacuate(L, c):
                kind, i = SECTION[c]
                g = GROUP0[c]
                if kind in ("rx", "mqk"):
                    dst, w, n, k0 = (lru_x, M_RW, 4, 0) if kind == "rx" else (mqk, M_CW, 8, 2)
                    ps = main[g % 2][:].rearrange("p (b t) -> p b t", b=2)
                    need(dve, "conv_tap", L, k0 + i + 1)
                    for s in (1, 2, 3):
                        for h in range(2):
                            j = 2 * i + h
                            col = w + (3 - s) * n + j
                            ins = STT(dst[:, j, s:T], ps[:, h, 0:T - s], pm[:, col:col + 1], dst[:, j, s:T],
                                      ALU.mult, ALU.add)
                            if s == 3 and h == 1:
                                ins.then_inc(sem["evac_dve"], 1)
                            else:
                                own(ins)
                        if s < 3:
                            own.settle()
                if kind == "wb":
                    branch = BRANCHES.index(i[0])
                    need(dve, "evac_act", L, evacuations(c, False))
                    for half in range(2):
                        need(dve, "group_done", L, g + half + 1)
                        ps = main[(g + half) % 2][:].rearrange("p (b t) -> p b t", b=2)
                        b = 4 * i[1] + 2 * half
                        dst = merged[:, b:b + 2, :] if branch == 0 else merge_t[half]
                        n = 4 * (branch - 1) + 2 * i[1] + half
                        if n >= 2:
                            need(dve, "wb_sum", L, n - 1)
                        V.tensor_tensor(dst, ps, gate[:, 2 * half:2 * half + 2, :], ALU.mult)\
                            .then_inc(sem["evac_dve"], 1)
                if kind == "wo":
                    need(dve, "group_done", L, g + 1)
                    ps = main[g % 2][:].rearrange("p (b t) -> p b t", b=2)
                    V.tensor_tensor(x_t[:, 2 * i:2 * i + 2, :], x_t[:, 2 * i:2 * i + 2, :], ps, ALU.add)\
                        .then_inc(sem["x_ready"], 1)

            def before(L):
                norm(L, 0)
                split(L, 2)
                need(dve, "small_hi", L, 1)
                V.tensor_tensor(small_l, small_raw, small_h.bitcast(F32), ALU.subtract).then_inc(sem["small_lo"], 1)
                lam = pm[:, M_LAM:M_LAM + NB]
                STT(lt[0], lam, -1.0, lam, ALU.mult, ALU.max).then_inc(sem["lam_abs"], 1)
                step(V.tensor_scalar(lt[4], lam, 0.0, None, ALU.min))
                need(dve, "lam_exp", L, 1)
                log1p_half(lt[1], lt[0], lt[2], lt[3])
                step(STT(lt[0], lt[2], -2.0, lt[4], ALU.mult, ALU.add))
                own(V.tensor_scalar(lam8[:, 0, :], lt[0], 8.0, None, ALU.mult))
                own.settle()
                V.tensor_scalar(lam8[:, 1, :], lt[0], -8.0, None, ALU.mult).then_inc(sem["lam_ready"], 1)

            def rope(L, i):
                dst = (qi, q_c, k_c)[i // 2][:, 2 * (i % 2):2 * (i % 2) + 2, :]
                k = 1 if i == 0 else i + 2
                need(dve, "rope_turned", L, k)
                own(V.tensor_tensor(rope_sin[i % 2], psum[6 + i % 2][:].rearrange("p (b t) -> p b t", b=2),
                                    sin_t[:].unsqueeze(1).to_broadcast([P, 2, T]), ALU.mult))
                own.settle()
                need(dve, "rope_cos", L, i + 1)
                V.tensor_tensor(dst, dst, rope_sin[i % 2], ALU.add).then_inc(sem["rope_done"], 1)

            def rope_key(L):
                need(dve, "rope_turned", L, 2)
                up = slice(64, 128)
                own(V.tensor_tensor(ki_sin[up, :], psum[7][up, 0:T], sin_t[up, :], ALU.mult))
                own(V.tensor_tensor(ki[up, :], rope_ki[up, :], cos_t[up, :], ALU.mult))
                own.settle()
                step(V.tensor_tensor(ki[up, :], ki[up, :], ki_sin[up, :], ALU.add))
                V.tensor_copy(ki[0:64, :], ki[up, :]).then_inc(sem["rope_done"], 1)

            def gate_rows(L, part):
                if part == 0:
                    need(dve, "rows_ready", L, 1)
                    step(V.tensor_copy(f_row, f_in[32:36, :]))
                    STT(t0, f_row, -1.0, f_row, ALU.mult, ALU.max).then_inc(sem["f_abs"], 1)
                    step(V.tensor_scalar(f_row, f_row, 0.0, None, ALU.min))
                if part == 1:
                    need(dve, "f_exp", L, 1)
                    log1p_half(t1, t0, t2, t3)
                    step(STT(t0, t2, -2.0, f_row, ALU.mult, ALU.add))
                    step(V.tensor_tensor_scan(g_row, ones[0:4, :], t0, 0.0, ALU.mult, ALU.add))
                    V.tensor_tensor(iw[0:4, :], iw[0:4, :], g_row, ALU.subtract).then_inc(sem["a_row"], 1)
                    need(dve, "a_row", L, 1)
                    step(V.tensor_tensor_scan(m_row, iw[0:4, :], iw[0:4, :], 0.0, ALU.max, ALU.max))
                    V.tensor_tensor(em_r, g_row, m_row, ALU.add).then_inc(sem["m_row"], 1)
                if part == 2:
                    need(dve, "aw_turned", L, 1)
                    ps = psum[5][:, 256:280].rearrange("p (s j) -> p s j", s=2)
                    own(V.tensor_copy(aw[:, :, 0:4], ps[:, :, 0:4]))
                    V.tensor_scalar(aw[:, :, 4:12], ps[:, :, 4:12], 8.0 ** -0.5 * 64.0 ** -0.5, None, ALU.mult)\
                        .then_inc(sem["aw_ready"], 1)

            def index_unit(L, u):
                if u == 0:
                    need(dve, "aw_ready", L, 1)
                tile = 1 if u < 2 else 0
                width = T if tile else P
                vis = cst[:, K_VIS:K_VIS + T] if tile else cst[:, K_VIS + P:K_VIS + T]
                for i in (2 * u, 2 * u + 1):
                    need(dve, "idx_relu", L, i + 1)
                    heads = 2 if tile else 4
                    r = relu[i % 2].rearrange("p b t -> p (b t)").rearrange("p (h s) -> p h s", h=heads)
                    for j in range(heads):
                        h = (4 * u if tile else 0) + i % 2 + 2 * j
                        first = h == 0
                        ins = STT(score[:, 0:width], r[:, j, :], aw[:, tile, 4 + h:5 + h],
                                  vis if first else score[:, 0:width], ALU.mult, ALU.add)
                        if j < heads - 1:
                            step(ins)
                        else:
                            ins.then_inc(sem["idx_used"], 1)
                            need(dve, "idx_used", L, i + 1)

            def select(L, tile, part):
                width = T if tile else P
                a, b = score[:, 0:width], score_work[:, 0:width]
                for r in range(part * TOPK // 16, (part + 1) * TOPK // 16):
                    src = a if r == 0 else b
                    own(V.memset(spare, 0.0))
                    step(V.max(top8, src))
                    own(V.memset(spare, 0.0))
                    step(V.match_replace(b, top8, src, GONE))
                if part == 0:
                    return
                step(V.tensor_scalar(b, b, GONE, 1.0, ALU.is_equal, ALU.subtract))
                vis = cst[:, K_VIS:K_VIS + T] if tile else cst[:, K_VIS + P:K_VIS + T]
                STT(mask[tile][:, 0:width], b, BIG, vis, ALU.mult, ALU.add).then_inc(sem["mask_ready"], 1)

            def logits(L, u):
                tile = 1 if u < 2 else 0
                need(dve, "mask_ready", L, 1 if tile else 2)
                for i in range(2):
                    need(dve, "att_done", L, 2 * u + i + 1)
                    if u == 2 and i == 0:
                        need(dve, "turned", L, 4)
                    if tile:
                        ps = psum[2 + i][:].rearrange("p (h s) -> p h s", h=2)
                        dst = prob[:, 4 * u + i:4 * u + 4:2, :]
                        m = mask[1].unsqueeze(1).to_broadcast([P, 2, T])
                    else:
                        ps = psum[2 + i][:].rearrange("p (h s) -> p h s", h=4)
                        dst = prob[:, i:HEADS_A:2, 0:P]
                        m = mask[0].unsqueeze(1).to_broadcast([P, 4, P])
                    STT(dst, ps, 64.0 ** -0.5, m, ALU.mult, ALU.add).then_inc(sem["logits_ready"], 1)

            def row_max(L, n):
                width = T if n == 0 else P
                need(dve, "logits_ready", L, 4 + 2 * n)
                step(V.reduce_max(a_max, prob[:, :, 0:width], AX_X))
                V.tensor_scalar(a_neg, a_max, -1.0, None, ALU.mult).then_inc(sem["max_ready"], 1)

            def normalise(L, n):
                width = T if n == 0 else P
                need(dve, "prob_exp", L, n + 1)
                step(V.reciprocal(a_max, a_sum))
                V.tensor_tensor(prob[:, :, 0:width], prob[:, :, 0:width],
                                a_max.unsqueeze(2).to_broadcast([P, HEADS_A, width]), ALU.mult)\
                    .then_inc(sem["prob_ready"], 1)

            def pv_out(L, n):
                need(dve, "pv_done", L, n + 1)
                tile = 1 - n
                ins = V.tensor_copy(y_attn[:, :, tile * P:tile * P + P],
                                    psum[2][:].rearrange("p (b t) -> p b t", b=NB))
                ins.then_inc(sem["pv_out" if n == 0 else "yc_ready"], 1)

            def mlstm(L, stage, h):
                if stage == 1:
                    need(dve, "ml_rows", L, h + 1)
                    if h:
                        need(dve, "ml_weight", L, h)
                    mk = cst[:, K_CAUS:K_CAUS + T]
                    own(STT(e_m[:, 0:T], psum[6][:, 0:T], aw[:, 0, h:h + 1], mk, ALU.subtract, ALU.max))
                    STT(e_m[:, T:T + P], psum[6][:, P:T], aw[:, 1, h:h + 1], mk[:, 0:P], ALU.subtract, ALU.max)\
                        .then_inc(sem["ml_sub"], 1)
                    need(dve, "ml_exp", L, h + 1)
                    if h:
                        need(dve, "ml_num", L, h)
                    STT(w_m, psum[7][:, 0:384], float(P) ** -0.5, e_m, ALU.mult, ALU.mult)\
                        .then_inc(sem["ml_weight"], 1)
                if stage == 2:
                    need(dve, "ml_num", L, h + 1)
                    need(dve, "ml_emb", L, h + 1)
                    step(STT(den_b, psum[4][:, 256:512], -1.0, em_b, ALU.mult, ALU.max))
                    step(V.tensor_tensor(den_b, psum[4][:, 256:512], den_b, ALU.max))
                    step(V.reciprocal(den_b, den_b))
                    V.tensor_tensor(h_m, psum[4][:, 0:256], den_b, ALU.mult).then_inc(sem["ml_h"], 1)
                if stage == 3:
                    need(dve, "ml_mean", L, h + 1)
                    STT(c_m, psum[5][:, 0:256], -1.0 / P, h_m, ALU.mult, ALU.add).then_inc(sem["ml_cent"], 1)
                if stage == 4:
                    need(dve, "ml_std", L, h + 1)
                    step(V.reciprocal(s_m, std_m))
                    step(STT(c_m, c_m, pm[:, M_G + h:M_G + h + 1], s_m, ALU.mult, ALU.mult))
                    V.tensor_tensor(std_m, c_m, mo[:, h, :], ALU.mult).then_inc(sem["y_ready"], 1)
                    need(dve, "y_hi", L, 2 + h)
                    V.tensor_tensor(y_l[1][:, h, :], std_m, y_h[1][:, h, :].bitcast(F32), ALU.subtract)\
                        .then_inc(sem["y_lo"], 1)

            def side(L, c):
                if c == 3:
                    need(dve, "lru_i", L, 1)
                    V.tensor_tensor(lru_i, lru_i, lru_x, ALU.mult).then_inc(sem["lru_in"], 1)
                if c == 4:
                    gate_rows(L, 0)
                    need(dve, "lru_a", L, 1)
                    need(dve, "lru_in", L, 1)
                    step(V.tensor_tensor(lru_x, lru_r, lru_r, ALU.mult))
                    STT(lru_t, lru_x, 1.0, lru_t, ALU.add, ALU.mult).then_inc(sem["lru_ratio"], 1)
                if c == 5:
                    rope(L, 0)
                    rope_key(L)
                    need(dve, "lru_root", L, 1)
                    step(V.tensor_tensor(lru_i, lru_i, lru_t, ALU.mult))
                    for b in range(NB):
                        own(V.tensor_tensor_scan(lru_x[:, b, :], lru_r[:, b, :], lru_i[:, b, :], 0.0,
                                                 ALU.mult, ALU.add))
                    own.settle()
                    V.tensor_tensor(lru_x, lru_x, lru_g, ALU.mult).then_inc(sem["y_ready"], 1)
                if c == 6:
                    rope(L, 1)
                    gate_rows(L, 1)
                if c == 7:
                    rope(L, 2)
                    need(dve, "y_hi", L, 1)
                    V.tensor_tensor(y_l[0][:], lru_x, y_h[0][:].bitcast(F32), ALU.subtract)\
                        .then_inc(sem["y_lo"], 1)
                if c == 8:
                    rope(L, 3)
                    gate_rows(L, 2)
                if c == 9:
                    rope(L, 4)
                if c == 10:
                    rope(L, 5)
                if c in (10, 11):
                    select(L, 1, c - 10)
                if c in (8, 9, 10):
                    index_unit(L, c - 8)
                if c == 12:
                    logits(L, 0)
                if c == 13:
                    logits(L, 1)
                    row_max(L, 0)
                if c == 14:
                    normalise(L, 0)
                if c in (15, 16):
                    select(L, 0, c - 15)
                if c == 17:
                    pv_out(L, 0)
                if c == 18:
                    logits(L, 2)
                    row_max(L, 1)
                if c == 19:
                    normalise(L, 1)
                if c == 21:
                    pv_out(L, 1)
                for s in (3, 2, 1, 0):
                    h = c - 20 - s
                    if 0 <= h < 4:
                        mlstm(L, s + 1, h)
                if c == 28:
                    need(dve, "y_hi", L, 6)
                    V.tensor_tensor(y_l[0][:], y_attn, y_h[0][:].bitcast(F32), ALU.subtract)\
                        .then_inc(sem["y_lo"], 1)
                if c in (MERGE - 1, MERGE):
                    for i in ((0, 1) if c < MERGE else (2, 3)):
                        need(dve, "merged_hi", L, i + 1)
                        V.tensor_tensor(act_l[:, 2 * i:2 * i + 2, :], merged[:, 2 * i:2 * i + 2, :],
                                        act_h[:, 2 * i:2 * i + 2, :].bitcast(F32), ALU.subtract)\
                            .then_inc(sem["merged_lo"], 1)

            def ffn_conv(L, n):
                need(dve, "ff_tap", L, n + 1)
                for s in (1, 2):
                    for h in range(2):
                        ins = STT(ff_c[:, h, s:T], main[0][:, 256 * h:256 * h + T - s],
                                  pf[:, bass.ds(F_CW + (2 - s) * 24 + 2 * n + h, 1)], ff_c[:, h, s:T],
                                  ALU.mult, ALU.add)
                        if s == 2 and h == 1:
                            ins.then_inc(sem["ff_conv"], 1)
                        else:
                            own(ins)
                    if s == 1:
                        own.settle()

            def ffn_product(L, n):
                need(dve, "ff_gelu", L, n + 1)
                need(dve, "group_done", L, ff_group(n, 1))
                if not (isinstance(n, int) and n == 0):
                    need(dve, "ff_lo", L, n)
                V.tensor_tensor(hid_f, ff_g, main[1][:].rearrange("p (b t) -> p b t", b=2), ALU.mult)\
                    .then_inc(sem["ff_prod"], 1)

            def ffn_hidden(L, n):
                need(dve, "ff_hi", L, n + 1)
                V.tensor_tensor(hid_l[:, 0:2, :], hid_f, hid_h[:, 0:2, :].bitcast(F32), ALU.subtract)\
                    .then_inc(sem["ff_lo"], 1)

            def layer(L):
                before(L)
                for c in range(MIX):
                    evacuate(L, c)
                    if c == MERGE:
                        side(L, c)
                        split(L, c + RING)
                    elif c < MIX - 1:
                        split(L, c + RING)
                        side(L, c)
                norm(L, 1)
                split(L, MIX + 2)
                ffn_conv(L, 0)
                split(L, MIX + 3)
                ffn_product(L, 0)
                ffn_hidden(L, 0)
                split(L, MIX + 4)
                own_each = 3
                with dve.Fori(1, N_FF) as n:
                    own.enter(n - 1, own_each)
                    ffn_conv(L, n)
                    split(L, MIX + 2, n)
                    ffn_product(L, n)
                    split(L, MIX + 3, n)
                    ffn_hidden(L, n)
                    split(L, MIX + 4, n)
                own.leave(N_FF - 1, own_each)
                need(dve, "group_done", L, ff_group(N_FF - 1, 2))
                for i in range(4):
                    V.tensor_tensor(x_t[:, 2 * i:2 * i + 2, :], x_t[:, 2 * i:2 * i + 2, :],
                                    psum[2 + i][:].rearrange("p (b t) -> p b t", b=2), ALU.add)\
                        .then_inc(sem["x_ready"], 1)

            pos = work[:, 0:T].bitcast(I32)
            ang, turns, tmp = work[:, T:2 * T], work[:, 2 * T:3 * T], work[:, 3 * T:4 * T]
            dve.wait_ge(sem["pos_loaded"], 16)
            dve.wait_ge(sem["const_loaded"], 16)
            step(V.tensor_copy(tmp, pos))
            step(V.tensor_scalar(ang, tmp, cst[:, K_INV:K_INV + 1], None, ALU.mult))
            part_1 = 6.28125
            part_2 = round((2 * math.pi - part_1) * 2 ** 21) / 2 ** 21
            part_3 = 2 * math.pi - part_1 - part_2
            pi_below = 3.1415925
            for table, quarter in ((sin_t, 0.0), (cos_t, 0.25)):
                step(V.tensor_scalar(turns, ang, 1.0 / (2 * math.pi), quarter, ALU.mult, ALU.add))
                step(V.tensor_scalar(turns, turns, 12582912.0, None, ALU.add))
                step(V.tensor_scalar(turns, turns, -12582912.0, None, ALU.add))
                step(STT(tmp, turns, -part_1, ang, ALU.mult, ALU.add))
                step(STT(tmp, turns, -part_2, tmp, ALU.mult, ALU.add))
                step(STT(tmp, turns, -part_3, tmp, ALU.mult, ALU.add))
                step(V.tensor_scalar(tmp, tmp, quarter * 2 * math.pi, -pi_below, ALU.add, ALU.max))
                V.tensor_scalar(table[:], tmp, pi_below, None, ALU.min).then_inc(sem["setup_dve"], 1)
                dve.wait_ge(sem["setup_dve"], 1 if quarter == 0.0 else 2)
            dve.wait_ge(sem["zeros_ready"], 1)
            split(0, 0)
            split(0, 1)
            with dve.Fori(0, DEPTH) as L:
                own.enter(L, COUNT["own_dve"])
                need(dve, "params", L, 1)
                layer(L)
            own.leave(DEPTH, COUNT["own_dve"])

            def split_2(c, e=0):
                need(dve, "hi_ready", DEPTH, 6 * e + (c + 1))
                V.tensor_tensor(w_lo[c % RING][:], w_raw[c % RING][:], w_hi[c % RING][:].bitcast(F32),
                                ALU.subtract).then_inc(sem["lo_ready"], 1)

            def scale_2(n, src, gain, std, r, dst, width, lower=False):
                add_squares(DEPTH, n, norm_f2[:, :, 0:width])
                need(dve, "std_ready", DEPTH, n + 1)
                step(V.reciprocal(r, std))
                for i in range(5):
                    if i < 4:
                        for k in (2 * i, 2 * i + 1):
                            STT(dst(k), src(k), p2[:, gain + k:gain + k + 1], r, ALU.mult, ALU.mult)\
                                .then_inc(sem["scaled"], 1)
                    if i and lower:
                        need(dve, "act_hi", DEPTH, 4 * (n - 1) + i)
                        V.tensor_tensor(act2_l[:, 2 * i - 2:2 * i, 0:width], norm_f2[:, 2 * i - 2:2 * i, 0:width],
                                        act2_h[:, 2 * i - 2:2 * i, 0:width].bitcast(F32), ALU.subtract)\
                            .then_inc(sem["act_lo"], 1)

            def evacuate_2(c):
                kind, i = SECTION_2[c]
                if kind in ("x", "B", "C"):
                    dst, k0 = {"x": (xs, 0), "B": (b_s, 8), "C": (c_s, 12)}[kind]
                    for half in range(2):
                        dve.wait_ge(sem["tap_2"], 2 * c + half + 1)
                        j = 2 * i + half
                        for s in (1, 2, 3):
                            col = Q_CW + (3 - s) * 16 + k0 + j
                            ins = STT(dst[:, j, s:TM], psum[(2 * c + half) % 4][:, 0:TM - s], p2[:, col:col + 1],
                                      dst[:, j, s:TM], ALU.mult, ALU.add)
                            if s < 3:
                                step(ins)
                            else:
                                ins.then_inc(sem["ev_dve_2"], 1)
                elif kind == "h":
                    for half in range(2):
                        g, j = 2 * c + half, 2 * i + half
                        need(dve, "group_done", DEPTH, g + 1)
                        dve.wait_ge(sem["ev_act_2"], 8 + j + 1)
                        V.tensor_tensor(ch[:, j, :], ch[:, j, :], psum[g % 4][:, 0:TM], ALU.mult)\
                            .then_inc(sem["ev_dve_2"], 1)
                elif kind == "b":
                    for half in range(2):
                        g, j = 2 * c + half, 2 * i + half
                        need(dve, "group_done", DEPTH, g + 1)
                        dve.wait_ge(sem["sc_conv"], j + 1)
                        ins = V.tensor_tensor(v_sc[:, j, :], v_sc[:, j, :], psum[g % 4][:, 0:T], ALU.mult)
                        ins.then_inc(sem["ev_dve_2"], 1)

            def ssd_head(h, part):
                e, w = decay[h % 2], weight[h % 2]
                if part == 0:
                    dve.wait_ge(sem["decay_rows"], h + 1)
                    if h >= 2:
                        dve.wait_ge(sem["decay_weight"], h - 1)
                    for s, (t0_, col, n) in enumerate(SPAN):
                        ins = STT(e[:, col:col + n], psum[4 + h % 2][:, t0_:T], cols2[:, s, h:h + 1],
                                  mask2[:, col:col + n], ALU.subtract, ALU.min)
                        if s < 2:
                            own(ins)
                        else:
                            ins.then_inc(sem["decay_sub"], 1)
                else:
                    dve.wait_ge(sem["decay_exp"], h + 1)
                    if h >= 2:
                        dve.wait_ge(sem["ssd_y"], h - 1)
                    V.tensor_tensor(w, e, cb[:, h // 4, :], ALU.mult).then_inc(sem["decay_weight"], 1)

            def ssd_group(g, part):
                if part == 0:
                    dve.wait_ge(sem["ssd_y"], 4 * g + 4)
                    if g:
                        dve.wait_ge(sem["y2_lo"], g)
                    for b in range(2):
                        own(STT(gy[:, b, :], xs[:, 2 * g + b, META:TM], p2[:, Q_D + 2 * g + b:Q_D + 2 * g + b + 1],
                                psum[6 + g % 2][:, b * T:b * T + T], ALU.mult, ALU.add))
                    own.settle()
                    dve.wait_ge(sem["ev_act_2"], min(8, 2 * g + 2))
                    V.tensor_tensor(gy, gy, zs[:, 2 * g:2 * g + 2, :], ALU.mult).then_inc(sem["ssd_gated"], 1)
                else:
                    dve.wait_ge(sem["ssd_std"], g + 1)
                    step(V.reciprocal(g_std, g_std))
                    for b in range(2):
                        ins = STT(gy[:, b, :], gy[:, b, :], p2[:, Q_G + 2 * g + b:Q_G + 2 * g + b + 1], g_std,
                                  ALU.mult, ALU.mult)
                        if b == 0:
                            own(ins)
                        else:
                            ins.then_inc(sem["ssd_norm"], 1)
                    dve.wait_ge(sem["y2_hi"], g + 1)
                    V.tensor_tensor(y2_l[:, 2 * g:2 * g + 2, :], gy, y2_h[:, 2 * g:2 * g + 2, :].bitcast(F32),
                                    ALU.subtract).then_inc(sem["y2_lo"], 1)

            def side_2(c):
                if c == 1:
                    dve.wait_ge(sem["dt_raw"], 1)
                    STT(rows2[1], rows2[0], -1.0, rows2[0], ALU.mult, ALU.max).then_inc(sem["dt_abs"], 1)
                    step(V.tensor_scalar(rows2[0], rows2[0], 0.0, None, ALU.max))
                    dve.wait_ge(sem["dt_exp"], 1)
                    log1p_half(rows2[2], rows2[1], rows2[3], rows2[4])
                    step(STT(rows2[0], rows2[3], 2.0, rows2[0], ALU.mult, ALU.add))
                    step(V.tensor_scalar(rows2[1], rows2[0], a_col[0:HEADS_S, :], -1.0, ALU.mult, ALU.mult))
                    own(V.memset(rows2[3], 1.0))
                    step(V.memset(cols2, 0.0))
                    V.tensor_tensor_scan(decay_row, rows2[3], rows2[1], 0.0, ALU.mult, ALU.add)\
                        .then_inc(sem["dt_done"], 1)
                if c == 4:
                    for s, n in enumerate((P, P, META)):
                        dve.wait_ge(sem["state_turned"], 1)
                        ps = psum[5][0:n, 32 * s:32 * s + 32]
                        ins = V.tensor_copy(cols2[0:n, s, :], ps)
                        if s < 2:
                            own(ins)
                        else:
                            ins.then_inc(sem["state_cols"], 1)
                    own(V.memset(cb[:, :, S_COLS - META:], 0.0))
                if c in (5, 6, 7):
                    s = c - 5
                    n = (P, P, META)[s]
                    for half in range(2):
                        dve.wait_ge(sem["x_turned"], 2 * s + half + 1)
                        if s == 0 and half == 0:
                            dve.wait_ge(sem["state_cols"], 1)
                        dt = cols2[0:n, s, HEADS_S + 8 * half:HEADS_S + 8 * half + 8]
                        V.tensor_tensor(xdt[0:n, s, 512 * half:512 * half + 512].rearrange("p (h d) -> p h d", h=8),
                                        psum[6 + half][0:n, :].rearrange("p (h d) -> p h d", h=8),
                                        dt.unsqueeze(2).to_broadcast([n, 8, 64]), ALU.mult)\
                            .then_inc(sem["x_scaled"], 1)
                if 10 <= c <= 17:
                    h = 2 * (c - 10)
                    if c == 10:
                        dve.wait_ge(sem["cb_ready"], 8)
                        own.settle()
                    ssd_head(h, 0)
                    ssd_head(h + 1, 0)
                    ssd_head(h, 1)
                    ssd_head(h + 1, 1)
                if 12 <= c <= 19:
                    ssd_group((c - 12) // 2, c % 2)
                if 17 <= c <= 20:
                    i = c - 17
                    dve.wait_ge(sem["sc_tap"], 2 * i + 2)
                    for s in (1, 2):
                        for j in (2 * i, 2 * i + 1):
                            col = Q_SW + (2 - s) * 8 + j
                            ins = STT(v_sc[:, j, :], ch[:, j, META - s:TM - s], p2[:, col:col + 1], v_sc[:, j, :],
                                      ALU.mult, ALU.add)
                            if s == 1:
                                own(ins)
                            else:
                                ins.then_inc(sem["sc_conv"], 1)
                        if s == 1:
                            own.settle()
                if 21 <= c <= 24:
                    i = c - 21
                    dve.wait_ge(sem["sc_std"], i + 1)
                    step(V.reciprocal(sc_s, sc_s))
                    for b in range(2):
                        j = 2 * i + b
                        ins = STT(v_sc[:, j, :], v_sc[:, j, :], p2[:, Q_SG + j:Q_SG + j + 1], sc_s[:, b, :],
                                  ALU.mult, ALU.mult)
                        if b == 0:
                            own(ins)
                        else:
                            ins.then_inc(sem["sc_norm"], 1)
                    dve.wait_ge(sem["y2_hi"], 4 + i + 1)
                    V.tensor_tensor(y2_l[:, 8 + 2 * i:10 + 2 * i, :], v_sc[:, 2 * i:2 * i + 2, :],
                                    y2_h[:, 8 + 2 * i:10 + 2 * i, :].bitcast(F32), ALU.subtract)\
                        .then_inc(sem["y2_lo"], 1)

            def add_out(pair):
                for half in range(2):
                    m = 2 * pair + half
                    need(dve, "group_done", DEPTH, 2 * (IN_2 + 2 * pair + 1) + half + 1)
                    V.tensor_tensor(hx[:, m, META:TM], hx[:, m, META:TM], psum[(2 * pair + half) % 4][:, 0:T],
                                    ALU.add).then_inc(sem["x2_ready"], 1)

            def first_hit(x, m, hit, left):
                step(V.tensor_tensor(hit, x, m.unsqueeze(2).to_broadcast([P, 2, 4]), ALU.is_equal))
                for j in (1, 2, 3):
                    if j == 1:
                        step(V.tensor_scalar(left, hit[:, :, 0], -1.0, 1.0, ALU.mult, ALU.add))
                    else:
                        step(V.tensor_tensor(left, left, hit[:, :, j - 1], ALU.subtract))
                    step(V.tensor_tensor(hit[:, :, j], hit[:, :, j], left, ALU.mult))

            def bc4(col):
                return col.unsqueeze(2).to_broadcast([P, 2, 4])

            def router():
                dve.wait_ge(sem["router_turned"], 1)
                step(V.tensor_copy(rt, psum[7][:, 0:40].rearrange("p (s j) -> p s j", s=2)))
                g = rt[:, :, 0:4]
                e = rt[:, :, 4:20].rearrange("p s (g j) -> p s g j", g=4)
                step(V.reduce_max(rcol[0], g, AX_X))
                V.tensor_tensor(route[0], g, bc4(rcol[0]), ALU.subtract).then_inc(sem["router_max"], 1)
                first_hit(g, rcol[0], route[1], rcol[1])
                step(V.tensor_tensor(route[2], e[:, :, 0, :], bc4(route[1][:, :, 0]), ALU.mult))
                for k in (1, 2, 3):
                    step(V.tensor_tensor(route[3], e[:, :, k, :], bc4(route[1][:, :, k]), ALU.mult))
                    step(V.tensor_tensor(route[2], route[2], route[3], ALU.add))
                step(V.reduce_max(rcol[2], route[2], AX_X))
                first_hit(route[2], rcol[2], route[4], rcol[1])
                step(STT(route[3], route[4], -BIG, route[2], ALU.mult, ALU.add))
                step(V.reduce_max(rcol[3], route[3], AX_X))
                V.tensor_tensor(rcol[4], rcol[3], rcol[2], ALU.subtract).then_inc(sem["pair_max"], 1)
                first_hit(route[3], rcol[3], route[5], rcol[1])
                dve.wait_ge(sem["router_exp"], 1)
                step(V.reduce_sum(rcol[5], route[0], AX_X))
                dve.wait_ge(sem["pair_exp"], 1)
                step(V.tensor_scalar(rcol[6], rcol[4], 1.0, None, ALU.add))
                step(V.tensor_tensor(rcol[6], rcol[6], rcol[5], ALU.mult))
                step(V.reciprocal(rcol[6], rcol[6]))
                step(V.tensor_tensor(rcol[7], rcol[6], rcol[4], ALU.mult))
                step(V.tensor_tensor(route[4], route[4], bc4(rcol[6]), ALU.mult))
                step(V.tensor_tensor(route[5], route[5], bc4(rcol[7]), ALU.mult))
                step(V.tensor_tensor(route[4], route[4], route[5], ALU.add))
                c4 = comb_t.rearrange("p s (g j) -> p s g j", g=4)
                for k in range(4):
                    ins = V.tensor_tensor(c4[:, :, k, :], route[4], bc4(route[1][:, :, k]), ALU.mult)
                    if k < 3:
                        own(ins)
                    else:
                        ins.then_inc(sem["combine_ready"], 1)
                dve.wait_ge(sem["combine_turned"], 1)
                V.tensor_copy(comb_row, psum[6][0:N_EXP, 0:T]).then_inc(sem["combine_rows"], 1)

            def moe_product(e, half):
                n = 2 * e + half
                dve.wait_ge(sem["moe_silu"], n + 1)
                V.tensor_tensor(m_sg, m_sg, combine[:, bass.ds(e, 1), :].to_broadcast([P, 2, T]),
                                ALU.mult).then_inc(sem["moe_scaled"], 1)
                dve.wait_ge(sem["moe_scaled"], n + 1)
                need(dve, "group_done", DEPTH, moe_group(n, 1))
                if not (isinstance(n, int) and n == 0):
                    dve.wait_ge(sem["moe_lo"], n)
                V.tensor_tensor(m_hf, m_sg, main[1][:].rearrange("p (b t) -> p b t", b=2), ALU.mult)\
                    .then_inc(sem["moe_prod"], 1)

            def moe_hidden(n):
                dve.wait_ge(sem["moe_hi"], n + 1)
                V.tensor_tensor(y2_l[:, 0:2, :], m_hf, y2_h[:, 0:2, :].bitcast(F32), ALU.subtract)\
                    .then_inc(sem["moe_lo"], 1)

            dve.wait_ge(sem["par_2"], 96)
            scale_2(0, lambda k: x_t[:, k, :], Q_NFIN, norm2_std[:, 0:T], norm2_r[:, 0:T],
                    lambda k: hx[:, k, META:TM], T)
            split_2(2)
            scale_2(1, lambda k: hx[:, k, :], Q_NMIX, norm2_std, norm2_r, lambda k: norm_f2[:, k, :], TM, True)
            for c in range(MIX_2):
                if c < IN_2:
                    evacuate_2(c)
                elif (c - IN_2) % 2:
                    add_out((c - IN_2) // 2)
                if c < MIX_2 - 1:
                    split_2(c + RING)
                side_2(c)
            scale_2(2, lambda k: hx[:, k, META:TM], Q_NFF, norm2_std[:, 0:T], norm2_r[:, 0:T],
                    lambda k: norm_f2[:, k, 0:T], T, True)
            split_2(MIX_2 + 2)
            router()
            split_2(MIX_2 + 3)
            dve.wait_ge(sem["combine_all"], 8)
            moe_product(0, 0)
            moe_hidden(0)
            split_2(MIX_2 + 4)

            def half_expert(e, half):
                split_2(MIX_2 + 3 * half + 2, e)
                split_2(MIX_2 + 3 * half + 3, e)
                moe_product(e, half)
                moe_hidden(2 * e + half)
                split_2(MIX_2 + 3 * half + 4, e)

            half_expert(0, 1)
            with dve.Fori(1, N_EXP - 1) as e:
                half_expert(e, 0)
                half_expert(e, 1)
            half_expert(N_EXP - 1, 0)
            split_2(CHUNKS_2 - 1)
            moe_product(N_EXP - 1, 1)
            moe_hidden(2 * N_EXP - 1)
            need(dve, "group_done", DEPTH, moe_group(2 * N_EXP - 1, 2))
            for i in range(4):
                V.tensor_tensor(hx[:, 2 * i:2 * i + 2, META:TM], hx[:, 2 * i:2 * i + 2, META:TM],
                                psum[2 + i][:].rearrange("p (b t) -> p b t", b=2), ALU.add)\
                    .then_inc(sem["x2_ready"], 1)
            scale_2(3, lambda k: hx[:, k, META:TM], Q_NOUT, fin_std, fin_r, lambda k: norm_f2[:, k, 0:T], T)

        @block.tensor
        def _(pe):
            mm = nc.tensor.matmul

            def product(out, a_hi, a_lo, b_hi, b_lo, first, last):
                mm(out, a_hi, b_hi, start=first, stop=False, skip_group_check=True)
                mm(out, a_hi, b_lo, start=False, stop=False, skip_group_check=True)
                return mm(out, a_lo, b_hi, start=False, stop=last, skip_group_check=True)

            def bank_free(L, g):
                if g < 2:
                    return
                c = max(i for i in range(MIX) if GROUP0[i] <= g - 2)
                kind = SECTION[c][0]
                if kind == "wo":
                    need(pe, "x_ready", L, SECTION[c][1] + 1)
                else:
                    dve = kind in DVE_EVACUATES
                    need(pe, "evac_dve" if dve else "evac_act", L, evacuations(c, dve) + g - 2 - GROUP0[c] + 1)

            def chunk(L, c):
                kind, i = SECTION[c]
                need(pe, "lo_ready", L, c + 1)
                g = GROUP0[c]
                hi, lo = w_hi[c % RING][:], w_lo[c % RING][:]
                if kind == "wb":
                    slot = {1: 0, 0: 1, 2: 0}[i[0]]
                    need(pe, "y_lo", L, {1: 1, 0: 5, 2: 6}[i[0]])
                    whi, wlo = (w.rearrange("p (t c) -> p t c", t=NB) for w in (hi, lo))
                    for half in range(2):
                        bank_free(L, g + half)
                        for m in range(2):
                            col = (2 * half + m) * P
                            for k in range(NB):
                                ins = product(main[(g + half) % 2][:, m * T:m * T + T],
                                              whi[:, k, col:col + P], wlo[:, k, col:col + P],
                                              y_h[slot][:, k, :], y_l[slot][:, k, :], k == 0, k == NB - 1)
                        ins.then_inc(sem["group_done"], 1)
                    return
                bank_free(L, g)
                whi, wlo = (w.rearrange("p (t c) -> p t c", t=KT) for w in (hi, lo))
                for m in range(2):
                    for k in range(KT):
                        if c == 0 and m == 0 and k % 2 == 0:
                            need(pe, "act_lo", L, k // 2 + 1)
                        if kind == "wo" and i == 0 and m == 0 and k % 2 == 0:
                            need(pe, "merged_lo", L, k // 2 + 1)
                        o = main[g % 2][:, m * T:m * T + T]
                        if kind in ("v", "mv"):
                            ts = slice(m * P, m * P + P)
                            ins = product(o, act_h[:, k, ts], act_l[:, k, ts], whi[:, k, :], wlo[:, k, :],
                                          k == 0, k == KT - 1)
                        else:
                            cs = slice(m * P, m * P + P)
                            ins = product(o, whi[:, k, cs], wlo[:, k, cs], act_h[:, k, :], act_l[:, k, :],
                                          k == 0, k == KT - 1)
                ins.then_inc(sem["group_done"], 1)

            def norm(L, which):
                need(pe, "squares_added", L, which + 1)
                mm(psum[7][:, 0:T], ones[:, 0:P], norm_f[:, 0, :], start=True, stop=True)\
                    .then_inc(sem["sum_done"], 1)

            def turn_pair(L, i):
                need(pe, "evac_act", L, 2 + i + 1)
                if i >= 2:
                    need(pe, "rope_done", L, i if i > 2 else 2)
                for b in range(2):
                    ins = mm(psum[6 + i % 2][:, b * T:b * T + T], rot, rope_in[i % 2][:, b, :],
                             start=True, stop=True)
                ins.then_inc(sem["rope_turned"], 1)

            def mlstm(L, stage, h):
                if stage == 1:
                    if h == 0:
                        need(pe, "em_row", L, 1)
                        need(pe, "aw_ready", L, 1)
                        need(pe, "silu_done", L, 4)
                    else:
                        need(pe, "ml_weight", L, h)
                        need(pe, "ml_emb", L, h)
                    pick = ident[0:4, h:h + 1].to_broadcast([4, P])
                    mm(psum[6][:, 0:T], pick, m_row, start=True, stop=True)
                    mm(psum[6][:, T:2 * T], pick, em_r, start=True, stop=True)
                    mm(psum[7][:, 0:T], mqk[:, 4 + h, 0:P], mqk[:, h, :], start=True, stop=True)
                    mm(psum[7][:, T:T + P], mqk[:, 4 + h, P:T], mqk[:, h, P:T], start=True, stop=True)\
                        .then_inc(sem["ml_rows"], 1)
                if stage == 2:
                    need(pe, "ml_weight", L, h + 1)
                    if h:
                        need(pe, "ml_h", L, h)
                    hs = slice(h * P, h * P + P)
                    mm(psum[4][:, 0:T], mv[:, 0, hs], w_m[:, 0:T], start=True, stop=False, skip_group_check=True)
                    mm(psum[4][:, P:T], mv[:, 1, hs], w_m[:, T:T + P], start=False, stop=True, skip_group_check=True)
                    mm(psum[4][:, T:2 * T], ones[:, 0:P], w_m[:, 0:T], start=True, stop=False,
                       skip_group_check=True)
                    mm(psum[4][:, T + P:2 * T], ones[:, 0:P], w_m[:, T:T + P], start=False, stop=True,
                       skip_group_check=True).then_inc(sem["ml_num"], 1)
                if stage == 3:
                    need(pe, "ml_h", L, h + 1)
                    if h:
                        need(pe, "ml_std", L, h)
                    mm(psum[5][:, 0:T], ones[:, 0:P], h_m, start=True, stop=True).then_inc(sem["ml_mean"], 1)
                if stage == 4:
                    need(pe, "ml_sq", L, h + 1)
                    mm(psum[5][:, T:2 * T], ones[:, 0:P], s_m, start=True, stop=True).then_inc(sem["ml_var"], 1)

            def attention_scores(L, u):
                tile = 1 if u < 2 else 0
                for i in range(2):
                    heads = range(4 * u + i, 4 * u + 4, 2) if tile else range(i, HEADS_A, 2)
                    width = T if tile else P
                    if u == 0 and i == 0:
                        need(pe, "rope_done", L, 7)
                        need(pe, "idx_relu", L, 6)
                    if u == 1:
                        need(pe, "logits_ready", L, i + 1)
                    if u == 2:
                        need(pe, "turned", L, 4)
                        need(pe, "pv_out", L, 1)
                    for j, h in enumerate(heads):
                        r = slice(64 * (h % 2), 64 * (h % 2) + 64)
                        ins = mm(psum[2 + i][:, j * width:j * width + width],
                                 q_c[r, h // 2, tile * P:tile * P + P], k_c[r, h // 2, 0:width],
                                 start=True, stop=True)
                    ins.then_inc(sem["att_done"], 1)

            def index_scores(L, u):
                tile = 1 if u < 2 else 0
                for i in range(2):
                    n = 2 * u + i
                    if n == 0:
                        need(pe, "rope_done", L, 3)
                        need(pe, "lru_i", L, 1)
                    if n >= 2:
                        need(pe, "idx_relu", L, n - 1)
                    width = T if tile else P
                    heads = range(4 * u + i, 4 * u + 4, 2) if tile else range(i, HEADS_A, 2)
                    for j, h in enumerate(heads):
                        r = slice(64 * (h % 2), 64 * (h % 2) + 64)
                        ins = mm(psum[2 + i][:, j * width:j * width + width],
                                 qi[r, h // 2, tile * P:tile * P + P], ki[r, 0:width], start=True, stop=True)
                    ins.then_inc(sem["idx_done"], 1)

            def turn_probs(L, i):
                s, half = (i // 2, i % 2) if i < 4 else (0, i % 2)
                need(pe, "prob_ready", L, 1 if i < 4 else 2)
                if i in (2, 3):
                    need(pe, "turned", L, i - 1)
                for j in range(4):
                    ins = nc.tensor.transpose(psum[2 + i % 2][:, j * P:j * P + P],
                                              prob[:, 4 * half + j, s * P:s * P + P], ident)
                ins.then_inc(sem["turn_done"], 1)

            def values(L, n):
                need(pe, "turned", L, 4 if n == 0 else 6)
                if n == 1:
                    need(pe, "pv_out", L, 1)
                spans = (0, 1) if n == 0 else (0,)
                for h in range(HEADS_A):
                    for s in spans:
                        r = 64 * (h % 2)
                        ins = mm(psum[2][r:r + 64, (h // 2) * P:(h // 2) * P + P],
                                 v_c[:, s, h * 64:h * 64 + 64], prob_t[:, s, h, :],
                                 start=s == spans[0], stop=s == spans[-1], skip_group_check=True)
                ins.then_inc(sem["pv_done"], 1)

            def side(L, c):
                if c == 3:
                    need(pe, "evac_dve", L, 2)
                    need(pe, "par_w", L, 64)
                    for w, bank in ((wa, 4), (wx, 2)):
                        for b in range(NB):
                            ins = mm(psum[bank + b // 2][:, T * (b % 2):T * (b % 2) + T], w[:, b, :], lru_x[:, b, :],
                                     start=True, stop=True)
                        ins.then_inc(sem["lru_gates"], 1)
                    need(pe, "small_lo", L, 1)
                    for k in range(KT):
                        ins = product(psum[6][:, 0:T], small_h[:, k, :], small_l[:, k, :], act_h[:, k, :],
                                      act_l[:, k, :], k == 0, k == KT - 1)
                    ins.then_inc(sem["small_done"], 1)
                if c == 5:
                    need(pe, "rows_ready", L, 1)
                    turn_pair(L, 0)
                    mm(psum[7][64:128, 0:T], rot[64:128, 64:128], rope_ki[64:128, :], start=True, stop=True)\
                        .then_inc(sem["rope_turned"], 1)
                if 6 <= c <= 10:
                    if c == 6:
                        need(pe, "rope_done", L, 2)
                    if c == 8:
                        need(pe, "a_row", L, 1)
                        need(pe, "lru_i", L, 1)
                    turn_pair(L, c - 5)
                if c == 8:
                    for s in range(2):
                        ins = nc.tensor.transpose(psum[5][:, 256 + 12 * s:268 + 12 * s], iw[:, s * P:s * P + P],
                                                  ident[0:12, 0:12])
                    ins.then_inc(sem["aw_turned"], 1)
                if c in (8, 9, 10):
                    index_scores(L, c - 8)
                if c in (12, 13):
                    attention_scores(L, c - 12)
                if c in (15, 16):
                    turn_probs(L, 2 * (c - 15))
                    turn_probs(L, 2 * (c - 15) + 1)
                if c == 17:
                    values(L, 0)
                if c == 18:
                    attention_scores(L, 2)
                if c == 20:
                    turn_probs(L, 4)
                    turn_probs(L, 5)
                if c == 21:
                    values(L, 1)
                for s in (3, 2, 1, 0):
                    h = c - 20 - s
                    if 0 <= h < 4:
                        mlstm(L, s + 1, h)

            def ffn_up_part(L, n, part):
                c = ff_group(n, part) - G_MIX - 1 + MIX
                slot = (MIX + part + (0 if isinstance(n, int) and n == 0 else RING - 1)) % RING
                need(pe, "lo_ready", L, c + 1)
                if isinstance(n, int) and n == 0:
                    need(pe, "x_ready", L, 3 + part)
                elif part == 0:
                    need(pe, "ff_conv", L, n)
                else:
                    need(pe, "ff_prod", L, n)
                whi, wlo = (w[slot][:].rearrange("p (t c) -> p t c", t=KT) for w in (w_hi, w_lo))
                for m in range(2):
                    for k in range(KT):
                        if isinstance(n, int) and n == 0 and part == 0 and m == 0 and k % 2 == 0:
                            need(pe, "act_lo", L, 4 + k // 2 + 1)
                        cs = slice(m * P, m * P + P)
                        ins = product(main[part][:, m * T:m * T + T], whi[:, k, cs], wlo[:, k, cs],
                                      act_h[:, k, :], act_l[:, k, :], k == 0, k == KT - 1)
                ins.then_inc(sem["group_done"], 1)

            def ffn_down_part(L, n, first, last):
                c = ff_group(n, 2) - G_MIX - 1 + MIX
                slot = (MIX + (2 if last else 4)) % RING
                need(pe, "lo_ready", L, c + 1)
                need(pe, "ff_lo", L, n + 1)
                whi, wlo = (w[slot][:].rearrange("p (t c) -> p t c", t=2) for w in (w_hi, w_lo))
                for m in range(KT):
                    for k in range(2):
                        cs = slice(m * P, m * P + P)
                        ins = product(psum[2 + m // 2][:, (m % 2) * T:(m % 2) * T + T], whi[:, k, cs], wlo[:, k, cs],
                                      hid_h[:, k, :], hid_l[:, k, :], first and m % 2 == 0 and k == 0,
                                      last and k == 1)
                ins.then_inc(sem["group_done"], 1)

            def layer(L):
                norm(L, 0)
                for c in range(MIX):
                    chunk(L, c)
                    side(L, c)
                norm(L, 1)
                ffn_up_part(L, 0, 0)
                ffn_up_part(L, 0, 1)
                ffn_up_part(L, 1, 0)
                ffn_up_part(L, 1, 1)
                ffn_down_part(L, 0, True, False)
                with pe.Fori(2, N_FF) as n:
                    ffn_up_part(L, n, 0)
                    ffn_up_part(L, n, 1)
                    ffn_down_part(L, n - 1, False, False)
                ffn_down_part(L, N_FF - 1, False, True)

            pe.wait_ge(sem["const_loaded"], 16)
            pe.wait_ge(sem["zeros_ready"], 1)
            with pe.Fori(0, DEPTH) as L:
                layer(L)

            def sum_squares(n, width):
                need(pe, "squares_added", DEPTH, n + 1)
                mm(psum[7][:, 0:width], ones[:, 0:P], norm_f2[:, 0, 0:width], start=True, stop=True)\
                    .then_inc(sem["sum_done"], 1)

            def bank_free_2(g):
                if g < 4:
                    return
                c = (g - 4) // 2
                dve = SECTION_2[c][0] in DVE_EVACUATES_2
                pe.wait_ge(sem["ev_dve_2" if dve else "ev_act_2"], evacuations_2(c, dve) + (g - 4) % 2 + 1)

            def chunk_2(c):
                need(pe, "lo_ready", DEPTH, c + 1)
                whi, wlo = (w[c % RING][:].rearrange("p (t c) -> p t c", t=KT) for w in (w_hi, w_lo))
                if c < IN_2:
                    ts = slice(META, TM) if SECTION_2[c][0] in ("z", "b") else slice(0, TM)
                    for half in range(2):
                        g = 2 * c + half
                        bank_free_2(g)
                        cs = slice(half * P, half * P + P)
                        for k in range(KT):
                            if g == 0 and k % 2 == 0:
                                need(pe, "act_lo", DEPTH, k // 2 + 1)
                            ins = product(psum[g % 4][:, 0:ts.stop - ts.start], whi[:, k, cs], wlo[:, k, cs],
                                          act2_h[:, k, ts], act2_l[:, k, ts], k == 0, k == KT - 1)
                        ins.then_inc(sem["group_done"], 1)
                    return
                pair, part = (c - IN_2) // 2, (c - IN_2) % 2
                for half in range(2):
                    if part == 0:
                        if pair < 2:
                            bank_free_2(2 * IN_2 + 2 * pair + half)
                        else:
                            pe.wait_ge(sem["x2_ready"], 2 * (pair - 2) + half + 1)
                    pe.wait_ge(sem["y2_lo"], 8 if part else 4)
                    cs = slice(half * P, half * P + P)
                    for k in range(KT):
                        ins = product(psum[(2 * pair + half) % 4][:, 0:T], whi[:, k, cs], wlo[:, k, cs],
                                      y2_h[:, KT * part + k, :], y2_l[:, KT * part + k, :],
                                      part == 0 and k == 0, part == 1 and k == KT - 1)
                    ins.then_inc(sem["group_done"], 1)

            def turn_x(s):
                n = (P, P, META)[s]
                for half in range(2):
                    if s == 0:
                        pe.wait_ge(sem["silu_2"], 4)
                    else:
                        pe.wait_ge(sem["x_scaled"], 2 * (s - 1) + half + 1)
                    for j in range(4):
                        ins = nc.tensor.transpose(psum[6 + half][0:n, j * P:j * P + P],
                                                  xs[:, 4 * half + j, s * P:s * P + n], ident)
                    ins.then_inc(sem["x_turned"], 1)

            def ssd_values(h):
                g, r = h // 4, 64 * (h % 2)
                pe.wait_ge(sem["decay_weight"], h + 1)
                if h % 4 == 0 and g >= 2:
                    pe.wait_ge(sem["ssd_std"], g - 1)
                o = ((h % 4) // 2) * T
                for s, (t_0, col, n) in enumerate(SPAN):
                    rows = (P, P, META)[s]
                    ins = mm(psum[6 + g % 2][r:r + 64, o + t_0:o + T], xdt[0:rows, s, h * 64:h * 64 + 64],
                             weight[h % 2][0:rows, col:col + n], start=s == 0, stop=s == 2, skip_group_check=True)
                ins.then_inc(sem["ssd_y"], 1)

            def side_2(c):
                if c == 1:
                    for k in range(KT):
                        ins = mm(psum[4][0:HEADS_S, 0:TM], dt_w[:, k, :], norm_f2[:, k, :], start=k == 0,
                                 stop=k == KT - 1)
                    ins.then_inc(sem["small_2"], 1)
                if c == 4:
                    pe.wait_ge(sem["dt_done"], 1)
                    for s, n in enumerate((P, P, META)):
                        nc.tensor.transpose(psum[5][0:n, 32 * s:32 * s + 16], decay_row[:, s * P:s * P + n],
                                            ident[0:16, 0:16])
                        ins = nc.tensor.transpose(psum[5][0:n, 32 * s + 16:32 * s + 32],
                                                  rows2[0][:, s * P:s * P + n], ident[0:16, 0:16])
                    ins.then_inc(sem["state_turned"], 1)
                if c in (5, 6, 7):
                    turn_x(c - 5)
                if c == 9:
                    pe.wait_ge(sem["silu_2"], 8)
                    pe.wait_ge(sem["x_scaled"], 6)
                    pe.wait_ge(sem["state_cols"], 1)
                    for g in range(GROUPS_S):
                        bank = psum[(6, 7, 4, 5)[g]]
                        for s, (t_0, col, n) in enumerate(SPAN):
                            rows = (P, P, META)[s]
                            ins = mm(bank[0:rows, col:col + n], b_s[:, g, s * P:s * P + rows],
                                     c_s[:, g, META + t_0:TM], start=True, stop=True)
                        ins.then_inc(sem["cb_done"], 1)
                if 11 <= c <= 18:
                    ssd_values(2 * (c - 11))
                    ssd_values(2 * (c - 11) + 1)
                if 10 <= c <= 17:
                    for h in (2 * (c - 10), 2 * (c - 10) + 1):
                        if c == 10:
                            pe.wait_ge(sem["cb_ready"], 8)
                        else:
                            pe.wait_ge(sem["decay_sub"], h - 1)
                        mm(psum[4 + h % 2][:, 0:T], ident[0:HEADS_S, h:h + 1].to_broadcast([HEADS_S, P]),
                           decay_row[:, META:TM], start=True, stop=True).then_inc(sem["decay_rows"], 1)
                if c in (13, 15, 17, 19):
                    g = (c - 13) // 2
                    pe.wait_ge(sem["ssd_sq"], g + 1)
                    for b in range(2):
                        ins = mm(psum[6 + g % 2][:, 0:T], ones[:, 0:P], gsq[:, b, :], start=b == 0, stop=b == 1)
                    ins.then_inc(sem["ssd_sum"], 1)
                if 21 <= c <= 24:
                    i = c - 21
                    pe.wait_ge(sem["sc_sq"], i + 1)
                    for b in range(2):
                        ins = mm(psum[4 + i % 2][:, b * T:b * T + T], cst[:, K_ONE64:K_ONE64 + P], sc_s[:, b, :],
                                 start=True, stop=True)
                    ins.then_inc(sem["sc_sum"], 1)

            def moe_up_part(n, part):
                c = moe_group(n, part) - 2 * MIX_2 - 1 + MIX_2
                slot = (MIX_2 + (part if isinstance(n, int) and n == 0 else part + 2)) % RING
                need(pe, "lo_ready", DEPTH, c + 1)
                if isinstance(n, int) and n == 0:
                    if part == 0:
                        pe.wait_ge(sem["x2_ready"], 8)
                elif part == 0:
                    pe.wait_ge(sem["moe_silu"], n)
                else:
                    pe.wait_ge(sem["moe_prod"], n)
                whi, wlo = (w[slot][:].rearrange("p (t c) -> p t c", t=KT) for w in (w_hi, w_lo))
                for m in range(2):
                    for k in range(KT):
                        if isinstance(n, int) and n == 0 and part == 0 and m == 0 and k % 2 == 0:
                            need(pe, "act_lo", DEPTH, 4 + k // 2 + 1)
                        cs = slice(m * P, m * P + P)
                        ins = product(main[part][:, m * T:m * T + T], whi[:, k, cs], wlo[:, k, cs],
                                      act2_h[:, k, 0:T], act2_l[:, k, 0:T], k == 0, k == KT - 1)
                ins.then_inc(sem["group_done"], 1)

            def moe_down_part(n, first, last):
                c = moe_group(n, 2) - 2 * MIX_2 - 1 + MIX_2
                slot = (MIX_2 + (2 if last else 4)) % RING
                need(pe, "lo_ready", DEPTH, c + 1)
                pe.wait_ge(sem["moe_lo"], n + 1)
                whi, wlo = (w[slot][:].rearrange("p (t c) -> p t c", t=2) for w in (w_hi, w_lo))
                for m in range(KT):
                    for k in range(2):
                        cs = slice(m * P, m * P + P)
                        ins = product(psum[2 + m // 2][:, (m % 2) * T:(m % 2) * T + T], whi[:, k, cs], wlo[:, k, cs],
                                      y2_h[:, k, :], y2_l[:, k, :], first and m % 2 == 0 and k == 0,
                                      last and k == 1)
                ins.then_inc(sem["group_done"], 1)

            sum_squares(0, T)
            sum_squares(1, TM)
            for c in range(MIX_2):
                chunk_2(c)
                side_2(c)
            sum_squares(2, T)
            need(pe, "scaled", DEPTH, 24)
            for k in range(KT):
                ins = mm(psum[6][0:20, 0:T], w_route[:, k, :], norm_f2[:, k, 0:T], start=k == 0, stop=k == KT - 1)
            ins.then_inc(sem["router_done"], 1)
            moe_up_part(0, 0)
            pe.wait_ge(sem["router_rows"], 1)
            for s in range(2):
                ins = nc.tensor.transpose(psum[7][:, 20 * s:20 * s + 20], lg[:, s * P:s * P + P], ident[0:20, 0:20])
            ins.then_inc(sem["router_turned"], 1)
            moe_up_part(0, 1)
            pe.wait_ge(sem["combine_ready"], 1)
            for s in range(2):
                ins = nc.tensor.transpose(psum[6][0:N_EXP, s * P:s * P + P], comb_t[:, s, :], ident)
            ins.then_inc(sem["combine_turned"], 1)
            pe.wait_ge(sem["combine_rows"], 1)
            for i in range(8):
                if i >= 2:
                    pe.wait_ge(sem["combine_all"], i - 1)
                for b in range(2):
                    ins = mm(psum[6 + i % 2][:, b * T:b * T + T],
                             ident[0:N_EXP, 2 * i + b:2 * i + b + 1].to_broadcast([N_EXP, P]), comb_row,
                             start=True, stop=True)
                ins.then_inc(sem["spread_done"], 1)

            def half_expert(n):
                moe_up_part(n, 0)
                moe_up_part(n, 1)
                moe_down_part(n - 1, isinstance(n, int) and n == 1, False)

            half_expert(1)
            with pe.Fori(1, N_EXP) as e:
                half_expert(2 * e)
                half_expert(2 * e + 1)
            moe_down_part(2 * N_EXP - 1, False, True)
            sum_squares(3, T)


def _by_partition(v):
    v = np.asarray(v)
    return np.ascontiguousarray(v.reshape(-1, P).T)


def _rows(pieces):
    col = np.zeros((P, 1), np.float32)
    for start, v in pieces:
        col[start:start + len(v), 0] = v
    return col


def _constants():
    p = np.arange(P)
    turn = np.zeros((P, P), np.float32)
    for m in range(P):
        if m % 64 < 32:
            turn[m + 32, m] = -1.0
        else:
            turn[m - 32, m] = 1.0
    one64 = (p[:, None] // 64 == p[None, :] // 64).astype(np.float32)
    causal = np.zeros((P, T), np.float32)
    causal[:, :P] = np.where(p[:, None] > p[None, :], BIG, 0.0)
    visible = np.zeros((P, T), np.float32)
    visible[:, P:] = np.where(p[None, :] > p[:, None], -BIG, 0.0)
    freq = (np.float32(10000.0) ** (-np.arange(0, 64, 2, dtype=np.float32) / np.float32(64))).astype(np.float32)
    consts = np.concatenate([np.eye(P, dtype=np.float32), turn, one64, causal, visible, freq[p % 32][:, None]], 1)
    mask_2 = np.zeros((P, S_COLS), np.float32)
    for s, (t_0, col, n) in enumerate(SPAN):
        key, query = s * P + p[:, None], META + t_0 + np.arange(n)[None, :]
        mask_2[:, col:col + n] = np.where(key > query, -BIG, 0.0)
    return consts.astype(np.float32), mask_2


def _arrays(d):
    par_1 = np.stack([np.concatenate(
        [_by_partition(d["norm_mix"][l]), _by_partition(d["mlstm_conv_w"][l]), _by_partition(d["mlstm_conv_b"][l]),
         _by_partition(d["mlstm_norm"][l]), _by_partition(d["rglru_conv_w"][l]),
         _by_partition(d["rglru_conv_b"][l]), _by_partition(d["rglru_b_a"][l]), _by_partition(d["rglru_b_x"][l]),
         _by_partition(d["rglru_lambda"][l]), _rows([(0, d["mlstm_i_bias"][l])]),
         _rows([(32, d["mlstm_f_bias"][l])]), _by_partition(d["ffn_conv_w"][l]), _by_partition(d["ffn_conv_b"][l]), _by_partition(d["norm_ffn"][l])], 1)
        for l in range(DEPTH)])
    par_2 = np.concatenate(
        [_by_partition(d["norm_final"]), _by_partition(d["norm_mix_2"][0]), _by_partition(d["ssd_conv_w_2"][0]),
         _by_partition(d["ssd_conv_b_2"][0]), _by_partition(np.repeat(d["D_skip_2"][0], 64)),
         _by_partition(d["ssd_norm_2"][0]), _by_partition(d["sc_conv_w_2"][0]), _by_partition(d["sc_norm_2"][0]),
         _by_partition(d["norm_ffn_2"][0]), _by_partition(d["norm_final_2"]), _rows([(0, d["dt_bias_2"][0])]),
         _rows([(0, d["A_log_2"][0])]),
         _rows([(0, d["router_group_b_2"][0]), (4, d["router_expert_b_2"][0])])], 1)
    consts, mask_2 = _constants()
    return dict(
        xT=np.ascontiguousarray(d["x"][0].T), positions=np.ascontiguousarray(d["positions"]), par_1=par_1,
        consts=consts, w_in=d["w_in"], w_a=d["rglru_w_a"], w_x=d["rglru_w_x"], w_branch=d["w_branch"],
        w_out=d["w_out"], ffn_up=d["ffn_up"], ffn_down=d["ffn_down"], par_2=par_2, mask_2=mask_2,
        metaT=np.ascontiguousarray(d["meta_tokens_2"].T), w_in_2=d["w_in_2"], w_out_2=d["w_out_2"],
        w_group=d["router_group_w_2"], w_expert=d["router_expert_w_2"], e_gate=d["expert_w_gate_2"],
        e_up=d["expert_w_up_2"], e_down=d["expert_w_down_2"])


def kernel(**inputs):
    import concourse.bacc as bacc
    from concourse.bass_utils import run_bass_kernel_spmd

    nc = bacc.Bacc("TRN2", target_bir_lowering=False, num_devices=1)
    data = _arrays({k: np.asarray(v) for k, v in inputs.items()})
    arrays, args = {}, {}
    for name, a in data.items():
        a = np.ascontiguousarray(a)
        arrays[f"in_{name}"] = a
        args[name] = nc.dram_tensor(f"in_{name}", a.shape, mybir.dt.from_np(a.dtype), kind="ExternalInput").ap()
    out = nc.dram_tensor("out_0", (D, T), F32, kind="ExternalOutput").ap()
    program(nc, **args, out=out)
    r = run_bass_kernel_spmd(nc, [arrays], core_ids=[0])
    return np.ascontiguousarray(r.results[0]["out_0"].T).reshape(1, T, D)
```

```python
import math
from contextlib import ExitStack

import numpy as np

import concourse.bass as bass
from concourse import mybir

F32 = mybir.dt.float32
F32R = mybir.dt.float32r
I32 = mybir.dt.int32
ALU = mybir.AluOpType
ACT = mybir.ActivationFunctionType
AX_X = mybir.AxisListType.X

P = 128
T = 256
D = 1024
KT = D // P
DEPTH = 2
DB = 512
NB = DB // P
DFF = 3072
EPS = 1e-6
HEADS_M = 4
HEADS_A = 8
TOPK = 64
BIG = 1e30
GONE = -3e38

C_MQK, C_MV, C_MO, C_MI, C_RX, C_RG = 0, 1024, 1536, 2048, 2056, 2568
C_AQ, C_AK, C_AV, C_AQI, C_AKI, C_GATE = 3080, 3592, 4104, 4616, 5128, 5200

M_NORM, M_CW, M_CB, M_G, M_RW, M_RB, M_BA, M_BX, M_LAM, M_IB, M_FB, M_N = (
    0, 8, 40, 48, 52, 68, 72, 76, 80, 84, 85, 86)
F_CW, F_CB, F_NORM, F_N = 0, 72, 96, 104
K_ID, K_ROT, K_ONE64, K_CAUS, K_VIS, K_INV, K_N = 0, 128, 256, 384, 640, 896, 897

RING = 3
SECTION = [("rx", 0), ("rx", 1), ("rg", 0), ("rg", 1), ("qi", 0), ("qi", 1), ("q", 0), ("q", 1),
           ("k", 0), ("k", 1), ("v", 0), ("v", 1), ("mqk", 0), ("mqk", 1), ("mqk", 2), ("mqk", 3),
           ("mv", 0), ("mv", 1), ("mo", 0), ("mo", 1)]
BRANCHES = (1, 2, 0)
for _branch in BRANCHES:
    for _half in range(2):
        SECTION += [("gate", (_branch, 2 * _half)), ("gate", (_branch, 2 * _half + 1)), ("wb", (_branch, _half))]
SECTION += [("wo", _i) for _i in range(4)]
MIX = len(SECTION)
FFN = 3 * (DFF // 256)
PER_LAYER = MIX + FFN
assert MIX % RING == 0 and FFN % RING == 0
SECTION_COL = {"rx": C_RX, "rg": C_RG, "qi": C_AQI, "q": C_AQ, "k": C_AK, "v": C_AV, "mqk": C_MQK,
               "mv": C_MV, "mo": C_MO}
DVE_EVACUATES = ("rx", "mqk", "wb", "wo")


def pool_splits(c, end):
    return RING <= c < end and c % RING != 0


def groups_of(c):
    return 2 if SECTION[c][0] == "wb" else 1


GROUP0 = [sum(groups_of(i) for i in range(c)) for c in range(MIX + 1)]
G_MIX = GROUP0[MIX]
G_LAYER = G_MIX + FFN
assert G_MIX % 2 == 0


def evacuations(c, dve):
    return sum(groups_of(i) for i in range(c)
               if SECTION[i][0] != "wo" and (SECTION[i][0] in DVE_EVACUATES) == dve)


EV_ACT = evacuations(MIX, False)
EV_DVE = evacuations(MIX, True)
WB = [c for c in range(MIX) if SECTION[c][0] == "wb"]

META = 16
TM = META + T
HEADS_S, GROUPS_S, N_EXP = 16, 4, 16
SECTION_2 = ([("x", i) for i in range(4)] + [("B", i) for i in range(2)] + [("C", i) for i in range(2)]
             + [("z", i) for i in range(4)] + [("c", i) for i in range(4)] + [("h", i) for i in range(4)]
             + [("b", i) for i in range(4)])
COL_2 = {"z": 0, "x": 1024, "B": 2048, "C": 2560, "dt": 3072, "b": 3088, "c": 4112, "h": 5136}
IN_2 = len(SECTION_2)
OUT_2 = 8
MIX_2 = IN_2 + OUT_2
CHUNKS_2 = MIX_2 + 6 * N_EXP
SSD_STEPS = (14, 16, 18, 20)
SC_STEPS = (21, 22, 24, 25)


def at_step(steps, c, later):
    return [i for i, first in enumerate(steps) if first + later == c]


DVE_EVACUATES_2 = ("x", "B", "C", "h", "b")
Q_NFIN, Q_NMIX, Q_CW, Q_CB, Q_D, Q_G, Q_SW, Q_SG, Q_NFF, Q_NOUT, Q_DT, Q_AL, Q_RB, Q_N = (
    0, 8, 16, 80, 96, 104, 112, 136, 144, 152, 160, 161, 162, 163)
SPAN = ((0, 0, T), (P - META, T, T - P + META), (2 * P - META, 2 * T - P + META, META))
S_COLS = SPAN[2][1] + META


def evacuations_2(c, dve):
    return 2 * sum(1 for i in range(c) if (SECTION_2[i][0] in DVE_EVACUATES_2) == dve)


def moe_group(n, part):
    if part == 2:
        return 2 * MIX_2 + (3 * n + 5 if not (isinstance(n, int) and n == 2 * N_EXP - 1) else 6 * N_EXP)
    if isinstance(n, int) and n == 0:
        return 2 * MIX_2 + 1 + part
    return 2 * MIX_2 + 3 * n + part


MERGE = max(WB)


ML_ROWS, ML_EXP, ML_NUM, ML_MEAN, ML_SQUARE, ML_STD, ML_SPLIT = 0, 1, 2, 3, 4, 5, 6


def mlstm_parts(c, parts):
    return [(part, (c - 20 - part) // 2) for part in sorted(parts, reverse=True)
            if 0 <= c - 20 - part < 2 * HEADS_M and (c - 20 - part) % 2 == 0]


N_FF = DFF // 256


def ff_group(n, part):
    if part == 2:
        return G_LAYER if isinstance(n, int) and n == N_FF - 1 else G_MIX + 3 * n + 5
    if isinstance(n, int) and n == 0:
        return G_MIX + 1 + part
    return G_MIX + 3 * n + part


COUNT = dict(
    hi_ready=PER_LAYER, lo_ready0=PER_LAYER // RING, lo_ready1=PER_LAYER // RING, lo_ready2=PER_LAYER // RING,
    group_done=G_LAYER, evac_act=EV_ACT, evac_dve=EV_DVE,
    landed0=16 * PER_LAYER // RING, landed1=16 * PER_LAYER // RING, landed2=16 * PER_LAYER // RING,
    own_act=50, own_dve=228, params=1, par_w=64, small_landed=64, small_hi=1, small_lo=1, small_done=1,
    squares=8, squares_added=2, sum_done=2, std_ready=2, scaled=16, act_hi=8, act_lo=8, x_ready=8,
    conv_tap=6, silu_done=4,
    lam_abs=1, lam_exp=1, lam_ready=1, lru_gates=2, lru_i=1, lru_in=1, lru_a=1, lru_ratio=1, lru_root=1,
    y_ready=5, yc_ready=1, y_hi=5, y_lo=5, yc_hi=1, yc_lo=1,
    rows_ready=1, f_abs=1, f_exp=1, a_row=1, m_row=1, em_row=1, aw_turned=1, aw_ready=1,
    rope_cos=6, rope_turned=7, rope_done=7, idx_done=6, idx_relu=6, idx_used=6, mask_ready=2,
    att_done=6, logits_ready=6, max_ready=2, prob_exp=2, prob_ready=2, turn_done=6, turned=6, pv_done=2, pv_out=1,
    ml_rows=4, ml_sub=4, ml_exp=4, ml_weight=4, ml_num=4, ml_h=4, ml_mean=4, ml_cent=4, ml_sq=4, ml_var=4,
    ml_std=4, ml_emb=4, wb_sum=8, merged_hi=4, merged_lo=4,
    ff_tap=N_FF, ff_conv=N_FF, ff_gelu=N_FF, ff_prod=N_FF, ff_hi=N_FF, ff_lo=N_FF, bank_done=3,
)


def program(nc, xT, positions, par_1, consts, w_in, w_a, w_x, w_branch, w_out, ffn_up, ffn_down,
            par_2, mask_2, metaT, w_in_2, w_out_2, w_group, w_expert, e_gate, e_up, e_down, out):
    ctx = ExitStack()
    with ctx:
        first, second = ExitStack(), ExitStack()

        def sb(name, shape, dt=F32, scope=ctx):
            return scope.enter_context(nc.sbuf_tensor(name, shape, dt))

        psum = [ctx.enter_context(nc.psum_tensor(f"bank{i}", [P, 512], F32)) for i in range(8)]
        main = psum[0:2]
        sem = {n: ctx.enter_context(nc.semaphore(n)) for n in COUNT}
        for n in ("x_loaded", "const_loaded", "pos_loaded", "par_loaded", "setup_dve", "setup_act", "zeros_ready",
                  "own_pool", "stored", "small_2", "par_2", "meta_ready", "rows_hi", "rows_lo",
                  "dt_raw", "dt_abs", "dt_exp", "dt_done", "a_exp", "state_turned", "state_cols", "x_turned",
                  "x_scaled", "cb_done", "cb_ready", "decay_rows", "decay_sub", "decay_exp", "decay_weight",
                  "ssd_y", "ssd_gated", "ssd_sq", "ssd_sum", "ssd_std", "ssd_norm", "y2_hi", "y2_lo",
                  "tap_2", "ev_act_2", "ev_dve_2", "silu_2", "sc_tap", "sc_conv", "sc_sq", "sc_sum", "sc_std",
                  "sc_norm", "x2_ready", "router_done", "router_rows", "router_turned", "router_max",
                  "router_exp", "pair_max", "pair_exp", "combine_ready", "combine_turned", "spread_done",
                  "combine_all", "moe_silu", "moe_scaled", "moe_prod", "moe_hi", "moe_lo"):
            sem[n] = ctx.enter_context(nc.semaphore(n))

        x_t = sb("x_t", [P, KT, T])
        w_raw = [sb(f"w_raw{i}", [P, 2048]) for i in range(RING)]
        w_hi = [sb(f"w_hi{i}", [P, 2048], F32R) for i in range(RING)]
        w_lo = [sb(f"w_lo{i}", [P, 2048], F32R) for i in range(RING)]
        cst = sb("cst", [P, K_N])
        ones = sb("ones", [P, T])
        eps = sb("eps", [P, 1])
        act_h = sb("act_h", [P, KT, T], F32R, first)
        act_l = sb("act_l", [P, KT, T], F32R, first)
        cos_t = sb("cos_t", [P, T], scope=first)
        sin_t = sb("sin_t", [P, T], scope=first)
        par_all = sb("par_all", [P, DEPTH, M_N + F_N], scope=first)
        par = sb("par", [P, M_N + F_N], scope=first)
        pm, pf = par[:, 0:M_N], par[:, M_N:M_N + F_N]
        wa = sb("wa", [P, NB, P], scope=first)
        wx = sb("wx", [P, NB, P], scope=first)
        lam8 = sb("lam8", [P, 2, NB], scope=first)
        y_h = [sb(f"y_h{i}", [P, NB, T], F32R, first) for i in range(2)]
        y_l = [sb(f"y_l{i}", [P, NB, T], F32R, first) for i in range(2)]
        work = sb("work", [P, 78 * T], scope=first)
        tiny = sb("tiny", [P, 896], scope=first)
        first.close()

        hx = sb("hx", [P, KT, TM], scope=second)
        act2_h = sb("act2_h", [P, KT, TM], F32R, second)
        act2_l = sb("act2_l", [P, KT, TM], F32R, second)
        y2_h = sb("y2_h", [P, 2 * KT, T], F32R, second)
        y2_l = sb("y2_l", [P, 2 * KT, T], F32R, second)
        dt_w = sb("dt_w", [P, KT, HEADS_S], scope=second)
        p2 = sb("p2", [P, Q_N], scope=second)
        w_route = sb("w_route", [P, KT, 20], scope=second)
        meta = sb("meta", [P, KT, META], scope=second)
        rows_h = sb("rows_h", [HEADS_S, T], F32R, second)
        rows_l = sb("rows_l", [HEADS_S, T], F32R, second)
        pick = sb("pick", [HEADS_S, HEADS_S], F32R, second)
        mask2 = sb("mask2", [P, S_COLS], scope=second)
        work2 = sb("work2", [P, 59 * T + P], scope=second)
        second.close()

        def at(kb, *shape):
            n = int(np.prod(shape))
            o = int(kb * T)
            ap = work[:, o:o + n]
            if len(shape) == 1:
                return ap
            names = "abcd"[:len(shape)]
            return ap.rearrange(f"p ({' '.join(names)}) -> p {' '.join(names)}",
                                **{a: s for a, s in zip(names[1:], shape[1:])})

        ident = cst[:, K_ID:K_ID + P]
        rot = cst[:, K_ROT:K_ROT + P]
        norm_f = at(0, KT, T)
        qi = at(0, NB, T)
        rope_in = [at(4, 2, T), at(6, 2, T)]
        prob = at(0, HEADS_A, T)
        q_c, k_c = at(8, NB, T), at(12, NB, T)
        v_c = at(16, 2, DB)
        ki = at(20, T)
        score, score_work = at(21, T), at(22, T)
        mask = [at(23.5, P), at(24, T)]
        rope_sin = [at(25, 2, T), at(27, 2, T)]
        relu = [at(37, 2, T), at(39, 2, T)]
        lru_x, lru_g, lru_r, lru_i, lru_t = (at(29 + 4 * i, NB, T) for i in range(5))
        prob_t = at(29, 2, HEADS_A, P)
        merged = at(37, KT, T)
        mqk = at(49, 2 * NB, T)
        mv = at(57, 2, DB)
        mo = at(61, NB, T)
        e_m, w_m = at(65, 384), at(66.5, 384)
        em_b, den_b, h_m, c_m, s_m, std_m = (at(68 + i, T) for i in range(6))
        gate = at(74, NB, T)
        small_raw = at(74, KT, P)
        small_h = y_h[1][:].rearrange("p b t -> p (b t)").rearrange("p (k m) -> p k m", k=KT)
        small_l = y_l[1][:].rearrange("p b t -> p (b t)").rearrange("p (k m) -> p k m", k=KT)
        sums_std, sums_r = at(65, T), at(66, T)
        f_row, t0, t1, t2, t3, g_row = (work[0:4, (53 + i) * T:(54 + i) * T] for i in range(6))
        rope_ki, f_in, ki_sin = at(49, T), at(50, T), at(51, T)
        iw = tiny[0:12, 0:T]
        m_row, em_r = tiny[0:4, T:2 * T], tiny[0:4, 2 * T:3 * T]
        lt = [tiny[:, 768 + 4 * i:772 + 4 * i] for i in range(5)]
        aw = tiny[:, 800:824].rearrange("p (s j) -> p s j", s=2)
        top8, a_max, a_sum, a_neg = (tiny[:, 824 + 8 * i:832 + 8 * i] for i in range(4))
        spare, spare_act = tiny[:, 856:857], tiny[:, 857:858]
        hid_f, ff_c, ff_g = at(0, 2, T), at(2, 2, T), at(4, 2, T)
        hid_h, hid_l = y_h[0], y_l[0]
        merge_t = [at(8, 2, T), at(10, 2, T)]
        y_attn = at(45, NB, T)

        def at2(col, *shape):
            n = int(np.prod(shape))
            ap = work2[:, col:col + n]
            if len(shape) == 1:
                return ap
            names = "abcd"[:len(shape)]
            return ap.rearrange(f"p ({' '.join(names)}) -> p {' '.join(names)}",
                                **{a: s for a, s in zip(names[1:], shape[1:])})

        o = 0
        norm_f2 = at2(o, KT, TM)
        v_sc = at2(o, KT, T)
        o += KT * TM
        xs = at2(o, KT, TM)
        o += KT * TM
        b_s, c_s = at2(o, 4, TM), at2(o + 4 * TM, 4, TM)
        ch = at2(o, KT, TM)
        o += KT * TM
        xdt = at2(o, 3, D)
        rows2 = [work2[0:HEADS_S, o + TM * i:o + TM * i + TM] for i in range(6)]
        combine = at2(KT * TM, N_EXP, T)
        o += 3 * D
        cb = at2(o, GROUPS_S, S_COLS)
        o += GROUPS_S * S_COLS
        decay = [at2(o + S_COLS * i, S_COLS) for i in range(2)]
        weight = [at2(o + S_COLS * (2 + i), S_COLS) for i in range(2)]
        o += 4 * S_COLS
        gy, gsq = at2(o, 2, T), at2(o + 2 * T, 2, T)
        o += 4 * T
        g_std = at2(o, T)
        o += T
        sc_s = [at2(o, 2, T), gsq]
        o += 2 * T
        cols2 = at2(o, 3, 2 * HEADS_S)
        o += 6 * HEADS_S
        a_col = at2(o, 1)
        decay_row = work2[0:HEADS_S, o + 1:o + 1 + TM]
        o += 1 + TM
        assert o <= 59 * T + P, o
        zs = x_t
        m_sg, m_hf = at2(KT * TM + N_EXP * T, 2, T), at2(KT * TM + N_EXP * T + 2 * T, 2, T)
        rt = at2(KT * TM + N_EXP * T + 4 * T, 2, 20)
        r_base = KT * TM + N_EXP * T + 4 * T + 64
        route = [at2(r_base + 8 * i, 2, 4) for i in range(8)]
        rcol = [at2(r_base + 64 + 2 * i, 2) for i in range(8)]
        comb_t = at2(r_base + 96, 2, N_EXP)
        lg = work2[0:20, r_base + 128:r_base + 128 + T]
        comb_row = work2[0:N_EXP, r_base + 128 + T:r_base + 128 + 2 * T]
        norm2_std, norm2_r = work2[:, 2 * KT * TM:2 * KT * TM + TM], work2[:, 2 * KT * TM + TM:2 * KT * TM + 2 * TM]
        fin_std, fin_r = at2(KT * TM, T), at2(KT * TM + T, T)

        def need(eng, name, L, k):
            v = L * COUNT[name] + k
            if not isinstance(v, int) or v > 0:
                eng.wait_ge(sem[name], v)

        class Own:

            def __init__(self, eng, name):
                self.eng, self.sem, self.base, self.k, self.outer = eng, sem[name], 0, 0, []

            def __call__(self, ins):
                ins.then_inc(self.sem, 1)
                self.k += 1

            def settle(self):
                self.eng.wait_ge(self.sem, self.base + self.k)

            def enter(self, rounds_before, each):
                self.outer.append((self.base, self.k))
                self.base, self.k = self.base + self.k + rounds_before * each, 0

            def leave(self, rounds, each):
                assert self.k == each, (self.k, each)
                self.base, self.k = self.outer.pop()
                self.k += rounds * each

        def lower_done(eng, L, c, n=0):
            need(eng, f"lo_ready{c % RING}", L, n + (c // RING + 1))

        def landed(c):
            return f"landed{c % RING}"

        def slot_free(eng, L, c, n=0):
            if isinstance(n, int) and c + 3 * n < RING:
                need(eng, "group_done", L, 0)
            elif isinstance(n, int) and c + 3 * n - RING < MIX:
                need(eng, "group_done", L, GROUP0[c + 3 * n - RING + 1])
            else:
                need(eng, "group_done", L, 3 * n + (G_MIX + c - RING - MIX + 1))

        def slot_free_2(eng, c, e=0):
            if isinstance(e, int) and c + 6 * e < RING:
                need(eng, "group_done", DEPTH, 0)
            elif isinstance(e, int) and c + 6 * e - RING < MIX_2:
                need(eng, "group_done", DEPTH, 2 * (c + 6 * e - RING + 1))
            else:
                need(eng, "group_done", DEPTH, 6 * e + (2 * MIX_2 + c - RING - MIX_2 + 1))

        block = ctx.enter_context(nc.Block())

        @block.sync
        def _(sp):
            sp.dma_start(work[:, 0:T].bitcast(I32), positions.rearrange("a t -> (a t)").partition_broadcast(P))\
                .then_inc(sem["pos_loaded"], 16)
            sp.dma_start(cst[:], consts).then_inc(sem["const_loaded"], 16)

            def tiles(w, rows, cols):
                return w[:, rows, cols].rearrange("l (t p) c -> p (l t) c", p=P)

            def source(L, c):
                kind, i = SECTION[c]
                if kind == "wb":
                    j, half = i
                    return w_branch.rearrange("l j r c -> (l j r) c")[bass.ds(L * 3 * DB + j * DB, DB),
                                                                     half * 512:half * 512 + 512]\
                        .rearrange("(t p) c -> p t c", p=P)
                if kind == "wo":
                    return tiles(w_out[bass.ds(L, 1)], slice(0, D), slice(i * 256, i * 256 + 256))
                if kind == "gate":
                    col = C_GATE + i[0] * D + i[1] * 256
                else:
                    col = SECTION_COL[kind] + i * 256
                if col == 0:
                    return w_in.rearrange("l r c -> (l r) c")[bass.ds(L * D, D), 0:256]\
                        .rearrange("(t p) c -> p t c", p=P)
                return tiles(w_in[bass.ds(L, 1)], slice(0, D), slice(col, col + 256))

            def ffn_source(L, part, n):
                if part < 2:
                    return tiles(ffn_up[bass.ds(L, 1)], slice(0, D), bass.ds(part * DFF + n * 256, 256))
                return tiles(ffn_down[bass.ds(L, 1)], bass.ds(n * 256, 256), slice(0, D))

            def load(L, c, src, n=0):
                lower_done(sp, L, c - RING, n)
                sp.dma_start(w_raw[c % RING][:].rearrange("p (t c) -> p t c", t=src.shape[1]), src)\
                    .then_inc(sem[landed(c)], 16)

            def load_small(L):
                need(sp, "lru_gates", L, 0)
                for dst, src in ((wa, w_a), (wx, w_x)):
                    for odd in range(2):
                        blocks = src[bass.ds(L, 1)].rearrange("l (b o) d e -> o d (l b) e", o=2)[odd]
                        at64 = slice(64 * odd, 64 * odd + 64)
                        sp.dma_start(dst[at64, :, at64], blocks).then_inc(sem["par_w"], 16)
                need(sp, "merged_lo", L, 0)
                for dst, col, n in ((0, C_MI, 4), (4, C_AKI + 64, 8), (32, C_MI + 4, 4), (64, C_AKI, 64)):
                    sp.dma_start(small_raw[:, :, dst:dst + n],
                                 tiles(w_in[bass.ds(L, 1)], slice(0, D), slice(col, col + n)))\
                        .then_inc(sem["small_landed"], 16)

            def load_2(c, src, e=0):
                lower_done(sp, DEPTH, c - RING, 2 * e)
                sp.dma_start(w_raw[c % RING][:].rearrange("p (t c) -> p t c", t=src.shape[1]), src)\
                    .then_inc(sem[landed(c)], 16)

            def source_2(c):
                if c < IN_2:
                    kind, i = SECTION_2[c]
                    col = COL_2[kind] + 256 * i
                    return tiles(w_in_2, slice(0, D), slice(col, col + 256))
                half, pair = (c - IN_2) // 4, (c - IN_2) % 4
                return tiles(w_out_2, slice(half * D, half * D + D), slice(pair * 256, pair * 256 + 256))

            def expert_source(e, half, part):
                cut = slice(half * 256, half * 256 + 256)
                if part == 2:
                    return tiles(e_down[0][bass.ds(e, 1)], cut, slice(0, D))
                return tiles((e_gate, e_up)[part][0][bass.ds(e, 1)], slice(0, D), cut)

            def layer(L, next_source):
                load(L, 2, source(L, 2))
                sp.wait_ge(sem["zeros_ready"], 1)
                load_small(L)
                for c in range(RING, MIX):
                    load(L, c, source(L, c))
                load(L, MIX, ffn_source(L, 0, 0))
                load(L, MIX + 1, ffn_source(L, 1, 0))
                if isinstance(L, int):
                    need(sp, "y_lo", L, 5)
                    for dst, src in ((p2[:], par_2), (mask2[:], mask_2),
                                     (meta[:], metaT.rearrange("(k p) t -> p k t", p=P)),
                                     (w_route[:, :, 0:4], w_group[0].rearrange("(k p) n -> p k n", p=P)),
                                     (w_route[:, :, 4:20], w_expert[0].rearrange("(k p) n -> p k n", p=P)),
                                     (dt_w[:], w_in_2[0][:, COL_2["dt"]:COL_2["dt"] + HEADS_S]
                                      .rearrange("(k p) n -> p k n", p=P))):
                        sp.dma_start(dst, src).then_inc(sem["par_2"], 16)
                with sp.Fori(0, N_FF - 1) as n:
                    load(L, MIX + 2, ffn_source(L, 0, n + 1), n)
                    load(L, MIX + 3, ffn_source(L, 1, n + 1), n)
                    load(L, MIX + 4, ffn_source(L, 2, n), n)
                load(L, PER_LAYER - 1, ffn_source(L, 2, N_FF - 1))
                load(L, PER_LAYER, next_source(0))
                load(L, PER_LAYER + 1, next_source(1))

            load(0, 0, source(0, 0))
            sp.dma_start(x_t[:], xT.rearrange("(k p) t -> p k t", p=P)).then_inc(sem["x_loaded"], 16)
            load(0, 1, source(0, 1))
            sp.dma_start(par_all[:], par_1.rearrange("l p n -> p l n")).then_inc(sem["par_loaded"], 16)
            with sp.Fori(0, DEPTH - 1) as L:
                layer(L, lambda c: source(L + 1, c))
            layer(DEPTH - 1, source_2)

            for c in range(2, MIX_2):
                load_2(c, source_2(c))
            load_2(MIX_2, expert_source(0, 0, 0))
            load_2(MIX_2 + 1, expert_source(0, 0, 1))

            def half_expert(e, half):
                c = MIX_2 + 3 * half - 1
                load_2(c, expert_source(e, half, 0), e)
                load_2(c + 1, expert_source(e, half, 1), e)
                load_2(c + 2, expert_source(e, 0, 2) if half else expert_source(e - 1, 1, 2), e)

            half_expert(0, 1)
            with sp.Fori(1, N_EXP) as e:
                half_expert(e, 0)
                half_expert(e, 1)
            load_2(CHUNKS_2 - 1, expert_source(N_EXP - 1, 1, 2))
            for i in range(4):
                need(sp, "scaled", DEPTH, 8 + 8 + 8 + 2 * i + 2)
                sp.dma_start(out.rearrange("(k p) t -> p k t", p=P)[:, 2 * i:2 * i + 2, :],
                             norm_f2[:, 2 * i:2 * i + 2, 0:T]).then_inc(sem["stored"], 16)
            sp.wait_ge(sem["stored"], 64)

        @block.gpsimd
        def _(pool):
            own = Own(pool, "own_pool")
            own(nc.gpsimd.memset(wa[:], 0.0))
            own(nc.gpsimd.memset(wx[:], 0.0))
            own(nc.gpsimd.memset(small_raw, 0.0))
            own(nc.gpsimd.memset(eps[:], EPS))
            own.settle()
            nc.gpsimd.memset(ones[:], 1.0).then_inc(sem["zeros_ready"], 1)

            def split(L, c):
                need(pool, "hi_ready", L, c + 1)
                nc.gpsimd.tensor_tensor(w_lo[c % RING][:], w_raw[c % RING][:], w_hi[c % RING][:].bitcast(F32),
                                        ALU.subtract).then_inc(sem[f"lo_ready{c % RING}"], 1)

            def layer(L):
                need(pool, "x_ready", L, 0)
                nc.gpsimd.tensor_copy(par[:], par_all[:, bass.ds(L, 1), :].rearrange("p l n -> p (l n)"))\
                    .then_inc(sem["params"], 1)
                for c in range(MIX - 1):
                    if 4 <= c <= 9:
                        i = c - 4
                        dst = (qi, q_c, k_c)[i // 2][:, 2 * (i % 2):2 * (i % 2) + 2, :]
                        need(pool, "evac_act", L, 2 + i + 1)
                        if i == 0:
                            need(pool, "act_lo", L, 4)
                        nc.gpsimd.tensor_tensor(dst, rope_in[i % 2], cos_t[:].unsqueeze(1).to_broadcast([P, 2, T]),
                                                ALU.mult).then_inc(sem["rope_cos"], 1)
                    if c in WB[2:]:
                        for half in range(2):
                            i = 2 * WB[2:].index(c) + half
                            b = 2 * (i % 4)
                            need(pool, "evac_dve", L, evacuations(c, True) + half + 1)
                            nc.gpsimd.tensor_tensor(merged[:, b:b + 2, :], merged[:, b:b + 2, :], merge_t[half],
                                                    ALU.add).then_inc(sem["wb_sum"], 1)
                    if pool_splits(c + RING, MIX):
                        split(L, c + RING)

            pool.wait_ge(sem["par_loaded"], 16)
            pool.wait_ge(sem["setup_act"], 2)
            with pool.Fori(0, DEPTH) as L:
                layer(L)

            pool.wait_ge(sem["par_2"], 96)
            pool.wait_ge(sem["x_ready"], DEPTH * 8)
            nc.gpsimd.tensor_copy(hx[:, :, 0:META], meta[:]).then_inc(sem["meta_ready"], 1)
            for c in range(MIX_2 - 1):
                if pool_splits(c + RING, MIX_2):
                    split(DEPTH, c + RING)


        @block.scalar
        def _(act):
            own = Own(act, "own_act")
            A = nc.scalar.activation

            def split(L, c, n=0):
                need(act, landed(c), L, 16 * n + 16 * (c // RING + 1))
                slot_free(act, L, c, n)
                nc.scalar.copy(w_hi[c % RING][:], w_raw[c % RING][:]).then_inc(sem["hi_ready"], 1)

            def norm(L, which):
                own(A(spare_act, eps[:], ACT.Sqrt))
                for i in range(4):
                    need(act, "x_ready", L, i + 1 if which else 0)
                    A(norm_f[:, 2 * i:2 * i + 2, :], x_t[:, 2 * i:2 * i + 2, :], ACT.Square)\
                        .then_inc(sem["squares"], 1)
                need(act, "sum_done", L, which + 1)
                A(sums_std, psum[7][:, 0:T], ACT.Sqrt, bias=eps[:], scale=1.0 / D).then_inc(sem["std_ready"], 1)
                for i in range(4):
                    need(act, "scaled", L, 8 * which + 2 * i + 2)
                    nc.scalar.copy(act_h[:, 2 * i:2 * i + 2, :], norm_f[:, 2 * i:2 * i + 2, :])\
                        .then_inc(sem["act_hi"], 1)

            def evacuate(L, c):
                kind, i = SECTION[c]
                g = GROUP0[c]
                if kind in ("wb", "wo"):
                    return
                need(act, "group_done", L, g + 1)
                ps = main[g % 2][:].rearrange("p (b t) -> p b t", b=2)
                if kind in ("rx", "mqk"):
                    dst, w, b, n = (lru_x, M_RW + 3 * 4, M_RB, 0) if kind == "rx" else (mqk, M_CW + 3 * 8, M_CB, 2)
                    for h in range(2):
                        j = 2 * i + h
                        ins = A(dst[:, j, :], ps[:, h, :], ACT.Identity, bias=pm[:, b + j:b + j + 1],
                                scale=pm[:, w + j:w + j + 1])
                        if h == 0:
                            own(ins)
                        else:
                            ins.then_inc(sem["conv_tap"], 1)
                    return
                if kind == "rg":
                    ins = A(lru_g[:, 2 * i:2 * i + 2, :], ps, ACT.Gelu_apprx_tanh)
                elif kind in ("qi", "q", "k"):
                    n = c - 4
                    if n >= 2:
                        need(act, "rope_cos", L, n - 1)
                        need(act, "rope_turned", L, n if n > 2 else 1)
                    ins = nc.scalar.copy(rope_in[n % 2], ps)
                elif kind == "v":
                    ins = nc.scalar.copy(v_c[:, :, i * 256:i * 256 + 256], ps)
                elif kind == "mv":
                    ins = nc.scalar.copy(mv[:, :, i * 256:i * 256 + 256], ps)
                elif kind == "mo":
                    ins = A(mo[:, 2 * i:2 * i + 2, :], ps, ACT.Sigmoid)
                elif kind == "gate":
                    before_it = [w for w in WB if w < c]
                    if before_it:
                        need(act, "evac_dve", L, evacuations(before_it[-1] + 1, True))
                    b = 2 * (i[1] % 2)
                    ins = A(gate[:, b:b + 2, :], ps, ACT.Tanh, scale=0.5)
                ins.then_inc(sem["evac_act"], 1)

            def silu(L, i):
                need(act, "evac_dve", L, 2 + i + 1)
                A(mqk[:, 2 * i:2 * i + 2, :], mqk[:, 2 * i:2 * i + 2, :], ACT.Silu).then_inc(sem["silu_done"], 1)

            def before(L):
                norm(L, 0)
                split(L, 2)
                need(act, "small_landed", L, 64)
                nc.scalar.copy(small_h, small_raw).then_inc(sem["small_hi"], 1)
                need(act, "lam_abs", L, 1)
                A(lt[1], lt[0], ACT.Exp, scale=-1.0).then_inc(sem["lam_exp"], 1)

            def attention_exp(L, tile, heads):
                width = T if tile == 0 else P
                need(act, "max_ready", L, tile + 1)
                for h in heads:
                    pr = prob[:, h, 0:width]
                    ins = A(pr, pr, ACT.Exp, bias=a_neg[:, h:h + 1], accum_out=a_sum[:, h:h + 1])
                    if h < HEADS_A - 1:
                        own(ins)
                    else:
                        ins.then_inc(sem["prob_exp"], 1)

            def turned(L, i):
                need(act, "turn_done", L, i + 1)
                ps = psum[2 + i % 2]
                s, half = (i // 2, i % 2) if i < 4 else (0, i % 2)
                nc.scalar.copy(prob_t[:, s, 4 * half:4 * half + 4, :],
                               ps[:].rearrange("p (h t) -> p h t", h=4)).then_inc(sem["turned"], 1)

            def mlstm(L, part, h):
                if part == ML_EXP:
                    need(act, "ml_sub", L, h + 1)
                    A(e_m, e_m, ACT.Exp, scale=-1.0).then_inc(sem["ml_exp"], 1)
                    if h >= 1:
                        need(act, "ml_h", L, h)
                    nc.scalar.copy(em_b, psum[6][:, 256:512]).then_inc(sem["ml_emb"], 1)
                if part == ML_SQUARE:
                    need(act, "ml_cent", L, h + 1)
                    A(s_m, c_m, ACT.Square).then_inc(sem["ml_sq"], 1)
                if part == ML_STD:
                    need(act, "ml_var", L, h + 1)
                    if h:
                        need(act, "y_lo", L, 1 + h)
                    A(std_m, psum[5][:, 256:512], ACT.Sqrt, bias=eps[:], scale=1.0 / P).then_inc(sem["ml_std"], 1)
                if part == ML_SPLIT:
                    y_upper(L, 2 + h, y_h[1][:, h, :], std_m)

            def y_upper(L, k, dst, src):
                need(act, "y_ready", L, k)
                nc.scalar.copy(dst, src).then_inc(sem["y_hi"], 1)

            def ahead(L, c):
                if c in (18, 19, 24):
                    i = {18: 0, 19: 2, 24: 4}[c]
                    turned(L, i)
                    turned(L, i + 1)
                for part, h in mlstm_parts(c, (ML_EXP, ML_SQUARE, ML_STD, ML_SPLIT)):
                    mlstm(L, part, h)

            def side(L, c):
                if c == 14:
                    attention_exp(L, 0, range(0, 4))
                if c == 15:
                    attention_exp(L, 0, range(4, 8))
                if c == 21:
                    attention_exp(L, 1, range(0, 8))
                if c == 3:
                    for gate_i, dst, bias in ((0, lru_r, M_BA), (1, lru_i, M_BX)):
                        need(act, "lru_gates", L, gate_i + 1)
                        for b in range(NB):
                            bank = psum[(4, 2)[gate_i] + b // 2][:, 256 * (b % 2):256 * (b % 2) + 256]
                            ins = A(dst[:, b, :], bank, ACT.Sigmoid, bias=pm[:, bias + b:bias + b + 1])
                            if gate_i == 1 and b == NB - 1:
                                ins.then_inc(sem["lru_i"], 1)
                            else:
                                own(ins)
                    need(act, "small_done", L, 1)
                    own(A(f_in[32:36, :], psum[6][32:36, 0:T], ACT.Identity, bias=pm[32:36, M_FB:M_FB + 1]))
                    own(nc.scalar.copy(rope_ki[64:128, :], psum[6][64:128, 0:T]))
                    own.settle()
                    A(iw, psum[6][0:12, 0:T], ACT.Identity, bias=pm[0:12, M_IB:M_IB + 1])\
                        .then_inc(sem["rows_ready"], 1)
                if c == 4:
                    need(act, "lam_ready", L, 1)
                    for b in range(NB):
                        own(A(lru_t[:, b, :], lru_r[:, b, :], ACT.Tanh, scale=lam8[:, 1, b:b + 1]))
                    own.settle()
                    for b in range(NB):
                        ins = A(lru_r[:, b, :], lru_r[:, b, :], ACT.Exp, scale=lam8[:, 0, b:b + 1])
                        if b == NB - 1:
                            ins.then_inc(sem["lru_a"], 1)
                        else:
                            own(ins)
                    need(act, "f_abs", L, 1)
                    A(t1, t0, ACT.Exp, scale=-1.0).then_inc(sem["f_exp"], 1)
                if c == 5:
                    need(act, "lru_ratio", L, 1)
                    A(lru_t, lru_t, ACT.Sqrt).then_inc(sem["lru_root"], 1)
                if c == 7:
                    need(act, "m_row", L, 1)
                    A(em_r, em_r, ACT.Exp, scale=-1.0).then_inc(sem["em_row"], 1)
                if c == 8:
                    y_upper(L, 1, y_h[0][:], lru_x)
                if c in (8, 9, 10):
                    for i in (2 * (c - 8), 2 * (c - 8) + 1):
                        need(act, "idx_done", L, i + 1)
                        if i >= 2:
                            need(act, "idx_used", L, i - 1)
                        A(relu[i % 2], psum[2 + i % 2][:].rearrange("p (b t) -> p b t", b=2), ACT.Relu)\
                            .then_inc(sem["idx_relu"], 1)
                if 13 <= c <= 16:
                    silu(L, c - 13)
                if c == 26:
                    need(act, "yc_ready", L, 1)
                    nc.scalar.copy(y_h[0][:], y_attn).then_inc(sem["yc_hi"], 1)
                if c in (MERGE - 1, MERGE):
                    for i in ((0, 1) if c < MERGE else (2, 3)):
                        need(act, "wb_sum", L, 4 + i + 1)
                        nc.scalar.mul(act_h[:, 2 * i:2 * i + 2, :], merged[:, 2 * i:2 * i + 2, :], 0.5)\
                            .then_inc(sem["merged_hi"], 1)

            def ffn_gate(L, n):
                need(act, "group_done", L, ff_group(n, 0))
                if not (isinstance(n, int) and n == 0):
                    need(act, "ff_gelu", L, n)
                for h in range(2):
                    j = 2 * n + h
                    ins = A(ff_c[:, h, :], main[0][:, 256 * h:256 * h + 256], ACT.Identity,
                            bias=pf[:, bass.ds(F_CB + j, 1)], scale=pf[:, bass.ds(F_CW + 48 + j, 1)])
                    if h == 0:
                        own(ins)
                    else:
                        ins.then_inc(sem["ff_tap"], 1)

            def ffn_mid(L, n):
                need(act, "ff_conv", L, n + 1)
                A(ff_g, ff_c, ACT.Gelu_apprx_tanh).then_inc(sem["ff_gelu"], 1)

            def ffn_hidden(L, n):
                need(act, "ff_prod", L, n + 1)
                if not (isinstance(n, int) and n == 0):
                    need(act, "group_done", L, ff_group(n - 1, 2))
                nc.scalar.copy(hid_h[:, 0:2, :], hid_f).then_inc(sem["ff_hi"], 1)

            def layer(L):
                before(L)
                for c in range(MIX):
                    ahead(L, c)
                    evacuate(L, c)
                    if c == MERGE:
                        side(L, c)
                        split(L, c + RING)
                    elif c < MIX - 1:
                        split(L, c + RING)
                        side(L, c)
                norm(L, 1)
                split(L, MIX + 2)
                ffn_gate(L, 0)
                split(L, MIX + 3)
                ffn_mid(L, 0)
                ffn_hidden(L, 0)
                split(L, MIX + 4)
                own_each = 1
                with act.Fori(1, N_FF) as n:
                    own.enter(n - 1, own_each)
                    ffn_gate(L, n)
                    split(L, MIX + 2, n)
                    ffn_mid(L, n)
                    split(L, MIX + 3, n)
                    ffn_hidden(L, n)
                    split(L, MIX + 4, n)
                own.leave(N_FF - 1, own_each)

            split(0, 0)
            act.wait_ge(sem["setup_dve"], 2)
            A(sin_t[:], sin_t[:], ACT.Sin).then_inc(sem["setup_act"], 1)
            A(cos_t[:], cos_t[:], ACT.Sin).then_inc(sem["setup_act"], 1)
            split(0, 1)
            act.wait_ge(sem["x_loaded"], 16)
            act.wait_ge(sem["zeros_ready"], 1)
            with act.Fori(0, DEPTH) as L:
                own.enter(L, COUNT["own_act"])
                layer(L)
            own.leave(DEPTH, COUNT["own_act"])

            def split_2(c, e=0):
                need(act, landed(c), DEPTH, 32 * e + 16 * (c // RING + 1))
                slot_free_2(act, c, e)
                nc.scalar.copy(w_hi[c % RING][:], w_raw[c % RING][:]).then_inc(sem["hi_ready"], 1)

            def deviation(n, out, width):
                need(act, "sum_done", DEPTH, n + 1)
                A(out, psum[7][:, 0:width], ACT.Sqrt, bias=eps[:], scale=1.0 / D).then_inc(sem["std_ready"], 1)

            def upper_2(n, width):
                for i in range(4):
                    need(act, "scaled", DEPTH, 8 * n + 2 * i + 2)
                    nc.scalar.copy(act2_h[:, 2 * i:2 * i + 2, 0:width], norm_f2[:, 2 * i:2 * i + 2, 0:width])\
                        .then_inc(sem["act_hi"], 1)

            def evacuate_2(c):
                kind, i = SECTION_2[c]
                for half in range(2):
                    g = 2 * c + half
                    j = 2 * i + half
                    ps = psum[g % 4]
                    if kind in ("h", "b"):
                        return
                    need(act, "group_done", DEPTH, g + 1)
                    if kind in ("x", "B", "C"):
                        dst, k = {"x": (xs, j), "B": (b_s, 8 + j), "C": (c_s, 12 + j)}[kind]
                        A(dst[:, j, :], ps[:, 0:TM], ACT.Identity, bias=p2[:, Q_CB + k:Q_CB + k + 1],
                          scale=p2[:, Q_CW + 48 + k:Q_CW + 49 + k]).then_inc(sem["tap_2"], 1)
                    elif kind == "z":
                        A(zs[:, j, :], ps[:, 0:T], ACT.Silu).then_inc(sem["ev_act_2"], 1)
                    else:
                        if j == 0:
                            act.wait_ge(sem["cb_ready"], 8)
                        nc.scalar.copy(ch[:, j, :], ps[:, 0:TM]).then_inc(sem["ev_act_2"], 1)

            def silu_2(i):
                j = 2 * i if i < 4 else 2 * (i % 2)
                dst = (xs if i < 4 else (b_s, c_s)[(i - 4) // 2])[:, j:j + 2, :]
                act.wait_ge(sem["ev_dve_2"], 2 * i + 2)
                A(dst, dst, ACT.Silu).then_inc(sem["silu_2"], 1)

            def ahead_2(c):
                if 11 <= c <= 18:
                    for h in (2 * (c - 11), 2 * (c - 11) + 1):
                        act.wait_ge(sem["decay_sub"], h + 1)
                        A(decay[h % 2], decay[h % 2], ACT.Exp).then_inc(sem["decay_exp"], 1)
                for g in at_step(SSD_STEPS, c, 2):
                    act.wait_ge(sem["ssd_norm"], g + 1)
                    nc.scalar.copy(y2_h[:, 2 * g:2 * g + 2, :], zs[:, 2 * g:2 * g + 2, :]).then_inc(sem["y2_hi"], 1)
                for g in at_step(SSD_STEPS, c, 0):
                    act.wait_ge(sem["ssd_gated"], g + 1)
                    A(gsq, gy, ACT.Square).then_inc(sem["ssd_sq"], 1)
                for g in at_step(SSD_STEPS, c, 1):
                    act.wait_ge(sem["ssd_sum"], g + 1)
                    A(g_std, psum[6 + g % 2][:, 0:T], ACT.Sqrt, bias=eps[:], scale=1.0 / 256)\
                        .then_inc(sem["ssd_std"], 1)
                for i in at_step(SC_STEPS, c, 2):
                    act.wait_ge(sem["sc_norm"], i + 1)
                    nc.scalar.copy(y2_h[:, 8 + 2 * i:10 + 2 * i, :], v_sc[:, 2 * i:2 * i + 2, :])\
                        .then_inc(sem["y2_hi"], 1)
                for i in at_step(SC_STEPS, c, 1):
                    act.wait_ge(sem["sc_sum"], i + 1)
                    A(sc_s[i % 2], psum[4 + i % 2][:].rearrange("p (b t) -> p b t", b=2), ACT.Sqrt, bias=eps[:],
                      scale=1.0 / 64).then_inc(sem["sc_std"], 1)
                for i in at_step(SC_STEPS, c, 0):
                    act.wait_ge(sem["ev_dve_2"], evacuations_2(20 + i + 1, True))
                    A(sc_s[i % 2], v_sc[:, 2 * i:2 * i + 2, :], ACT.Square).then_inc(sem["sc_sq"], 1)

            def side_2(c):
                if c == 1:
                    act.wait_ge(sem["small_2"], 1)
                    A(rows2[0], psum[4][0:HEADS_S, 0:TM], ACT.Identity, bias=p2[0:HEADS_S, Q_DT:Q_DT + 1])\
                        .then_inc(sem["dt_raw"], 1)
                    A(a_col[0:HEADS_S, :], p2[0:HEADS_S, Q_AL:Q_AL + 1], ACT.Exp).then_inc(sem["a_exp"], 1)
                    act.wait_ge(sem["dt_abs"], 1)
                    A(rows2[2], rows2[1], ACT.Exp, scale=-1.0).then_inc(sem["dt_exp"], 1)
                if c == 2:
                    own(nc.scalar.copy(pick[:], ident[0:HEADS_S, 0:HEADS_S]))
                    own.settle()
                    act.wait_ge(sem["dt_done"], 1)
                    nc.scalar.copy(rows_h[:], decay_row[:, META:TM]).then_inc(sem["rows_hi"], 1)
                if 1 <= c <= 8:
                    silu_2(c - 1)
                if c == 9:
                    for g in range(GROUPS_S):
                        act.wait_ge(sem["cb_done"], g + 1)
                        bank = psum[(6, 7, 4, 5)[g]]
                        nc.scalar.copy(cb[:, g, 0:S_COLS - META], bank[:, 0:S_COLS - META])\
                            .then_inc(sem["cb_ready"], 1)
                        nc.scalar.copy(cb[0:META, g, S_COLS - META:], bank[0:META, S_COLS - META:S_COLS])\
                            .then_inc(sem["cb_ready"], 1)
                if 17 <= c <= 20:
                    i = c - 17
                    act.wait_ge(sem["ev_dve_2"], evacuations_2(16 + i + 1, True))
                    for j in (2 * i, 2 * i + 1):
                        A(v_sc[:, j, :], ch[:, j, META:TM], ACT.Copy, scale=p2[:, Q_SW + 16 + j:Q_SW + 17 + j])\
                            .then_inc(sem["sc_tap"], 1)

            def moe_gate(n):
                need(act, "group_done", DEPTH, moe_group(n, 0))
                if not (isinstance(n, int) and n == 0):
                    act.wait_ge(sem["moe_prod"], n)
                A(m_sg, main[0][:].rearrange("p (b t) -> p b t", b=2), ACT.Silu).then_inc(sem["moe_silu"], 1)

            def moe_hidden(n):
                act.wait_ge(sem["moe_prod"], n + 1)
                if not (isinstance(n, int) and n == 0):
                    need(act, "group_done", DEPTH, moe_group(n - 1, 2))
                nc.scalar.copy(y2_h[:, 0:2, :], m_hf).then_inc(sem["moe_hi"], 1)

            act.wait_ge(sem["par_2"], 96)
            for i in range(4):
                act.wait_ge(sem["x_ready"], 8 * (DEPTH - 1) + 4 + i + 1)
                A(norm_f2[:, 2 * i:2 * i + 2, 0:T], x_t[:, 2 * i:2 * i + 2, :], ACT.Square)\
                    .then_inc(sem["squares"], 1)
            deviation(0, norm2_std[:, 0:T], T)
            for i in range(4):
                need(act, "scaled", DEPTH, 2 * i + 2)
                act.wait_ge(sem["meta_ready"], 1)
                A(norm_f2[:, 2 * i:2 * i + 2, :], hx[:, 2 * i:2 * i + 2, :], ACT.Square)\
                    .then_inc(sem["squares"], 1)
            deviation(1, norm2_std, TM)
            upper_2(1, TM)
            split_2(2)
            for c in range(MIX_2):
                ahead_2(c)
                if c < IN_2:
                    evacuate_2(c)
                if c < MIX_2 - 1:
                    split_2(c + RING)
                side_2(c)
            for i in range(4):
                act.wait_ge(sem["x2_ready"], i + 1)
                A(norm_f2[:, 2 * i:2 * i + 2, 0:T], hx[:, 2 * i:2 * i + 2, META:TM], ACT.Square)\
                    .then_inc(sem["squares"], 1)
            deviation(2, norm2_std[:, 0:T], T)
            upper_2(2, T)
            split_2(MIX_2 + 2)
            act.wait_ge(sem["router_done"], 1)
            A(lg, psum[6][0:20, 0:T], ACT.Identity, bias=p2[0:20, Q_RB:Q_RB + 1]).then_inc(sem["router_rows"], 1)
            moe_gate(0)
            act.wait_ge(sem["router_max"], 1)
            A(route[0], route[0], ACT.Exp).then_inc(sem["router_exp"], 1)
            act.wait_ge(sem["pair_max"], 1)
            A(rcol[4], rcol[4], ACT.Exp).then_inc(sem["pair_exp"], 1)
            split_2(MIX_2 + 3)
            for i in range(8):
                act.wait_ge(sem["spread_done"], i + 1)
                nc.scalar.copy(combine[:, 2 * i:2 * i + 2, :], psum[6 + i % 2][:].rearrange("p (b t) -> p b t", b=2))\
                    .then_inc(sem["combine_all"], 1)
            moe_hidden(0)
            split_2(MIX_2 + 4)

            def half_expert(e, half):
                moe_gate(2 * e + half)
                split_2(MIX_2 + 3 * half + 2, e)
                split_2(MIX_2 + 3 * half + 3, e)
                moe_hidden(2 * e + half)
                split_2(MIX_2 + 3 * half + 4, e)

            half_expert(0, 1)
            with act.Fori(1, N_EXP - 1) as e:
                half_expert(e, 0)
                half_expert(e, 1)
            half_expert(N_EXP - 1, 0)
            moe_gate(2 * N_EXP - 1)
            split_2(CHUNKS_2 - 1)
            moe_hidden(2 * N_EXP - 1)
            for i in range(4):
                act.wait_ge(sem["x2_ready"], 4 + i + 1)
                A(norm_f2[:, 2 * i:2 * i + 2, 0:T], hx[:, 2 * i:2 * i + 2, META:TM], ACT.Square)\
                    .then_inc(sem["squares"], 1)
            deviation(3, fin_std, T)

        @block.vector
        def _(dve):
            own = Own(dve, "own_dve")
            V = nc.vector
            STT = nc.vector.scalar_tensor_tensor

            def step(ins):
                own(ins)
                own.settle()

            def log1p_half(e, t_a, t_b, t_c):
                step(V.tensor_scalar(t_a, e, 2.0, None, ALU.add))
                step(V.reciprocal(t_b, t_a))
                step(V.tensor_tensor(t_a, e, t_b, ALU.mult))
                step(V.tensor_tensor(t_b, t_a, t_a, ALU.mult))
                step(V.tensor_scalar(t_c, t_b, 1.0 / 17.0, None, ALU.mult))
                for k in (15, 13, 11, 9, 7, 5, 3):
                    step(STT(t_c, t_c, 1.0 / k, t_b, ALU.add, ALU.mult))
                step(STT(t_b, t_c, 1.0, t_a, ALU.add, ALU.mult))

            def split(L, c, n=0):
                need(dve, "hi_ready", L, 3 * n + (c + 1))
                V.tensor_tensor(w_lo[c % RING][:], w_raw[c % RING][:], w_hi[c % RING][:].bitcast(F32),
                                ALU.subtract).then_inc(sem[f"lo_ready{c % RING}"], 1)

            def add_squares(L, n, sq):
                for i in (1, 2, 3):
                    need(dve, "squares", L, 4 * n + i + 1)
                    step(V.tensor_tensor(sq[:, 0:2, :], sq[:, 0:2, :], sq[:, 2 * i:2 * i + 2, :], ALU.add))
                V.tensor_tensor(sq[:, 0, :], sq[:, 0, :], sq[:, 1, :], ALU.add).then_inc(sem["squares_added"], 1)

            def norm(L, which):
                gains, col = (pf, F_NORM) if which else (pm, M_NORM)
                add_squares(L, which, norm_f)
                need(dve, "std_ready", L, which + 1)
                step(V.reciprocal(sums_r, sums_std))
                for i in range(5):
                    if i < 4:
                        for k in (2 * i, 2 * i + 1):
                            STT(norm_f[:, k, :], x_t[:, k, :], gains[:, col + k:col + k + 1], sums_r,
                                ALU.mult, ALU.mult).then_inc(sem["scaled"], 1)
                    if i:
                        need(dve, "act_hi", L, 4 * which + i)
                        V.tensor_tensor(act_l[:, 2 * i - 2:2 * i, :], norm_f[:, 2 * i - 2:2 * i, :],
                                        act_h[:, 2 * i - 2:2 * i, :].bitcast(F32), ALU.subtract)\
                            .then_inc(sem["act_lo"], 1)

            def evacuate(L, c):
                kind, i = SECTION[c]
                g = GROUP0[c]
                if kind in ("rx", "mqk"):
                    dst, w, n, k0 = (lru_x, M_RW, 4, 0) if kind == "rx" else (mqk, M_CW, 8, 2)
                    ps = main[g % 2][:].rearrange("p (b t) -> p b t", b=2)
                    need(dve, "conv_tap", L, k0 + i + 1)
                    for s in (1, 2, 3):
                        for h in range(2):
                            j = 2 * i + h
                            col = w + (3 - s) * n + j
                            ins = STT(dst[:, j, s:T], ps[:, h, 0:T - s], pm[:, col:col + 1], dst[:, j, s:T],
                                      ALU.mult, ALU.add)
                            if s == 3 and h == 1:
                                ins.then_inc(sem["evac_dve"], 1)
                            else:
                                own(ins)
                        if s < 3:
                            own.settle()
                if kind == "wb":
                    branch = BRANCHES.index(i[0])
                    need(dve, "evac_act", L, evacuations(c, False))
                    for half in range(2):
                        need(dve, "group_done", L, g + half + 1)
                        ps = main[(g + half) % 2][:].rearrange("p (b t) -> p b t", b=2)
                        b = 4 * i[1] + 2 * half
                        dst = merged[:, b:b + 2, :] if branch == 0 else merge_t[half]
                        n = 4 * (branch - 1) + 2 * i[1] + half
                        if n >= 2:
                            need(dve, "wb_sum", L, n - 1)
                        STT(dst, gate[:, 2 * half:2 * half + 2, :], 1.0, ps, ALU.add, ALU.mult)\
                            .then_inc(sem["evac_dve"], 1)
                if kind == "wo":
                    need(dve, "group_done", L, g + 1)
                    ps = main[g % 2][:].rearrange("p (b t) -> p b t", b=2)
                    V.tensor_tensor(x_t[:, 2 * i:2 * i + 2, :], x_t[:, 2 * i:2 * i + 2, :], ps, ALU.add)\
                        .then_inc(sem["x_ready"], 1)

            def before(L):
                norm(L, 0)
                split(L, 2)
                need(dve, "small_hi", L, 1)
                V.tensor_tensor(small_l, small_raw, small_h.bitcast(F32), ALU.subtract).then_inc(sem["small_lo"], 1)
                lam = pm[:, M_LAM:M_LAM + NB]
                STT(lt[0], lam, -1.0, lam, ALU.mult, ALU.max).then_inc(sem["lam_abs"], 1)
                step(V.tensor_scalar(lt[4], lam, 0.0, None, ALU.min))
                need(dve, "lam_exp", L, 1)
                log1p_half(lt[1], lt[0], lt[2], lt[3])
                step(STT(lt[0], lt[2], -2.0, lt[4], ALU.mult, ALU.add))
                own(V.tensor_scalar(lam8[:, 0, :], lt[0], 8.0, None, ALU.mult))
                own.settle()
                V.tensor_scalar(lam8[:, 1, :], lt[0], -8.0, None, ALU.mult).then_inc(sem["lam_ready"], 1)

            def rope(L, i):
                dst = (qi, q_c, k_c)[i // 2][:, 2 * (i % 2):2 * (i % 2) + 2, :]
                k = 1 if i == 0 else i + 2
                need(dve, "rope_turned", L, k)
                own(V.tensor_tensor(rope_sin[i % 2], psum[6 + i % 2][:].rearrange("p (b t) -> p b t", b=2),
                                    sin_t[:].unsqueeze(1).to_broadcast([P, 2, T]), ALU.mult))
                own.settle()
                need(dve, "rope_cos", L, i + 1)
                V.tensor_tensor(dst, dst, rope_sin[i % 2], ALU.add).then_inc(sem["rope_done"], 1)

            def rope_key(L):
                need(dve, "rope_turned", L, 2)
                up = slice(64, 128)
                own(V.tensor_tensor(ki_sin[up, :], psum[7][up, 0:T], sin_t[up, :], ALU.mult))
                own(V.tensor_tensor(ki[up, :], rope_ki[up, :], cos_t[up, :], ALU.mult))
                own.settle()
                step(V.tensor_tensor(ki[up, :], ki[up, :], ki_sin[up, :], ALU.add))
                V.tensor_copy(ki[0:64, :], ki[up, :]).then_inc(sem["rope_done"], 1)

            def gate_rows(L, part):
                if part == 0:
                    need(dve, "rows_ready", L, 1)
                    step(V.tensor_copy(f_row, f_in[32:36, :]))
                    STT(t0, f_row, -1.0, f_row, ALU.mult, ALU.max).then_inc(sem["f_abs"], 1)
                    step(V.tensor_scalar(f_row, f_row, 0.0, None, ALU.min))
                if part == 1:
                    need(dve, "f_exp", L, 1)
                    log1p_half(t1, t0, t2, t3)
                if part == 2:
                    step(STT(t0, t2, -2.0, f_row, ALU.mult, ALU.add))
                    step(V.tensor_tensor_scan(g_row, ones[0:4, :], t0, 0.0, ALU.mult, ALU.add))
                    V.tensor_tensor(iw[0:4, :], iw[0:4, :], g_row, ALU.subtract).then_inc(sem["a_row"], 1)
                    need(dve, "a_row", L, 1)
                    step(V.tensor_tensor_scan(m_row, iw[0:4, :], iw[0:4, :], 0.0, ALU.max, ALU.max))
                    V.tensor_tensor(em_r, g_row, m_row, ALU.add).then_inc(sem["m_row"], 1)
                if part == 3:
                    need(dve, "aw_turned", L, 1)
                    ps = psum[5][:, 256:280].rearrange("p (s j) -> p s j", s=2)
                    own(V.tensor_copy(aw[:, :, 0:4], ps[:, :, 0:4]))
                    V.tensor_scalar(aw[:, :, 4:12], ps[:, :, 4:12], 8.0 ** -0.5 * 64.0 ** -0.5, None, ALU.mult)\
                        .then_inc(sem["aw_ready"], 1)

            def index_unit(L, u):
                if u == 0:
                    need(dve, "aw_ready", L, 1)
                tile = 1 if u < 2 else 0
                width = T if tile else P
                vis = cst[:, K_VIS:K_VIS + T] if tile else cst[:, K_VIS + P:K_VIS + T]
                for i in (2 * u, 2 * u + 1):
                    need(dve, "idx_relu", L, i + 1)
                    heads = 2 if tile else 4
                    r = relu[i % 2].rearrange("p b t -> p (b t)").rearrange("p (h s) -> p h s", h=heads)
                    for j in range(heads):
                        h = (4 * u if tile else 0) + i % 2 + 2 * j
                        first = h == 0
                        ins = STT(score[:, 0:width], r[:, j, :], aw[:, tile, 4 + h:5 + h],
                                  vis if first else score[:, 0:width], ALU.mult, ALU.add)
                        if j < heads - 1:
                            step(ins)
                        else:
                            ins.then_inc(sem["idx_used"], 1)
                            need(dve, "idx_used", L, i + 1)

            def select(L, tile, part):
                width = T if tile else P
                a, b = score[:, 0:width], score_work[:, 0:width]
                for r in range(part * TOPK // 16, (part + 1) * TOPK // 16):
                    src = a if r == 0 else b
                    own(V.memset(spare, 0.0))
                    step(V.max(top8, src))
                    own(V.memset(spare, 0.0))
                    step(V.match_replace(b, top8, src, GONE))
                if part == 0:
                    return
                step(V.tensor_scalar(b, b, GONE, 1.0, ALU.is_equal, ALU.subtract))
                vis = cst[:, K_VIS:K_VIS + T] if tile else cst[:, K_VIS + P:K_VIS + T]
                STT(mask[tile][:, 0:width], b, BIG, vis, ALU.mult, ALU.add).then_inc(sem["mask_ready"], 1)

            def logits(L, u):
                tile = 1 if u < 2 else 0
                need(dve, "mask_ready", L, 1 if tile else 2)
                for i in range(2):
                    need(dve, "att_done", L, 2 * u + i + 1)
                    if u == 2 and i == 0:
                        need(dve, "turned", L, 4)
                    if tile:
                        ps = psum[(4 if u == 1 else 2) + i][:].rearrange("p (h s) -> p h s", h=2)
                        dst = prob[:, 4 * u + i:4 * u + 4:2, :]
                        m = mask[1].unsqueeze(1).to_broadcast([P, 2, T])
                    else:
                        ps = psum[2 + i][:].rearrange("p (h s) -> p h s", h=4)
                        dst = prob[:, i:HEADS_A:2, 0:P]
                        m = mask[0].unsqueeze(1).to_broadcast([P, 4, P])
                    STT(dst, ps, 64.0 ** -0.5, m, ALU.mult, ALU.add).then_inc(sem["logits_ready"], 1)

            def row_max(L, n):
                width = T if n == 0 else P
                need(dve, "logits_ready", L, 4 + 2 * n)
                step(V.reduce_max(a_max, prob[:, :, 0:width], AX_X))
                V.tensor_scalar(a_neg, a_max, -1.0, None, ALU.mult).then_inc(sem["max_ready"], 1)

            def normalise(L, n):
                width = T if n == 0 else P
                need(dve, "prob_exp", L, n + 1)
                step(V.reciprocal(a_max, a_sum))
                V.tensor_tensor(prob[:, :, 0:width], prob[:, :, 0:width],
                                a_max.unsqueeze(2).to_broadcast([P, HEADS_A, width]), ALU.mult)\
                    .then_inc(sem["prob_ready"], 1)

            def pv_out(L, n):
                need(dve, "pv_done", L, n + 1)
                tile = 1 - n
                ins = V.tensor_copy(y_attn[:, :, tile * P:tile * P + P],
                                    psum[2][:].rearrange("p (b t) -> p b t", b=NB))
                ins.then_inc(sem["pv_out" if n == 0 else "yc_ready"], 1)

            def mlstm(L, part, h):
                if part == ML_ROWS:
                    need(dve, "ml_rows", L, h + 1)
                    mk = cst[:, K_CAUS:K_CAUS + T]
                    if h:
                        need(dve, "ml_weight", L, h)
                    own(STT(e_m[:, 0:T], psum[6][:, 0:T], aw[:, 0, h:h + 1], mk, ALU.subtract, ALU.max))
                    STT(e_m[:, T:T + P], psum[6][:, P:T], aw[:, 1, h:h + 1], mk[:, 0:P], ALU.subtract, ALU.max)\
                        .then_inc(sem["ml_sub"], 1)
                if part == ML_EXP:
                    need(dve, "ml_exp", L, h + 1)
                    if h:
                        need(dve, "ml_num", L, h)
                    STT(w_m, psum[7][:, 0:384], float(P) ** -0.5, e_m, ALU.mult, ALU.mult)\
                        .then_inc(sem["ml_weight"], 1)
                if part == ML_NUM:
                    need(dve, "ml_num", L, h + 1)
                    need(dve, "ml_emb", L, h + 1)
                    step(STT(den_b, psum[4][:, 256:512], -1.0, em_b, ALU.mult, ALU.max))
                    step(V.tensor_tensor(den_b, psum[4][:, 256:512], den_b, ALU.max))
                    step(V.reciprocal(den_b, den_b))
                    if h:
                        need(dve, "ml_mean", L, h)
                    V.tensor_tensor(h_m, psum[4][:, 0:256], den_b, ALU.mult).then_inc(sem["ml_h"], 1)
                if part == ML_MEAN:
                    need(dve, "ml_mean", L, h + 1)
                    if h:
                        need(dve, "y_ready", L, 1 + h)
                    STT(c_m, psum[5][:, 0:256], -1.0 / P, h_m, ALU.mult, ALU.add).then_inc(sem["ml_cent"], 1)
                if part == ML_STD:
                    need(dve, "ml_std", L, h + 1)
                    step(V.reciprocal(s_m, std_m))
                    step(STT(c_m, c_m, pm[:, M_G + h:M_G + h + 1], s_m, ALU.mult, ALU.mult))
                    V.tensor_tensor(std_m, c_m, mo[:, h, :], ALU.mult).then_inc(sem["y_ready"], 1)
                if part == ML_SPLIT:
                    need(dve, "y_hi", L, 2 + h)
                    V.tensor_tensor(y_l[1][:, h, :], std_m, y_h[1][:, h, :].bitcast(F32), ALU.subtract)\
                        .then_inc(sem["y_lo"], 1)

            def ahead(L, c):
                if c == 9:
                    need(dve, "y_hi", L, 1)
                    V.tensor_tensor(y_l[0][:], lru_x, y_h[0][:].bitcast(F32), ALU.subtract)\
                        .then_inc(sem["y_lo"], 1)
                if c in (16, 22):
                    normalise(L, (c - 16) // 6)
                for part, h in mlstm_parts(c, (ML_EXP, ML_STD, ML_SPLIT)):
                    mlstm(L, part, h)

            def side(L, c):
                if c == 3:
                    need(dve, "lru_i", L, 1)
                    V.tensor_tensor(lru_i, lru_i, lru_x, ALU.mult).then_inc(sem["lru_in"], 1)
                if c == 4:
                    gate_rows(L, 0)
                    need(dve, "lru_a", L, 1)
                    need(dve, "lru_in", L, 1)
                    step(V.tensor_tensor(lru_x, lru_r, lru_r, ALU.mult))
                    STT(lru_t, lru_x, 1.0, lru_t, ALU.add, ALU.mult).then_inc(sem["lru_ratio"], 1)
                if c == 5:
                    rope(L, 0)
                    rope_key(L)
                    gate_rows(L, 1)
                if c == 6:
                    rope(L, 1)
                    gate_rows(L, 2)
                if c == 7:
                    rope(L, 2)
                    need(dve, "lru_root", L, 1)
                    step(V.tensor_tensor(lru_i, lru_i, lru_t, ALU.mult))
                    for b in range(NB):
                        own(V.tensor_tensor_scan(lru_x[:, b, :], lru_r[:, b, :], lru_i[:, b, :], 0.0,
                                                 ALU.mult, ALU.add))
                    own.settle()
                    V.tensor_tensor(lru_x, lru_x, lru_g, ALU.mult).then_inc(sem["y_ready"], 1)
                if c == 8:
                    rope(L, 3)
                    gate_rows(L, 3)
                if c == 9:
                    rope(L, 4)
                if c == 10:
                    rope(L, 5)
                if c in (10, 11):
                    select(L, 1, c - 10)
                if c in (8, 9, 10):
                    index_unit(L, c - 8)
                if c == 12:
                    logits(L, 0)
                if c == 13:
                    logits(L, 1)
                    row_max(L, 0)
                if c in (15, 16):
                    select(L, 0, c - 15)
                if c == 19:
                    pv_out(L, 0)
                if c == 20:
                    logits(L, 2)
                    row_max(L, 1)
                if c == 24:
                    pv_out(L, 1)
                for part, h in mlstm_parts(c, (ML_ROWS, ML_NUM, ML_MEAN)):
                    mlstm(L, part, h)
                if c == 26:
                    need(dve, "yc_hi", L, 1)
                    V.tensor_tensor(y_l[0][:], y_attn, y_h[0][:].bitcast(F32), ALU.subtract)\
                        .then_inc(sem["yc_lo"], 1)
                if c in (MERGE - 1, MERGE):
                    for i in ((0, 1) if c < MERGE else (2, 3)):
                        need(dve, "merged_hi", L, i + 1)
                        STT(act_l[:, 2 * i:2 * i + 2, :], merged[:, 2 * i:2 * i + 2, :], 0.5,
                            act_h[:, 2 * i:2 * i + 2, :].bitcast(F32), ALU.mult, ALU.subtract)\
                            .then_inc(sem["merged_lo"], 1)

            def ffn_conv(L, n):
                need(dve, "ff_tap", L, n + 1)
                for s in (1, 2):
                    for h in range(2):
                        ins = STT(ff_c[:, h, s:T], main[0][:, 256 * h:256 * h + T - s],
                                  pf[:, bass.ds(F_CW + (2 - s) * 24 + 2 * n + h, 1)], ff_c[:, h, s:T],
                                  ALU.mult, ALU.add)
                        if s == 2 and h == 1:
                            ins.then_inc(sem["ff_conv"], 1)
                        else:
                            own(ins)
                    if s == 1:
                        own.settle()

            def ffn_product(L, n):
                need(dve, "ff_gelu", L, n + 1)
                need(dve, "group_done", L, ff_group(n, 1))
                if not (isinstance(n, int) and n == 0):
                    need(dve, "ff_lo", L, n)
                V.tensor_tensor(hid_f, ff_g, main[1][:].rearrange("p (b t) -> p b t", b=2), ALU.mult)\
                    .then_inc(sem["ff_prod"], 1)

            def ffn_hidden(L, n):
                need(dve, "ff_hi", L, n + 1)
                V.tensor_tensor(hid_l[:, 0:2, :], hid_f, hid_h[:, 0:2, :].bitcast(F32), ALU.subtract)\
                    .then_inc(sem["ff_lo"], 1)

            def layer(L):
                before(L)
                for c in range(MIX):
                    if SECTION[c][0] == "wb":
                        evacuate(L, c)
                        ahead(L, c)
                    else:
                        ahead(L, c)
                        evacuate(L, c)
                    if c == MERGE:
                        side(L, c)
                        if not pool_splits(c + RING, MIX):
                            split(L, c + RING)
                    elif c < MIX - 1:
                        if not pool_splits(c + RING, MIX):
                            split(L, c + RING)
                        side(L, c)
                norm(L, 1)
                split(L, MIX + 2)
                ffn_conv(L, 0)
                split(L, MIX + 3)
                ffn_product(L, 0)
                ffn_hidden(L, 0)
                split(L, MIX + 4)
                own_each = 3
                with dve.Fori(1, N_FF) as n:
                    own.enter(n - 1, own_each)
                    ffn_conv(L, n)
                    split(L, MIX + 2, n)
                    ffn_product(L, n)
                    split(L, MIX + 3, n)
                    ffn_hidden(L, n)
                    split(L, MIX + 4, n)
                own.leave(N_FF - 1, own_each)
                for i in range(4):
                    if i < 3:
                        need(dve, "bank_done", L, i + 1)
                    else:
                        need(dve, "group_done", L, ff_group(N_FF - 1, 2))
                    V.tensor_tensor(x_t[:, 2 * i:2 * i + 2, :], x_t[:, 2 * i:2 * i + 2, :],
                                    psum[2 + i][:].rearrange("p (b t) -> p b t", b=2), ALU.add)\
                        .then_inc(sem["x_ready"], 1)

            pos = work[:, 0:T].bitcast(I32)
            ang, turns, tmp = work[:, T:2 * T], work[:, 2 * T:3 * T], work[:, 3 * T:4 * T]
            dve.wait_ge(sem["pos_loaded"], 16)
            dve.wait_ge(sem["const_loaded"], 16)
            step(V.tensor_copy(tmp, pos))
            step(V.tensor_scalar(ang, tmp, cst[:, K_INV:K_INV + 1], None, ALU.mult))
            part_1 = 6.28125
            part_2 = round((2 * math.pi - part_1) * 2 ** 21) / 2 ** 21
            part_3 = 2 * math.pi - part_1 - part_2
            pi_below = 3.1415925
            for table, quarter in ((sin_t, 0.0), (cos_t, 0.25)):
                step(V.tensor_scalar(turns, ang, 1.0 / (2 * math.pi), quarter, ALU.mult, ALU.add))
                step(V.tensor_scalar(turns, turns, 12582912.0, None, ALU.add))
                step(V.tensor_scalar(turns, turns, -12582912.0, None, ALU.add))
                step(STT(tmp, turns, -part_1, ang, ALU.mult, ALU.add))
                step(STT(tmp, turns, -part_2, tmp, ALU.mult, ALU.add))
                step(STT(tmp, turns, -part_3, tmp, ALU.mult, ALU.add))
                step(V.tensor_scalar(tmp, tmp, quarter * 2 * math.pi, -pi_below, ALU.add, ALU.max))
                V.tensor_scalar(table[:], tmp, pi_below, None, ALU.min).then_inc(sem["setup_dve"], 1)
                dve.wait_ge(sem["setup_dve"], 1 if quarter == 0.0 else 2)
            dve.wait_ge(sem["zeros_ready"], 1)
            split(0, 0)
            split(0, 1)
            with dve.Fori(0, DEPTH) as L:
                own.enter(L, COUNT["own_dve"])
                need(dve, "params", L, 1)
                layer(L)
            own.leave(DEPTH, COUNT["own_dve"])

            def split_2(c, e=0):
                need(dve, "hi_ready", DEPTH, 6 * e + (c + 1))
                V.tensor_tensor(w_lo[c % RING][:], w_raw[c % RING][:], w_hi[c % RING][:].bitcast(F32),
                                ALU.subtract).then_inc(sem[f"lo_ready{c % RING}"], 1)

            def scale_2(n, src, gain, std, r, dst, width, lower=False):
                add_squares(DEPTH, n, norm_f2[:, :, 0:width])
                need(dve, "std_ready", DEPTH, n + 1)
                step(V.reciprocal(r, std))
                for i in range(5):
                    if i < 4:
                        for k in (2 * i, 2 * i + 1):
                            STT(dst(k), src(k), p2[:, gain + k:gain + k + 1], r, ALU.mult, ALU.mult)\
                                .then_inc(sem["scaled"], 1)
                    if i and lower:
                        need(dve, "act_hi", DEPTH, 4 * (n - 1) + i)
                        V.tensor_tensor(act2_l[:, 2 * i - 2:2 * i, 0:width], norm_f2[:, 2 * i - 2:2 * i, 0:width],
                                        act2_h[:, 2 * i - 2:2 * i, 0:width].bitcast(F32), ALU.subtract)\
                            .then_inc(sem["act_lo"], 1)

            def evacuate_2(c):
                kind, i = SECTION_2[c]
                if kind in ("x", "B", "C"):
                    dst, k0 = {"x": (xs, 0), "B": (b_s, 8), "C": (c_s, 12)}[kind]
                    for half in range(2):
                        dve.wait_ge(sem["tap_2"], 2 * c + half + 1)
                        j = 2 * i + half
                        for s in (1, 2, 3):
                            col = Q_CW + (3 - s) * 16 + k0 + j
                            ins = STT(dst[:, j, s:TM], psum[(2 * c + half) % 4][:, 0:TM - s], p2[:, col:col + 1],
                                      dst[:, j, s:TM], ALU.mult, ALU.add)
                            if s < 3:
                                step(ins)
                            else:
                                ins.then_inc(sem["ev_dve_2"], 1)
                elif kind == "h":
                    for half in range(2):
                        g, j = 2 * c + half, 2 * i + half
                        need(dve, "group_done", DEPTH, g + 1)
                        dve.wait_ge(sem["ev_act_2"], 8 + j + 1)
                        V.tensor_tensor(ch[:, j, :], ch[:, j, :], psum[g % 4][:, 0:TM], ALU.mult)\
                            .then_inc(sem["ev_dve_2"], 1)
                elif kind == "b":
                    for half in range(2):
                        g, j = 2 * c + half, 2 * i + half
                        need(dve, "group_done", DEPTH, g + 1)
                        dve.wait_ge(sem["sc_conv"], j + 1)
                        ins = V.tensor_tensor(v_sc[:, j, :], v_sc[:, j, :], psum[g % 4][:, 0:T], ALU.mult)
                        ins.then_inc(sem["ev_dve_2"], 1)

            def ssd_head(h, part):
                e, w = decay[h % 2], weight[h % 2]
                if part == 0:
                    dve.wait_ge(sem["decay_rows"], h + 1)
                    if h >= 2:
                        dve.wait_ge(sem["decay_weight"], h - 1)
                    for s, (t0_, col, n) in enumerate(SPAN):
                        ins = STT(e[:, col:col + n], psum[4 + h % 2][:, t0_:T], cols2[:, s, h:h + 1],
                                  mask2[:, col:col + n], ALU.subtract, ALU.min)
                        if s < 2:
                            own(ins)
                        else:
                            ins.then_inc(sem["decay_sub"], 1)
                else:
                    dve.wait_ge(sem["decay_exp"], h + 1)
                    if h >= 2:
                        dve.wait_ge(sem["ssd_y"], h - 1)
                    V.tensor_tensor(w, e, cb[:, h // 4, :], ALU.mult).then_inc(sem["decay_weight"], 1)

            def ahead_2(c):
                if c == 11:
                    dve.wait_ge(sem["cb_ready"], 8)
                if 11 <= c <= 18:
                    ssd_head(2 * (c - 11), 1)
                    ssd_head(2 * (c - 11) + 1, 1)
                for g in at_step(SSD_STEPS, c, 2):
                    dve.wait_ge(sem["y2_hi"], g + 1)
                    V.tensor_tensor(y2_l[:, 2 * g:2 * g + 2, :], zs[:, 2 * g:2 * g + 2, :],
                                    y2_h[:, 2 * g:2 * g + 2, :].bitcast(F32), ALU.subtract).then_inc(sem["y2_lo"], 1)
                for g in at_step(SSD_STEPS, c, 1):
                    dve.wait_ge(sem["ssd_std"], g + 1)
                    step(V.reciprocal(g_std, g_std))
                    for b in range(2):
                        ins = STT(zs[:, 2 * g + b, :], gy[:, b, :], p2[:, Q_G + 2 * g + b:Q_G + 2 * g + b + 1], g_std,
                                  ALU.mult, ALU.mult)
                        if b == 0:
                            own(ins)
                        else:
                            ins.then_inc(sem["ssd_norm"], 1)
                for g in at_step(SSD_STEPS, c, -1):
                    dve.wait_ge(sem["ssd_y"], 4 * g + 4)
                    if g:
                        own.settle()
                        dve.wait_ge(sem["ssd_norm"], g)
                    for b in range(2):
                        own(STT(gy[:, b, :], xs[:, 2 * g + b, META:TM], p2[:, Q_D + 2 * g + b:Q_D + 2 * g + b + 1],
                                psum[6 + g % 2][:, b * T:b * T + T], ALU.mult, ALU.add))
                    own.settle()
                    dve.wait_ge(sem["ev_act_2"], min(8, 2 * g + 2))
                    V.tensor_tensor(gy, gy, zs[:, 2 * g:2 * g + 2, :], ALU.mult).then_inc(sem["ssd_gated"], 1)
                for i in at_step(SC_STEPS, c, 2):
                    dve.wait_ge(sem["y2_hi"], 4 + i + 1)
                    V.tensor_tensor(y2_l[:, 8 + 2 * i:10 + 2 * i, :], v_sc[:, 2 * i:2 * i + 2, :],
                                    y2_h[:, 8 + 2 * i:10 + 2 * i, :].bitcast(F32), ALU.subtract)\
                        .then_inc(sem["y2_lo"], 1)
                for i in at_step(SC_STEPS, c, 1):
                    dve.wait_ge(sem["sc_std"], i + 1)
                    step(V.reciprocal(sc_s[i % 2], sc_s[i % 2]))
                    for b in range(2):
                        j = 2 * i + b
                        ins = STT(v_sc[:, j, :], v_sc[:, j, :], p2[:, Q_SG + j:Q_SG + j + 1], sc_s[i % 2][:, b, :],
                                  ALU.mult, ALU.mult)
                        if b == 0:
                            own(ins)
                        else:
                            ins.then_inc(sem["sc_norm"], 1)

            def side_2(c):
                if c == 1:
                    dve.wait_ge(sem["dt_raw"], 1)
                    STT(rows2[1], rows2[0], -1.0, rows2[0], ALU.mult, ALU.max).then_inc(sem["dt_abs"], 1)
                    step(V.tensor_scalar(rows2[0], rows2[0], 0.0, None, ALU.max))
                    dve.wait_ge(sem["dt_exp"], 1)
                    log1p_half(rows2[2], rows2[1], rows2[3], rows2[4])
                    step(STT(rows2[0], rows2[3], 2.0, rows2[0], ALU.mult, ALU.add))
                    step(V.tensor_scalar(rows2[1], rows2[0], a_col[0:HEADS_S, :], -1.0, ALU.mult, ALU.mult))
                    own(V.memset(rows2[3], 1.0))
                    step(V.memset(cols2, 0.0))
                    V.tensor_tensor_scan(decay_row, rows2[3], rows2[1], 0.0, ALU.mult, ALU.add)\
                        .then_inc(sem["dt_done"], 1)
                if c == 2:
                    dve.wait_ge(sem["rows_hi"], 1)
                    V.tensor_tensor(rows_l[:], decay_row[:, META:TM], rows_h[:].bitcast(F32), ALU.subtract)\
                        .then_inc(sem["rows_lo"], 1)
                if c == 4:
                    for s, n in enumerate((P, P, META)):
                        dve.wait_ge(sem["state_turned"], 1)
                        ps = psum[5][0:n, 32 * s:32 * s + 32]
                        ins = V.tensor_copy(cols2[0:n, s, :], ps)
                        if s < 2:
                            own(ins)
                        else:
                            ins.then_inc(sem["state_cols"], 1)
                    own(V.memset(cb[:, :, S_COLS - META:], 0.0))
                if c in (5, 6, 7):
                    s = c - 5
                    n = (P, P, META)[s]
                    for half in range(2):
                        dve.wait_ge(sem["x_turned"], 2 * s + half + 1)
                        if s == 0 and half == 0:
                            dve.wait_ge(sem["state_cols"], 1)
                        dt = cols2[0:n, s, HEADS_S + 8 * half:HEADS_S + 8 * half + 8]
                        V.tensor_tensor(xdt[0:n, s, 512 * half:512 * half + 512].rearrange("p (h d) -> p h d", h=8),
                                        psum[6 + half][0:n, :].rearrange("p (h d) -> p h d", h=8),
                                        dt.unsqueeze(2).to_broadcast([n, 8, 64]), ALU.mult)\
                            .then_inc(sem["x_scaled"], 1)
                if 10 <= c <= 17:
                    h = 2 * (c - 10)
                    if c == 10:
                        own.settle()
                    ssd_head(h, 0)
                    ssd_head(h + 1, 0)
                if 17 <= c <= 20:
                    i = c - 17
                    dve.wait_ge(sem["sc_tap"], 2 * i + 2)
                    for s in (1, 2):
                        for j in (2 * i, 2 * i + 1):
                            col = Q_SW + (2 - s) * 8 + j
                            ins = STT(v_sc[:, j, :], ch[:, j, META - s:TM - s], p2[:, col:col + 1], v_sc[:, j, :],
                                      ALU.mult, ALU.add)
                            if s == 1:
                                own(ins)
                            else:
                                ins.then_inc(sem["sc_conv"], 1)
                        if s == 1:
                            own.settle()

            def add_out(c):
                m = 2 * (c - IN_2 - 4)
                need(dve, "group_done", DEPTH, 2 * c + 2)
                V.tensor_tensor(hx[:, m:m + 2, META:TM], hx[:, m:m + 2, META:TM],
                                psum[m // 2][:].rearrange("p (b t) -> p b t", b=2), ALU.add)\
                    .then_inc(sem["x2_ready"], 1)

            def first_hit(x, m, hit, left):
                step(V.tensor_tensor(hit, x, m.unsqueeze(2).to_broadcast([P, 2, 4]), ALU.is_equal))
                for j in (1, 2, 3):
                    if j == 1:
                        step(V.tensor_scalar(left, hit[:, :, 0], -1.0, 1.0, ALU.mult, ALU.add))
                    else:
                        step(V.tensor_tensor(left, left, hit[:, :, j - 1], ALU.subtract))
                    step(V.tensor_tensor(hit[:, :, j], hit[:, :, j], left, ALU.mult))

            def bc4(col):
                return col.unsqueeze(2).to_broadcast([P, 2, 4])

            def router():
                dve.wait_ge(sem["router_turned"], 1)
                step(V.tensor_copy(rt, psum[7][:, 0:40].rearrange("p (s j) -> p s j", s=2)))
                g = rt[:, :, 0:4]
                e = rt[:, :, 4:20].rearrange("p s (g j) -> p s g j", g=4)
                step(V.reduce_max(rcol[0], g, AX_X))
                V.tensor_tensor(route[0], g, bc4(rcol[0]), ALU.subtract).then_inc(sem["router_max"], 1)
                first_hit(g, rcol[0], route[1], rcol[1])
                step(V.tensor_tensor(route[2], e[:, :, 0, :], bc4(route[1][:, :, 0]), ALU.mult))
                for k in (1, 2, 3):
                    step(V.tensor_tensor(route[3], e[:, :, k, :], bc4(route[1][:, :, k]), ALU.mult))
                    step(V.tensor_tensor(route[2], route[2], route[3], ALU.add))
                step(V.reduce_max(rcol[2], route[2], AX_X))
                first_hit(route[2], rcol[2], route[4], rcol[1])
                step(STT(route[3], route[4], -BIG, route[2], ALU.mult, ALU.add))
                step(V.reduce_max(rcol[3], route[3], AX_X))
                V.tensor_tensor(rcol[4], rcol[3], rcol[2], ALU.subtract).then_inc(sem["pair_max"], 1)
                first_hit(route[3], rcol[3], route[5], rcol[1])
                dve.wait_ge(sem["router_exp"], 1)
                step(V.reduce_sum(rcol[5], route[0], AX_X))
                dve.wait_ge(sem["pair_exp"], 1)
                step(V.tensor_scalar(rcol[6], rcol[4], 1.0, None, ALU.add))
                step(V.tensor_tensor(rcol[6], rcol[6], rcol[5], ALU.mult))
                step(V.reciprocal(rcol[6], rcol[6]))
                step(V.tensor_tensor(rcol[7], rcol[6], rcol[4], ALU.mult))
                step(V.tensor_tensor(route[4], route[4], bc4(rcol[6]), ALU.mult))
                step(V.tensor_tensor(route[5], route[5], bc4(rcol[7]), ALU.mult))
                step(V.tensor_tensor(route[4], route[4], route[5], ALU.add))
                c4 = comb_t.rearrange("p s (g j) -> p s g j", g=4)
                for k in range(4):
                    ins = V.tensor_tensor(c4[:, :, k, :], route[4], bc4(route[1][:, :, k]), ALU.mult)
                    if k < 3:
                        own(ins)
                    else:
                        ins.then_inc(sem["combine_ready"], 1)
                dve.wait_ge(sem["combine_turned"], 1)
                step(V.tensor_copy(comb_row, psum[6][0:N_EXP, 0:T]))
                step(V.tensor_copy(rows_h[:], comb_row))
                V.tensor_tensor(rows_l[:], comb_row, rows_h[:].bitcast(F32), ALU.subtract)\
                    .then_inc(sem["rows_lo"], 1)

            def moe_product(e, half):
                n = 2 * e + half
                dve.wait_ge(sem["moe_silu"], n + 1)
                V.tensor_tensor(m_sg, m_sg, combine[:, bass.ds(e, 1), :].to_broadcast([P, 2, T]),
                                ALU.mult).then_inc(sem["moe_scaled"], 1)
                dve.wait_ge(sem["moe_scaled"], n + 1)
                need(dve, "group_done", DEPTH, moe_group(n, 1))
                if not (isinstance(n, int) and n == 0):
                    dve.wait_ge(sem["moe_lo"], n)
                V.tensor_tensor(m_hf, m_sg, main[1][:].rearrange("p (b t) -> p b t", b=2), ALU.mult)\
                    .then_inc(sem["moe_prod"], 1)

            def moe_hidden(n):
                dve.wait_ge(sem["moe_hi"], n + 1)
                V.tensor_tensor(y2_l[:, 0:2, :], m_hf, y2_h[:, 0:2, :].bitcast(F32), ALU.subtract)\
                    .then_inc(sem["moe_lo"], 1)

            dve.wait_ge(sem["par_2"], 96)
            scale_2(0, lambda k: x_t[:, k, :], Q_NFIN, norm2_std[:, 0:T], norm2_r[:, 0:T],
                    lambda k: hx[:, k, META:TM], T)
            scale_2(1, lambda k: hx[:, k, :], Q_NMIX, norm2_std, norm2_r, lambda k: norm_f2[:, k, :], TM, True)
            split_2(2)
            for c in range(MIX_2):
                ahead_2(c)
                if c < IN_2:
                    evacuate_2(c)
                elif c >= IN_2 + 4:
                    add_out(c)
                if c < MIX_2 - 1 and not pool_splits(c + RING, MIX_2):
                    split_2(c + RING)
                side_2(c)
            scale_2(2, lambda k: hx[:, k, META:TM], Q_NFF, norm2_std[:, 0:T], norm2_r[:, 0:T],
                    lambda k: norm_f2[:, k, 0:T], T, True)
            split_2(MIX_2 + 2)
            router()
            split_2(MIX_2 + 3)
            dve.wait_ge(sem["combine_all"], 8)
            moe_product(0, 0)
            moe_hidden(0)
            split_2(MIX_2 + 4)

            def half_expert(e, half):
                split_2(MIX_2 + 3 * half + 2, e)
                split_2(MIX_2 + 3 * half + 3, e)
                moe_product(e, half)
                moe_hidden(2 * e + half)
                split_2(MIX_2 + 3 * half + 4, e)

            half_expert(0, 1)
            with dve.Fori(1, N_EXP - 1) as e:
                half_expert(e, 0)
                half_expert(e, 1)
            half_expert(N_EXP - 1, 0)
            split_2(CHUNKS_2 - 1)
            moe_product(N_EXP - 1, 1)
            moe_hidden(2 * N_EXP - 1)
            for i in range(4):
                if i < 3:
                    need(dve, "bank_done", DEPTH, i + 1)
                else:
                    need(dve, "group_done", DEPTH, moe_group(2 * N_EXP - 1, 2))
                V.tensor_tensor(hx[:, 2 * i:2 * i + 2, META:TM], hx[:, 2 * i:2 * i + 2, META:TM],
                                psum[2 + i][:].rearrange("p (b t) -> p b t", b=2), ALU.add)\
                    .then_inc(sem["x2_ready"], 1)
            scale_2(3, lambda k: hx[:, k, META:TM], Q_NOUT, fin_std, fin_r, lambda k: norm_f2[:, k, 0:T], T)

        @block.tensor
        def _(pe):
            mm = nc.tensor.matmul

            def product(out, a_hi, a_lo, b_hi, b_lo, first, last):
                mm(out, a_hi, b_hi, start=first, stop=False, skip_group_check=True)
                mm(out, a_hi, b_lo, start=False, stop=False, skip_group_check=True)
                return mm(out, a_lo, b_hi, start=False, stop=last, skip_group_check=True)

            def bank_free(L, g):
                if g < 2:
                    return
                c = max(i for i in range(MIX) if GROUP0[i] <= g - 2)
                kind = SECTION[c][0]
                if kind == "wo":
                    need(pe, "x_ready", L, SECTION[c][1] + 1)
                else:
                    dve = kind in DVE_EVACUATES
                    need(pe, "evac_dve" if dve else "evac_act", L, evacuations(c, dve) + g - 2 - GROUP0[c] + 1)

            def chunk(L, c):
                kind, i = SECTION[c]
                lower_done(pe, L, c)
                g = GROUP0[c]
                hi, lo = w_hi[c % RING][:], w_lo[c % RING][:]
                if kind == "wb":
                    slot = {1: 0, 0: 1, 2: 0}[i[0]]
                    if i[0] == 2:
                        need(pe, "yc_lo", L, 1)
                    else:
                        need(pe, "y_lo", L, {1: 1, 0: 5}[i[0]])
                    whi, wlo = (w.rearrange("p (t c) -> p t c", t=NB) for w in (hi, lo))
                    for half in range(2):
                        bank_free(L, g + half)
                        for m in range(2):
                            col = (2 * half + m) * P
                            for k in range(NB):
                                ins = product(main[(g + half) % 2][:, m * T:m * T + T],
                                              whi[:, k, col:col + P], wlo[:, k, col:col + P],
                                              y_h[slot][:, k, :], y_l[slot][:, k, :], k == 0, k == NB - 1)
                        ins.then_inc(sem["group_done"], 1)
                    return
                bank_free(L, g)
                whi, wlo = (w.rearrange("p (t c) -> p t c", t=KT) for w in (hi, lo))
                for m in range(2):
                    for k in range(KT):
                        if c == 0 and m == 0 and k % 2 == 0:
                            need(pe, "act_lo", L, k // 2 + 1)
                        if kind == "wo" and i == 0 and m == 0 and k % 2 == 0:
                            need(pe, "merged_lo", L, k // 2 + 1)
                        o = main[g % 2][:, m * T:m * T + T]
                        if kind in ("v", "mv"):
                            ts = slice(m * P, m * P + P)
                            ins = product(o, act_h[:, k, ts], act_l[:, k, ts], whi[:, k, :], wlo[:, k, :],
                                          k == 0, k == KT - 1)
                        else:
                            cs = slice(m * P, m * P + P)
                            ins = product(o, whi[:, k, cs], wlo[:, k, cs], act_h[:, k, :], act_l[:, k, :],
                                          k == 0, k == KT - 1)
                ins.then_inc(sem["group_done"], 1)

            def norm(L, which):
                need(pe, "squares_added", L, which + 1)
                mm(psum[7][:, 0:T], ones[:, 0:P], norm_f[:, 0, :], start=True, stop=True)\
                    .then_inc(sem["sum_done"], 1)

            def turn_pair(L, i):
                need(pe, "evac_act", L, 2 + i + 1)
                if i >= 2:
                    need(pe, "rope_done", L, i if i > 2 else 2)
                for b in range(2):
                    ins = mm(psum[6 + i % 2][:, b * T:b * T + T], rot, rope_in[i % 2][:, b, :],
                             start=True, stop=True)
                ins.then_inc(sem["rope_turned"], 1)

            def mlstm(L, part, h):
                if part == ML_ROWS:
                    if h == 0:
                        need(pe, "em_row", L, 1)
                        need(pe, "aw_ready", L, 1)
                        need(pe, "silu_done", L, 4)
                    else:
                        need(pe, "ml_weight", L, h)
                        need(pe, "ml_emb", L, h)
                    pick = ident[0:4, h:h + 1].to_broadcast([4, P])
                    mm(psum[6][:, 0:T], pick, m_row, start=True, stop=True)
                    mm(psum[6][:, T:2 * T], pick, em_r, start=True, stop=True)
                    mm(psum[7][:, 0:T], mqk[:, 4 + h, 0:P], mqk[:, h, :], start=True, stop=True)
                    mm(psum[7][:, T:T + P], mqk[:, 4 + h, P:T], mqk[:, h, P:T], start=True, stop=True)\
                        .then_inc(sem["ml_rows"], 1)
                if part == ML_NUM:
                    need(pe, "ml_weight", L, h + 1)
                    if h:
                        need(pe, "ml_h", L, h)
                    hs = slice(h * P, h * P + P)
                    mm(psum[4][:, 0:T], mv[:, 0, hs], w_m[:, 0:T], start=True, stop=False, skip_group_check=True)
                    mm(psum[4][:, P:T], mv[:, 1, hs], w_m[:, T:T + P], start=False, stop=True, skip_group_check=True)
                    mm(psum[4][:, T:2 * T], ones[:, 0:P], w_m[:, 0:T], start=True, stop=False,
                       skip_group_check=True)
                    mm(psum[4][:, T + P:2 * T], ones[:, 0:P], w_m[:, T:T + P], start=False, stop=True,
                       skip_group_check=True).then_inc(sem["ml_num"], 1)
                if part == ML_MEAN:
                    need(pe, "ml_h", L, h + 1)
                    if h:
                        need(pe, "ml_std", L, h)
                    mm(psum[5][:, 0:T], ones[:, 0:P], h_m, start=True, stop=True).then_inc(sem["ml_mean"], 1)
                if part == ML_SQUARE:
                    need(pe, "ml_sq", L, h + 1)
                    mm(psum[5][:, T:2 * T], ones[:, 0:P], s_m, start=True, stop=True).then_inc(sem["ml_var"], 1)

            def attention_scores(L, u):
                tile = 1 if u < 2 else 0
                for i in range(2):
                    heads = range(4 * u + i, 4 * u + 4, 2) if tile else range(i, HEADS_A, 2)
                    width = T if tile else P
                    if u == 0 and i == 0:
                        need(pe, "rope_done", L, 7)
                        need(pe, "idx_relu", L, 6)
                    if u == 2:
                        need(pe, "turned", L, 4)
                        need(pe, "pv_out", L, 1)
                    for j, h in enumerate(heads):
                        r = slice(64 * (h % 2), 64 * (h % 2) + 64)
                        ins = mm(psum[(4 if u == 1 else 2) + i][:, j * width:j * width + width],
                                 q_c[r, h // 2, tile * P:tile * P + P], k_c[r, h // 2, 0:width],
                                 start=True, stop=True)
                    ins.then_inc(sem["att_done"], 1)

            def index_scores(L, u):
                tile = 1 if u < 2 else 0
                for i in range(2):
                    n = 2 * u + i
                    if n == 0:
                        need(pe, "rope_done", L, 3)
                        need(pe, "lru_i", L, 1)
                    if n >= 2:
                        need(pe, "idx_relu", L, n - 1)
                    width = T if tile else P
                    heads = range(4 * u + i, 4 * u + 4, 2) if tile else range(i, HEADS_A, 2)
                    for j, h in enumerate(heads):
                        r = slice(64 * (h % 2), 64 * (h % 2) + 64)
                        ins = mm(psum[2 + i][:, j * width:j * width + width],
                                 qi[r, h // 2, tile * P:tile * P + P], ki[r, 0:width], start=True, stop=True)
                    ins.then_inc(sem["idx_done"], 1)

            def turn_probs(L, i):
                s, half = (i // 2, i % 2) if i < 4 else (0, i % 2)
                need(pe, "prob_ready", L, 1 if i < 4 else 2)
                if i in (2, 3):
                    need(pe, "turned", L, i - 1)
                for j in range(4):
                    ins = nc.tensor.transpose(psum[2 + i % 2][:, j * P:j * P + P],
                                              prob[:, 4 * half + j, s * P:s * P + P], ident)
                ins.then_inc(sem["turn_done"], 1)

            def values(L, n):
                need(pe, "turned", L, 4 if n == 0 else 6)
                if n == 1:
                    need(pe, "pv_out", L, 1)
                spans = (0, 1) if n == 0 else (0,)
                for h in range(HEADS_A):
                    for s in spans:
                        r = 64 * (h % 2)
                        ins = mm(psum[2][r:r + 64, (h // 2) * P:(h // 2) * P + P],
                                 v_c[:, s, h * 64:h * 64 + 64], prob_t[:, s, h, :],
                                 start=s == spans[0], stop=s == spans[-1], skip_group_check=True)
                ins.then_inc(sem["pv_done"], 1)

            def side(L, c):
                if c == 3:
                    need(pe, "evac_dve", L, 2)
                    need(pe, "par_w", L, 64)
                    for w, bank in ((wa, 4), (wx, 2)):
                        for b in range(NB):
                            ins = mm(psum[bank + b // 2][:, T * (b % 2):T * (b % 2) + T], w[:, b, :], lru_x[:, b, :],
                                     start=True, stop=True)
                        ins.then_inc(sem["lru_gates"], 1)
                    need(pe, "small_lo", L, 1)
                    for k in range(KT):
                        ins = product(psum[6][:, 0:T], small_h[:, k, :], small_l[:, k, :], act_h[:, k, :],
                                      act_l[:, k, :], k == 0, k == KT - 1)
                    ins.then_inc(sem["small_done"], 1)
                if c == 5:
                    need(pe, "rows_ready", L, 1)
                    turn_pair(L, 0)
                    mm(psum[7][64:128, 0:T], rot[64:128, 64:128], rope_ki[64:128, :], start=True, stop=True)\
                        .then_inc(sem["rope_turned"], 1)
                if 6 <= c <= 10:
                    if c == 6:
                        need(pe, "rope_done", L, 2)
                    if c == 8:
                        need(pe, "a_row", L, 1)
                        need(pe, "lru_i", L, 1)
                    turn_pair(L, c - 5)
                if c == 8:
                    for s in range(2):
                        ins = nc.tensor.transpose(psum[5][:, 256 + 12 * s:268 + 12 * s], iw[:, s * P:s * P + P],
                                                  ident[0:12, 0:12])
                    ins.then_inc(sem["aw_turned"], 1)
                if c in (8, 9, 10):
                    index_scores(L, c - 8)
                if c in (12, 13):
                    attention_scores(L, c - 12)
                if c in (17, 18, 23):
                    i = {17: 0, 18: 2, 23: 4}[c]
                    turn_probs(L, i)
                    turn_probs(L, i + 1)
                if c == 19:
                    values(L, 0)
                if c == 20:
                    attention_scores(L, 2)
                if c == 24:
                    values(L, 1)
                for part, h in mlstm_parts(c, (ML_ROWS, ML_NUM, ML_MEAN, ML_SQUARE)):
                    mlstm(L, part, h)

            def ffn_up_part(L, n, part):
                c = MIX + part - (0 if isinstance(n, int) and n == 0 else 1)
                slot = c % RING
                lower_done(pe, L, c, n)
                if isinstance(n, int) and n == 0:
                    need(pe, "x_ready", L, 3 + part)
                elif part == 0:
                    need(pe, "ff_conv", L, n)
                else:
                    need(pe, "ff_prod", L, n)
                whi, wlo = (w[slot][:].rearrange("p (t c) -> p t c", t=KT) for w in (w_hi, w_lo))
                for m in range(2):
                    for k in range(KT):
                        if isinstance(n, int) and n == 0 and part == 0 and m == 0 and k % 2 == 0:
                            need(pe, "act_lo", L, 4 + k // 2 + 1)
                        cs = slice(m * P, m * P + P)
                        ins = product(main[part][:, m * T:m * T + T], whi[:, k, cs], wlo[:, k, cs],
                                      act_h[:, k, :], act_l[:, k, :], k == 0, k == KT - 1)
                ins.then_inc(sem["group_done"], 1)

            def ffn_down_part(L, n, first, last):
                c = PER_LAYER - 1 - 3 * n if last else MIX + 4
                slot = c % RING
                lower_done(pe, L, c, n)
                need(pe, "ff_lo", L, n + 1)
                whi, wlo = (w[slot][:].rearrange("p (t c) -> p t c", t=2) for w in (w_hi, w_lo))
                for m in range(KT):
                    for k in range(2):
                        cs = slice(m * P, m * P + P)
                        ins = product(psum[2 + m // 2][:, (m % 2) * T:(m % 2) * T + T], whi[:, k, cs], wlo[:, k, cs],
                                      hid_h[:, k, :], hid_l[:, k, :], first and m % 2 == 0 and k == 0,
                                      last and k == 1)
                    if last and m in (1, 3, 5):
                        ins.then_inc(sem["bank_done"], 1)
                ins.then_inc(sem["group_done"], 1)

            def layer(L):
                norm(L, 0)
                for c in range(MIX):
                    chunk(L, c)
                    side(L, c)
                norm(L, 1)
                ffn_up_part(L, 0, 0)
                ffn_up_part(L, 0, 1)
                ffn_up_part(L, 1, 0)
                ffn_up_part(L, 1, 1)
                ffn_down_part(L, 0, True, False)
                with pe.Fori(2, N_FF) as n:
                    ffn_up_part(L, n, 0)
                    ffn_up_part(L, n, 1)
                    ffn_down_part(L, n - 1, False, False)
                ffn_down_part(L, N_FF - 1, False, True)

            pe.wait_ge(sem["const_loaded"], 16)
            pe.wait_ge(sem["zeros_ready"], 1)
            with pe.Fori(0, DEPTH) as L:
                layer(L)

            def sum_squares(n, width):
                need(pe, "squares_added", DEPTH, n + 1)
                mm(psum[7][:, 0:width], ones[:, 0:P], norm_f2[:, 0, 0:width], start=True, stop=True)\
                    .then_inc(sem["sum_done"], 1)

            def bank_free_2(g):
                if g < 4:
                    return
                c = (g - 4) // 2
                dve = SECTION_2[c][0] in DVE_EVACUATES_2
                pe.wait_ge(sem["ev_dve_2" if dve else "ev_act_2"], evacuations_2(c, dve) + (g - 4) % 2 + 1)

            def chunk_2(c):
                lower_done(pe, DEPTH, c)
                whi, wlo = (w[c % RING][:].rearrange("p (t c) -> p t c", t=KT) for w in (w_hi, w_lo))
                if c < IN_2:
                    ts = slice(META, TM) if SECTION_2[c][0] in ("z", "b") else slice(0, TM)
                    for half in range(2):
                        g = 2 * c + half
                        bank_free_2(g)
                        cs = slice(half * P, half * P + P)
                        for k in range(KT):
                            if g == 0 and k % 2 == 0:
                                need(pe, "act_lo", DEPTH, k // 2 + 1)
                            ins = product(psum[g % 4][:, 0:ts.stop - ts.start], whi[:, k, cs], wlo[:, k, cs],
                                          act2_h[:, k, ts], act2_l[:, k, ts], k == 0, k == KT - 1)
                        ins.then_inc(sem["group_done"], 1)
                    return
                part, pair = (c - IN_2) // 4, (c - IN_2) % 4
                if part == 0:
                    bank_free_2(2 * IN_2 + pair)
                for half in range(2):
                    cs = slice(half * P, half * P + P)
                    for k in range(KT):
                        if pair == 0 and half == 0 and k % 2 == 0:
                            pe.wait_ge(sem["y2_lo"], 4 * part + k // 2 + 1)
                        ins = product(psum[pair][:, half * T:half * T + T], whi[:, k, cs], wlo[:, k, cs],
                                      y2_h[:, KT * part + k, :], y2_l[:, KT * part + k, :],
                                      part == 0 and half == 0 and k == 0, part == 1 and k == KT - 1)
                    ins.then_inc(sem["group_done"], 1)

            def spread(out, row):
                one = pick[:, row:row + 1].to_broadcast([HEADS_S, P])
                mm(out, one, rows_h[:], start=True, stop=False, skip_group_check=True)
                return mm(out, one, rows_l[:], start=False, stop=True, skip_group_check=True)

            def turn_x(s):
                n = (P, P, META)[s]
                for half in range(2):
                    if s == 0:
                        pe.wait_ge(sem["silu_2"], 4)
                    else:
                        pe.wait_ge(sem["x_scaled"], 2 * (s - 1) + half + 1)
                    for j in range(4):
                        ins = nc.tensor.transpose(psum[6 + half][0:n, j * P:j * P + P],
                                                  xs[:, 4 * half + j, s * P:s * P + n], ident)
                    ins.then_inc(sem["x_turned"], 1)

            def ssd_values(h):
                g, r = h // 4, 64 * (h % 2)
                pe.wait_ge(sem["decay_weight"], h + 1)
                if h % 4 == 0 and g >= 2:
                    pe.wait_ge(sem["ssd_std"], g - 1)
                o = ((h % 4) // 2) * T
                for s, (t_0, col, n) in enumerate(SPAN):
                    rows = (P, P, META)[s]
                    ins = mm(psum[6 + g % 2][r:r + 64, o + t_0:o + T], xdt[0:rows, s, h * 64:h * 64 + 64],
                             weight[h % 2][0:rows, col:col + n], start=s == 0, stop=s == 2, skip_group_check=True)
                ins.then_inc(sem["ssd_y"], 1)

            def side_2(c):
                if c == 1:
                    for k in range(KT):
                        ins = mm(psum[4][0:HEADS_S, 0:TM], dt_w[:, k, :], norm_f2[:, k, :], start=k == 0,
                                 stop=k == KT - 1)
                    ins.then_inc(sem["small_2"], 1)
                if c == 4:
                    pe.wait_ge(sem["dt_done"], 1)
                    for s, n in enumerate((P, P, META)):
                        nc.tensor.transpose(psum[5][0:n, 32 * s:32 * s + 16], decay_row[:, s * P:s * P + n],
                                            ident[0:16, 0:16])
                        ins = nc.tensor.transpose(psum[5][0:n, 32 * s + 16:32 * s + 32],
                                                  rows2[0][:, s * P:s * P + n], ident[0:16, 0:16])
                    ins.then_inc(sem["state_turned"], 1)
                if c in (5, 6, 7):
                    turn_x(c - 5)
                if c == 9:
                    pe.wait_ge(sem["silu_2"], 8)
                    pe.wait_ge(sem["x_scaled"], 6)
                    pe.wait_ge(sem["state_cols"], 1)
                    for g in range(GROUPS_S):
                        bank = psum[(6, 7, 4, 5)[g]]
                        for s, (t_0, col, n) in enumerate(SPAN):
                            rows = (P, P, META)[s]
                            ins = mm(bank[0:rows, col:col + n], b_s[:, g, s * P:s * P + rows],
                                     c_s[:, g, META + t_0:TM], start=True, stop=True)
                        ins.then_inc(sem["cb_done"], 1)
                if 11 <= c <= 18:
                    ssd_values(2 * (c - 11))
                    ssd_values(2 * (c - 11) + 1)
                if 10 <= c <= 17:
                    for h in (2 * (c - 10), 2 * (c - 10) + 1):
                        if c == 10:
                            pe.wait_ge(sem["cb_ready"], 8)
                        else:
                            pe.wait_ge(sem["decay_sub"], h - 1)
                        if h == 0:
                            pe.wait_ge(sem["rows_lo"], 1)
                        spread(psum[4 + h % 2][:, 0:T], h).then_inc(sem["decay_rows"], 1)
                for g in at_step(SSD_STEPS, c, 0):
                    pe.wait_ge(sem["ssd_sq"], g + 1)
                    for b in range(2):
                        ins = mm(psum[6 + g % 2][:, 0:T], ones[:, 0:P], gsq[:, b, :], start=b == 0, stop=b == 1)
                    ins.then_inc(sem["ssd_sum"], 1)
                for i in at_step(SC_STEPS, c, 0):
                    pe.wait_ge(sem["sc_sq"], i + 1)
                    for b in range(2):
                        ins = mm(psum[4 + i % 2][:, b * T:b * T + T], cst[:, K_ONE64:K_ONE64 + P],
                                 sc_s[i % 2][:, b, :], start=True, stop=True)
                    ins.then_inc(sem["sc_sum"], 1)

            def moe_up_part(n, part):
                c = MIX_2 + part - (0 if isinstance(n, int) and n == 0 else 1)
                slot = c % RING
                lower_done(pe, DEPTH, c, n)
                if isinstance(n, int) and n == 0:
                    if part == 0:
                        pe.wait_ge(sem["x2_ready"], 4)
                elif part == 0:
                    pe.wait_ge(sem["moe_silu"], n)
                else:
                    pe.wait_ge(sem["moe_prod"], n)
                whi, wlo = (w[slot][:].rearrange("p (t c) -> p t c", t=KT) for w in (w_hi, w_lo))
                for m in range(2):
                    for k in range(KT):
                        if isinstance(n, int) and n == 0 and part == 0 and m == 0 and k % 2 == 0:
                            need(pe, "act_lo", DEPTH, 4 + k // 2 + 1)
                        cs = slice(m * P, m * P + P)
                        ins = product(main[part][:, m * T:m * T + T], whi[:, k, cs], wlo[:, k, cs],
                                      act2_h[:, k, 0:T], act2_l[:, k, 0:T], k == 0, k == KT - 1)
                ins.then_inc(sem["group_done"], 1)

            def moe_down_part(n, first, last):
                c = CHUNKS_2 - 1 - 3 * n if last else MIX_2 + 4
                slot = c % RING
                lower_done(pe, DEPTH, c, n)
                pe.wait_ge(sem["moe_lo"], n + 1)
                whi, wlo = (w[slot][:].rearrange("p (t c) -> p t c", t=2) for w in (w_hi, w_lo))
                for m in range(KT):
                    for k in range(2):
                        cs = slice(m * P, m * P + P)
                        ins = product(psum[2 + m // 2][:, (m % 2) * T:(m % 2) * T + T], whi[:, k, cs], wlo[:, k, cs],
                                      y2_h[:, k, :], y2_l[:, k, :], first and m % 2 == 0 and k == 0,
                                      last and k == 1)
                    if last and m in (1, 3, 5):
                        ins.then_inc(sem["bank_done"], 1)
                ins.then_inc(sem["group_done"], 1)

            sum_squares(0, T)
            sum_squares(1, TM)
            for c in range(MIX_2):
                chunk_2(c)
                side_2(c)
            sum_squares(2, T)
            for k in range(KT):
                need(pe, "scaled", DEPTH, 16 + k + 1)
                ins = mm(psum[6][0:20, 0:T], w_route[:, k, :], norm_f2[:, k, 0:T], start=k == 0, stop=k == KT - 1)
            ins.then_inc(sem["router_done"], 1)
            moe_up_part(0, 0)
            pe.wait_ge(sem["router_rows"], 1)
            for s in range(2):
                ins = nc.tensor.transpose(psum[7][:, 20 * s:20 * s + 20], lg[:, s * P:s * P + P], ident[0:20, 0:20])
            ins.then_inc(sem["router_turned"], 1)
            moe_up_part(0, 1)
            moe_up_part(1, 0)
            pe.wait_ge(sem["combine_ready"], 1)
            for s in range(2):
                ins = nc.tensor.transpose(psum[6][0:N_EXP, s * P:s * P + P], comb_t[:, s, :], ident)
            ins.then_inc(sem["combine_turned"], 1)
            pe.wait_ge(sem["rows_lo"], 2)
            for i in range(8):
                if i >= 2:
                    pe.wait_ge(sem["combine_all"], i - 1)
                for b in range(2):
                    ins = spread(psum[6 + i % 2][:, b * T:b * T + T], 2 * i + b)
                ins.then_inc(sem["spread_done"], 1)

            def half_expert(n):
                moe_up_part(n, 0)
                moe_up_part(n, 1)
                moe_down_part(n - 1, False, False)

            moe_up_part(1, 1)
            moe_down_part(0, True, False)
            with pe.Fori(1, N_EXP) as e:
                half_expert(2 * e)
                half_expert(2 * e + 1)
            moe_down_part(2 * N_EXP - 1, False, True)
            sum_squares(3, T)


def _by_partition(v):
    v = np.asarray(v)
    return np.ascontiguousarray(v.reshape(-1, P).T)


def _rows(pieces):
    col = np.zeros((P, 1), np.float32)
    for start, v in pieces:
        col[start:start + len(v), 0] = v
    return col


def _constants():
    p = np.arange(P)
    turn = np.zeros((P, P), np.float32)
    for m in range(P):
        if m % 64 < 32:
            turn[m + 32, m] = -1.0
        else:
            turn[m - 32, m] = 1.0
    one64 = (p[:, None] // 64 == p[None, :] // 64).astype(np.float32)
    causal = np.zeros((P, T), np.float32)
    causal[:, :P] = np.where(p[:, None] > p[None, :], BIG, 0.0)
    visible = np.zeros((P, T), np.float32)
    visible[:, P:] = np.where(p[None, :] > p[:, None], -BIG, 0.0)
    freq = (np.float32(10000.0) ** (-np.arange(0, 64, 2, dtype=np.float32) / np.float32(64))).astype(np.float32)
    consts = np.concatenate([np.eye(P, dtype=np.float32), turn, one64, causal, visible, freq[p % 32][:, None]], 1)
    mask_2 = np.zeros((P, S_COLS), np.float32)
    for s, (t_0, col, n) in enumerate(SPAN):
        key, query = s * P + p[:, None], META + t_0 + np.arange(n)[None, :]
        mask_2[:, col:col + n] = np.where(key > query, -BIG, 0.0)
    return consts.astype(np.float32), mask_2


def _arrays(d):
    par_1 = np.stack([np.concatenate(
        [_by_partition(d["norm_mix"][l]), _by_partition(d["mlstm_conv_w"][l]), _by_partition(d["mlstm_conv_b"][l]),
         _by_partition(d["mlstm_norm"][l]), _by_partition(d["rglru_conv_w"][l]),
         _by_partition(d["rglru_conv_b"][l]), _by_partition(d["rglru_b_a"][l]), _by_partition(d["rglru_b_x"][l]),
         _by_partition(d["rglru_lambda"][l]), _rows([(0, d["mlstm_i_bias"][l])]),
         _rows([(32, d["mlstm_f_bias"][l])]), _by_partition(d["ffn_conv_w"][l]),
         _by_partition(d["ffn_conv_b"][l]), _by_partition(d["norm_ffn"][l])], 1)
        for l in range(DEPTH)])
    par_2 = np.concatenate(
        [_by_partition(d["norm_final"]), _by_partition(d["norm_mix_2"][0]), _by_partition(d["ssd_conv_w_2"][0]),
         _by_partition(d["ssd_conv_b_2"][0]), _by_partition(np.repeat(d["D_skip_2"][0], 64)),
         _by_partition(d["ssd_norm_2"][0]), _by_partition(d["sc_conv_w_2"][0]), _by_partition(d["sc_norm_2"][0]),
         _by_partition(d["norm_ffn_2"][0]), _by_partition(d["norm_final_2"]), _rows([(0, d["dt_bias_2"][0])]),
         _rows([(0, d["A_log_2"][0])]),
         _rows([(0, d["router_group_b_2"][0]), (4, d["router_expert_b_2"][0])])], 1)
    consts, mask_2 = _constants()
    return dict(
        xT=np.ascontiguousarray(d["x"][0].T), positions=np.ascontiguousarray(d["positions"]), par_1=par_1,
        consts=consts, w_in=d["w_in"], w_a=d["rglru_w_a"], w_x=d["rglru_w_x"], w_branch=d["w_branch"],
        w_out=d["w_out"], ffn_up=d["ffn_up"], ffn_down=d["ffn_down"], par_2=par_2, mask_2=mask_2,
        metaT=np.ascontiguousarray(d["meta_tokens_2"].T), w_in_2=d["w_in_2"], w_out_2=d["w_out_2"],
        w_group=d["router_group_w_2"], w_expert=d["router_expert_w_2"], e_gate=d["expert_w_gate_2"],
        e_up=d["expert_w_up_2"], e_down=d["expert_w_down_2"])


def kernel(**inputs):
    import concourse.bacc as bacc
    from concourse.bass_utils import run_bass_kernel_spmd

    nc = bacc.Bacc("TRN2", target_bir_lowering=False, num_devices=1)
    data = _arrays({k: np.asarray(v) for k, v in inputs.items()})
    arrays, args = {}, {}
    for name, a in data.items():
        a = np.ascontiguousarray(a)
        arrays[f"in_{name}"] = a
        args[name] = nc.dram_tensor(f"in_{name}", a.shape, mybir.dt.from_np(a.dtype), kind="ExternalInput").ap()
    out = nc.dram_tensor("out_0", (D, T), F32, kind="ExternalOutput").ap()
    program(nc, **args, out=out)
    r = run_bass_kernel_spmd(nc, [arrays], core_ids=[0])
    return np.ascontiguousarray(r.results[0]["out_0"].T).reshape(1, T, D)
```
